# Optimizing a Trainium2 kernel written in Bass

```python
import jax, jax.numpy as jnp
from jax import lax
import numpy as np

D_MODEL = 2048
BATCH = 1
SEQ = 256
DEPTH = 1

HEAD_DIM = 64
N_HEADS_SWA = 16
N_KV_SWA = 2
N_HEADS_FOX = 16
WINDOW = 128
BLOCK = 128
D_FF = 5632
CONV_WIDTH = 3
EPS = 1e-6
D_SWA = N_HEADS_SWA * HEAD_DIM
D_KV_SWA = N_KV_SWA * HEAD_DIM
D_FOX = N_HEADS_FOX * HEAD_DIM
D_MIX = D_SWA + D_FOX
D_IN = D_SWA + 2 * D_KV_SWA + 3 * D_FOX + N_HEADS_FOX


def rmsnorm(x, g):
    xf = x.astype(jnp.float32)
    y = xf * lax.rsqrt(jnp.mean(xf * xf, axis=-1, keepdims=True) + EPS)
    return (y * g.astype(jnp.float32)).astype(x.dtype)

def alibi_slopes(n):
    return jnp.asarray(2.0 ** (-8.0 * np.arange(1, n + 1) / n), dtype=jnp.float32)

def swa_sink_attention(q, k, v, sinks):
    B, S, H, D = q.shape
    KV = k.shape[2]
    G = H // KV
    nB = S // BLOCK
    scale = 1.0 / np.sqrt(D)
    qb = q.reshape(B, nB, BLOCK, KV, G, D)

    def band(t):
        tp = jnp.pad(t, ((0, 0), (BLOCK, 0), (0, 0), (0, 0)))[:, :S]
        return jnp.concatenate([tp.reshape(B, nB, BLOCK, KV, D), t.reshape(B, nB, BLOCK, KV, D)], axis=2)

    kb, vb = band(k), band(v)
    s = jnp.einsum('bnqkgd,bnskd->bnkgqs', qb, kb).astype(jnp.float32) * scale
    q_loc = BLOCK + jnp.arange(BLOCK)
    k_loc = jnp.arange(2 * BLOCK)
    dist = (q_loc[:, None] - k_loc[None, :]).astype(jnp.float32)
    blk_start = jnp.arange(nB) * BLOCK - BLOCK
    k_abs = blk_start[:, None] + k_loc[None, :]
    mask = (dist >= 0)[None] & (dist < WINDOW)[None] & (k_abs >= 0)[:, None, :]
    slopes = alibi_slopes(H).reshape(KV, G)
    s = s - slopes[:, :, None, None] * dist
    s = jnp.where(mask[None, :, None, None], s, -jnp.inf)
    sink = sinks.astype(jnp.float32).reshape(KV, G)[None, None, :, :, None, None]
    m = jnp.maximum(jnp.max(s, axis=-1, keepdims=True), sink)
    p = jnp.exp(s - m)
    p = p / (jnp.sum(p, axis=-1, keepdims=True) + jnp.exp(sink - m))
    o = jnp.einsum('bnkgqs,bnskd->bnqkgd', p.astype(v.dtype), vb)
    return o.reshape(B, S, H, D)

def forgetting_attention(q, k, v, log_f):
    B, S, H, D = q.shape
    nB = S // BLOCK
    scale = 1.0 / np.sqrt(D)
    c = lax.cumsum(log_f, axis=1)
    cT = jnp.transpose(c, (0, 2, 1))
    qb = jnp.moveaxis(q.reshape(B, nB, BLOCK, H, D), 1, 0)
    cb = jnp.moveaxis(cT.reshape(B, H, nB, BLOCK), 2, 0)
    k_pos = jnp.arange(S)

    def one_block(args):
        q_blk, c_blk, n = args
        s = jnp.einsum('bqhd,bshd->bhqs', q_blk, k).astype(jnp.float32) * scale
        s = s + c_blk[..., None] - cT[:, :, None, :]
        q_pos = n * BLOCK + jnp.arange(BLOCK)
        s = jnp.where((q_pos[:, None] >= k_pos[None, :])[None, None], s, -jnp.inf)
        p = jax.nn.softmax(s, axis=-1)
        return jnp.einsum('bhqs,bshd->bqhd', p.astype(v.dtype), v)

    o = lax.map(one_block, (qb, cb, jnp.arange(nB)))
    return jnp.moveaxis(o, 0, 1).reshape(B, S, H, D)

def causal_dwconv(u, w, b):
    S = u.shape[1]
    up = jnp.pad(u, ((0, 0), (CONV_WIDTH - 1, 0), (0, 0)))
    y = b
    for kk in range(CONV_WIDTH):
        y = y + up[:, kk:kk + S] * w[kk]
    return y

def first_inputs(seed: int = 0) -> dict:
    key = jax.random.key(seed)
    ks = jax.random.split(key, 17)
    f32 = jnp.float32
    nrm = lambda k, shape, s: jax.random.normal(k, shape, f32) * s
    gain = lambda k, n: 1.0 + 0.05 * jax.random.normal(k, (DEPTH, n), f32)
    return {
        "x": jax.random.normal(ks[0], (BATCH, SEQ, D_MODEL), f32),
        "pre_mix_g": gain(ks[1], D_MODEL),
        "w_in": nrm(ks[2], (DEPTH, D_MODEL, D_IN), D_MODEL ** -0.5),
        "b_forget": 2.0 + 0.5 * jax.random.normal(ks[3], (DEPTH, N_HEADS_FOX), f32),
        "sinks": nrm(ks[4], (DEPTH, N_HEADS_SWA), 1.0),
        "grp_swa_g": gain(ks[5], D_SWA),
        "grp_fox_g": gain(ks[6], D_FOX),
        "w_out": nrm(ks[7], (DEPTH, D_MIX, D_MODEL), D_MIX ** -0.5),
        "post_mix_g": gain(ks[8], D_MODEL),
        "pre_ffn_g": gain(ks[9], D_MODEL),
        "w_up": nrm(ks[10], (DEPTH, D_MODEL, 2 * D_FF), D_MODEL ** -0.5),
        "conv_w": nrm(ks[11], (DEPTH, CONV_WIDTH, 2 * D_FF), CONV_WIDTH ** -0.5),
        "conv_b": nrm(ks[12], (DEPTH, 2 * D_FF), 0.02),
        "w_down": nrm(ks[13], (DEPTH, D_FF, D_MODEL), D_FF ** -0.5),
        "post_ffn_g": gain(ks[14], D_MODEL),
    }

def first_block(x, pre_mix_g, w_in, b_forget, sinks, grp_swa_g, grp_fox_g, w_out, post_mix_g,
              pre_ffn_g, w_up, conv_w, conv_b, w_down, post_ffn_g):
    B, S, _ = x.shape
    cuts = np.cumsum([D_SWA, D_KV_SWA, D_KV_SWA, D_FOX, D_FOX, D_FOX])
    for l in range(DEPTH):
        h = rmsnorm(x, pre_mix_g[l])
        proj = h @ w_in[l]
        q_a, k_a, v_a, q_b, k_b, v_b, f_b = jnp.split(proj, cuts, axis=-1)
        o_a = swa_sink_attention(q_a.reshape(B, S, N_HEADS_SWA, HEAD_DIM),
                                 k_a.reshape(B, S, N_KV_SWA, HEAD_DIM),
                                 v_a.reshape(B, S, N_KV_SWA, HEAD_DIM), sinks[l])
        log_f = jax.nn.log_sigmoid(f_b.astype(jnp.float32) + b_forget[l].astype(jnp.float32))
        o_b = forgetting_attention(q_b.reshape(B, S, N_HEADS_FOX, HEAD_DIM),
                                   k_b.reshape(B, S, N_HEADS_FOX, HEAD_DIM),
                                   v_b.reshape(B, S, N_HEADS_FOX, HEAD_DIM), log_f)
        o_a = rmsnorm(o_a.reshape(B, S, D_SWA), grp_swa_g[l])
        o_b = rmsnorm(o_b.reshape(B, S, D_FOX), grp_fox_g[l])
        mix = jnp.concatenate([o_a, o_b], axis=-1) @ w_out[l]
        x = x + rmsnorm(mix, post_mix_g[l])
        h = rmsnorm(x, pre_ffn_g[l])
        u = causal_dwconv(h @ w_up[l], conv_w[l], conv_b[l])
        gate, val = jnp.split(u, 2, axis=-1)
        y = (jax.nn.gelu(gate, approximate=True) * val) @ w_down[l]
        x = x + rmsnorm(y, post_ffn_g[l])
    return x


CTX_LEN = 256
GRID_W = 64
N_Q_HEADS = D_MODEL // (2 * HEAD_DIM)
N_KV_HEADS = N_Q_HEADS // 4
ATTN_WIDTH = N_Q_HEADS * HEAD_DIM
KV_WIDTH = N_KV_HEADS * HEAD_DIM
POOL_WINDOWS = (2, 4, 8, 16)
POOL_GROUPS = len(POOL_WINDOWS)
POOL_WIDTH = D_MODEL - ATTN_WIDTH
POOL_GROUP_DIM = POOL_WIDTH // POOL_GROUPS
MIX_WIDTH = ATTN_WIDTH + POOL_WIDTH
IN_WIDTH = ATTN_WIDTH + 2 * KV_WIDTH + POOL_WIDTH
D_FF_2 = 4 * D_MODEL
ROPE_BASE = 10000.0
N_MOD = 6
NEG_INF = -1e30


def rms_norm(x, w):
    xf = x.astype(jnp.float32)
    y = xf * lax.rsqrt(jnp.mean(xf * xf, axis=-1, keepdims=True) + EPS)
    return (y * w.astype(jnp.float32)).astype(x.dtype)

def ada_modulation(cond, w, b):
    m = jax.nn.silu(cond) @ w + b
    return jnp.split(m[..., None, :], N_MOD, axis=-1)

def modulate(h, shift, scale):
    return h * (1.0 + scale) + shift

def split_projection(p):
    B, L, _ = p.shape
    q, k, v, u = jnp.split(p, [ATTN_WIDTH, ATTN_WIDTH + KV_WIDTH, ATTN_WIDTH + 2 * KV_WIDTH], axis=-1)
    return (q.reshape(B, L, N_Q_HEADS, HEAD_DIM), k.reshape(B, L, N_KV_HEADS, HEAD_DIM),
            v.reshape(B, L, N_KV_HEADS, HEAD_DIM), u)

def axial_positions(seq_len):
    rows = seq_len // GRID_W
    row = jnp.broadcast_to(jnp.arange(rows)[:, None], (rows, GRID_W)).reshape(-1)
    col = jnp.broadcast_to(jnp.arange(GRID_W)[None, :], (rows, GRID_W)).reshape(-1)
    return row, col

def rope_2d(x, row, col):
    half = HEAD_DIM // 2
    inv_freq = ROPE_BASE ** (-jnp.arange(0, half, 2, dtype=jnp.float32) / half)

    def rot(xa, pos):
        ang = pos.astype(jnp.float32)[:, None] * inv_freq[None, :]
        cos = jnp.cos(ang)[None, :, None, :]
        sin = jnp.sin(ang)[None, :, None, :]
        x1, x2 = jnp.split(xa, 2, axis=-1)
        return jnp.concatenate([x1 * cos - x2 * sin, x1 * sin + x2 * cos], axis=-1)

    xf = x.astype(jnp.float32)
    out = jnp.concatenate([rot(xf[..., :half], row), rot(xf[..., half:], col)], axis=-1)
    return out.astype(x.dtype)

def latent_window_attention(q, k, v, k_ctx, v_ctx, sink):
    B, L, H, D = q.shape
    G = H // N_KV_HEADS
    nb = L // BLOCK
    scale = HEAD_DIM ** -0.5
    qb = q.reshape(B, nb, BLOCK, N_KV_HEADS, G, D)
    pad = ((0, 0), (BLOCK, BLOCK), (0, 0), (0, 0))
    kp = jnp.pad(k, pad).reshape(B, nb + 2, BLOCK, N_KV_HEADS, D)
    vp = jnp.pad(v, pad).reshape(B, nb + 2, BLOCK, N_KV_HEADS, D)
    kb = jnp.concatenate([kp[:, :-2], kp[:, 1:-1], kp[:, 2:]], axis=2)
    vb = jnp.concatenate([vp[:, :-2], vp[:, 1:-1], vp[:, 2:]], axis=2)
    s_win = jnp.einsum('bnqhgd,bnkhd->bhgnqk', qb, kb).astype(jnp.float32) * scale
    blk = jnp.arange(nb)[:, None, None] * BLOCK
    qpos = blk + jnp.arange(BLOCK)[None, :, None]
    kpos = blk - BLOCK + jnp.arange(3 * BLOCK)[None, None, :]
    valid = (jnp.abs(qpos - kpos) <= WINDOW) & (kpos >= 0) & (kpos < L)
    s_win = jnp.where(valid, s_win, NEG_INF)
    s_ctx = jnp.einsum('bnqhgd,bchd->bhgnqc', qb, k_ctx).astype(jnp.float32) * scale
    s_sink = jnp.broadcast_to(sink.astype(jnp.float32).reshape(N_KV_HEADS, G)[None, :, :, None, None, None],
                              s_win.shape[:-1] + (1,))
    p = jax.nn.softmax(jnp.concatenate([s_win, s_ctx, s_sink], axis=-1), axis=-1)
    n_win = 3 * BLOCK
    n_ctx = k_ctx.shape[1]
    p_win = p[..., :n_win].astype(v.dtype)
    p_ctx = p[..., n_win:n_win + n_ctx].astype(v.dtype)
    out = (jnp.einsum('bhgnqk,bnkhd->bnqhgd', p_win, vb)
           + jnp.einsum('bhgnqc,bchd->bnqhgd', p_ctx, v_ctx))
    return out.reshape(B, L, H * D)

def context_attention(q, k, v, sink):
    B, C, H, D = q.shape
    G = H // N_KV_HEADS
    qg = q.reshape(B, C, N_KV_HEADS, G, D)
    s = jnp.einsum('bqhgd,bkhd->bhgqk', qg, k).astype(jnp.float32) * (HEAD_DIM ** -0.5)
    s_sink = jnp.broadcast_to(sink.astype(jnp.float32).reshape(N_KV_HEADS, G)[None, :, :, None, None],
                              s.shape[:-1] + (1,))
    p = jax.nn.softmax(jnp.concatenate([s, s_sink], axis=-1), axis=-1)[..., :C].astype(v.dtype)
    out = jnp.einsum('bhgqk,bkhd->bqhgd', p, v)
    return out.reshape(B, C, H * D)

def multiscale_pool(u, pool_w, pool_scale):
    B, L, _ = u.shape
    uf = u.astype(jnp.float32)
    csum = jnp.pad(jnp.cumsum(uf, axis=1), ((0, 0), (1, 0), (0, 0)))
    t = jnp.arange(L)
    outs = []
    for g, w in enumerate(POOL_WINDOWS):
        lo = jnp.clip(t - w // 2, 0, L)
        hi = jnp.clip(t - w // 2 + w, 0, L)
        cs = csum[..., g * POOL_GROUP_DIM:(g + 1) * POOL_GROUP_DIM]
        mean = (cs[:, hi] - cs[:, lo]) / (hi - lo).astype(jnp.float32)[None, :, None]
        outs.append(mean - uf[..., g * POOL_GROUP_DIM:(g + 1) * POOL_GROUP_DIM])
    pooled = jnp.stack(outs, axis=2)
    mixed = jnp.einsum('blgc,gcd->blgd', pooled, pool_w.astype(jnp.float32)).reshape(B, L, POOL_WIDTH)
    return (mixed * pool_scale.astype(jnp.float32)).astype(u.dtype)

def squared_relu_mlp(h, w_up, w_down):
    return jnp.square(jax.nn.relu(h @ w_up)) @ w_down

def second_inputs(seed: int = 0) -> dict:
    key = jax.random.key(seed)
    ks = jax.random.split(key, 18)
    f32 = jnp.float32
    nrm = lambda k, shape, s: jax.random.normal(k, shape, f32) * s
    return {
        "x": nrm(ks[0], (BATCH, SEQ, D_MODEL), 1.0),
        "c": nrm(ks[1], (BATCH, D_MODEL), 1.0),
        "ctx": nrm(ks[2], (BATCH, CTX_LEN, D_MODEL), 1.0),
        "c_ctx": nrm(ks[3], (D_MODEL,), 1.0),
        "norm_attn_w": 1.0 + nrm(ks[4], (DEPTH, D_MODEL), 0.02),
        "norm_mlp_w": 1.0 + nrm(ks[5], (DEPTH, D_MODEL), 0.02),
        "w_ada": nrm(ks[6], (DEPTH, D_MODEL, N_MOD * D_MODEL), 0.5 * D_MODEL ** -0.5),
        "b_ada": nrm(ks[7], (DEPTH, N_MOD * D_MODEL), 0.02),
        "w_in": nrm(ks[8], (DEPTH, D_MODEL, IN_WIDTH), D_MODEL ** -0.5),
        "attn_sink": nrm(ks[9], (DEPTH, N_Q_HEADS), 1.0),
        "pool_w": nrm(ks[10], (DEPTH, POOL_GROUPS, POOL_GROUP_DIM, POOL_GROUP_DIM), POOL_GROUP_DIM ** -0.5),
        "pool_scale": 1.0 + nrm(ks[11], (DEPTH, POOL_WIDTH), 0.1),
        "w_out": nrm(ks[12], (DEPTH, MIX_WIDTH, D_MODEL), MIX_WIDTH ** -0.5),
        "w_mlp_up": nrm(ks[13], (DEPTH, D_MODEL, D_FF_2), D_MODEL ** -0.5),
        "w_mlp_down": nrm(ks[14], (DEPTH, D_FF_2, D_MODEL), D_FF_2 ** -0.5),
        "final_norm_w": 1.0 + nrm(ks[15], (D_MODEL,), 0.02),
    }

def second_block(x, c, ctx, c_ctx, norm_attn_w, norm_mlp_w, w_ada, b_ada, w_in, attn_sink,
              pool_w, pool_scale, w_out, w_mlp_up, w_mlp_down, final_norm_w):
    seq_len = x.shape[1]
    row, col = axial_positions(seq_len)
    for layer in range(DEPTH):
        sh_a, sc_a, g_a, sh_m, sc_m, g_m = ada_modulation(c, w_ada[layer], b_ada[layer])
        csh_a, csc_a, cg_a, csh_m, csc_m, cg_m = ada_modulation(c_ctx, w_ada[layer], b_ada[layer])

        h = modulate(rms_norm(x, norm_attn_w[layer]), sh_a, sc_a)
        hc = modulate(rms_norm(ctx, norm_attn_w[layer]), csh_a, csc_a)
        q, k, v, u = split_projection(h @ w_in[layer])
        qc, kc, vc, uc = split_projection(hc @ w_in[layer])
        q = rope_2d(q, row, col)
        k = rope_2d(k, row, col)
        attn = latent_window_attention(q, k, v, kc, vc, attn_sink[layer])
        pool = multiscale_pool(u, pool_w[layer], pool_scale[layer])
        x = x + g_a * (jnp.concatenate([attn, pool], axis=-1) @ w_out[layer])

        hm = modulate(rms_norm(x, norm_mlp_w[layer]), sh_m, sc_m)
        x = x + g_m * squared_relu_mlp(hm, w_mlp_up[layer], w_mlp_down[layer])

        if layer < DEPTH - 1:
            attn_c = context_attention(qc, kc, vc, attn_sink[layer])
            pool_c = multiscale_pool(uc, pool_w[layer], pool_scale[layer])
            ctx = ctx + cg_a * (jnp.concatenate([attn_c, pool_c], axis=-1) @ w_out[layer])
            hcm = modulate(rms_norm(ctx, norm_mlp_w[layer]), csh_m, csc_m)
            ctx = ctx + cg_m * squared_relu_mlp(hcm, w_mlp_up[layer], w_mlp_down[layer])
    return rms_norm(x, final_norm_w)


def setup_inputs(seed=0):
    out = dict(first_inputs(seed))
    for name, value in second_inputs(seed + 1).items():
        if name != "x":
            out[name + "_2"] = value
    return out


def reference(
    x, pre_mix_g, w_in, b_forget, sinks, grp_swa_g, grp_fox_g, w_out, post_mix_g, pre_ffn_g,
    w_up, conv_w, conv_b, w_down, post_ffn_g, c_2, ctx_2, c_ctx_2, norm_attn_w_2, norm_mlp_w_2,
    w_ada_2, b_ada_2, w_in_2, attn_sink_2, pool_w_2, pool_scale_2, w_out_2, w_mlp_up_2,
    w_mlp_down_2, final_norm_w_2,
):
    x = first_block(
        x, pre_mix_g, w_in, b_forget, sinks, grp_swa_g, grp_fox_g, w_out, post_mix_g, pre_ffn_g,
        w_up, conv_w, conv_b, w_down, post_ffn_g,
    )
    return second_block(
        x, c_2, ctx_2, c_ctx_2, norm_attn_w_2, norm_mlp_w_2, w_ada_2, b_ada_2, w_in_2,
        attn_sink_2, pool_w_2, pool_scale_2, w_out_2, w_mlp_up_2, w_mlp_down_2, final_norm_w_2,
    )


_drawn_inputs = setup_inputs


def setup_inputs(seed=0):
    import zlib

    import numpy as np

    out = dict(_drawn_inputs(seed))
    spreads = {}
    factors = {'conv_b': 3.515,
     'ctx_2': 6.005,
     'norm_attn_w_2': 8.0,
     'norm_mlp_w_2': 8.0,
     'b_ada_2': 2.928,
     'attn_sink_2': 8.0,
     'pool_scale_2': 4.858,
     'final_norm_w_2': 2.91}
    for name, (base, spread) in spreads.items():
        noise = np.random.default_rng([zlib.crc32(name.encode()), seed]).standard_normal(out[name].shape)
        drawn = base * np.exp(spread * noise) if base else spread * noise
        out[name] = __import__('jax').numpy.asarray(drawn.astype(out[name].dtype))
    for name, factor in factors.items():
        out[name] = (out[name] * factor).astype(out[name].dtype)
    return out
```

```python
from contextlib import ExitStack

import numpy as np

import concourse.bass as bass
from concourse import mybir

F32 = mybir.dt.float32
F32R = mybir.dt.float32r
ALU = mybir.AluOpType
ACT = mybir.ActivationFunctionType
AX_X = mybir.AxisListType.X

P = 128
TOK = 256
NB = TOK // P
D = 2048
KT = D // P
DH = 64
SCALE = DH ** -0.5
EPS = 1e-6
N = 512
CK = N // P
LOADK = 4
STEPK = 2

HEADS = 16
W_IN1 = 4368
QA, KA, VA, QB, KB, VB, FB = 0, 1024, 1152, 1280, 2304, 3328, 4352
FF1 = 5632
GV = N // 2
CT1 = FF1 // P
CTS = 2 * CT1
UPS1 = (8, 8, 6)
W_IN2 = 2560
Q2, K2, V2, U2 = 0, 1024, 1280, 1536
KV2 = 4
FF2 = 8192
GROUPS2 = 4
WINDOWS = (2, 4, 8, 16)
PG = 256
ADA_HALF = 1024
ADA_ORDER = ((0, True), (2, False), (3, False), (4, False), (1, True), (5, False))
NEG = -1e30

C_ID, C_TRI, C_ONE, C_ALI, C_CAU, C_MASK, C_COS, C_SIN, C_END = 0, 128, 256, 384, 768, 1152, 2176, 2304, 2432

PHASES = [("in1", 9, 4), ("out1", 4, 4), ("up1a", 8, 4), ("down1a", 4, 4), ("up1b", 8, 4), ("down1b", 4, 4),
          ("up1c", 6, 4), ("down1c", 4, 3), ("in2", 5, 4), ("out2", 4, 4), ("mlp2", 32, 4)]
FIRST_LOAD, FIRST_EVAC = {}, {}
_l = _e = 0
for _name, _n, _per in PHASES:
    FIRST_LOAD[_name], FIRST_EVAC[_name] = _l, _e
    _l += _n * _per
    _e += 2 * _n + (2 if _name == "in2" else 0)
LOADS = _l
STEPS = 2 * LOADS
UP0 = {"up1a": 0, "up1b": 8, "up1c": 16, "mlp2": 22}


def constants():
    t = np.zeros((P, C_END), np.float32)
    p = np.arange(P)[:, None]
    c = np.arange(TOK)[None, :]
    t[:, C_ID:C_ID + P] = p == c[:, :P]
    t[:, C_TRI:C_TRI + P] = p <= c[:, :P]
    t[:, C_ONE:C_ONE + P] = 1.0
    t[:, C_ALI:C_ALI + P] = np.where(c[:, :P] <= p, c[:, :P] - p, NEG)
    far = P + p - c
    t[:, C_ALI + P:C_ALI + 3 * P] = np.where((far >= 0) & (far < P), -far, NEG)
    t[:, C_CAU:C_CAU + P] = np.where(c[:, :P] <= p, 0.0, NEG)
    t[:, C_CAU + P:C_CAU + 3 * P] = np.where(far >= 0, 0.0, NEG)
    freq = (10000.0 ** (-np.arange(0, 32, 2, dtype=np.float32) / np.float32(32))).astype(np.float32)
    for b in range(NB):
        q = b * P + p
        t[:, C_MASK + b * N:C_MASK + b * N + TOK] = np.where(np.abs(q - c) <= 128, 0.0, NEG)
        for rc, pos in enumerate((q // 64, q % 64)):
            ang = (pos.astype(np.float32) * freq[None, :]).astype(np.float32)
            for half in range(2):
                at = b * DH + rc * 32 + half * 16
                t[:, C_COS + at:C_COS + at + 16] = np.cos(ang)
                t[:, C_SIN + at:C_SIN + at + 16] = np.sin(ang) * (-1.0 if half == 0 else 1.0)
    pool = np.zeros((TOK, len(WINDOWS), TOK), np.float32)
    s, q = np.arange(TOK)[:, None], np.arange(TOK)[None, :]
    for g, w in enumerate(WINDOWS):
        lo, hi = np.clip(q - w // 2, 0, TOK), np.clip(q - w // 2 + w, 0, TOK)
        pool[:, g, :] = ((s >= lo) & (s < hi)) / (hi - lo).astype(np.float32) - (s == q)
    return t, np.ascontiguousarray(pool.reshape(NB, P, len(WINDOWS) * TOK).transpose(1, 0, 2))


def build(nc, a):
    ctx = ExitStack()
    base = (nc.sbuf_base + 63) // 64 * 64
    top = [base]
    at = {}

    def region(name, size):
        at[name] = top[0]
        top[0] += size

    KB_ = 1024
    region("raw", 32 * KB_)
    region("whi", 16 * KB_)
    region("wlo", 16 * KB_)
    region("h", 32 * KB_)
    region("act", 32 * KB_)
    region("y", 16 * KB_)
    region("x", 16 * KB_)
    region("ada", 24 * KB_)
    region("tmp", 18 * KB_)
    region("small", nc.sbuf_usable_end - top[0])
    small_at = [at["small"]]

    def place(name, shape, where, off=0, dt=F32):
        return nc.alloc_sbuf_tensor_at(name, shape, dt, offset=at[where] + off)

    def small(name, shape):
        t = nc.alloc_sbuf_tensor_at(name, shape, F32, offset=small_at[0])
        size = 4
        for n in shape[1:]:
            size *= n
        small_at[0] += (size + 31) // 32 * 32
        assert small_at[0] <= nc.sbuf_usable_end
        return t

    raw = place("raw", [P, 4, LOADK, N], "raw")
    w_hi = place("w_hi", [P, 4, STEPK, N], "whi", dt=F32R)
    w_lo = place("w_lo", [P, 4, STEPK, N], "wlo", dt=F32R)
    h_hi = place("h_hi", [P, KT, TOK], "h", dt=F32R)
    h_lo = place("h_lo", [P, KT, TOK], "h", 16 * KB_, F32R)
    a_hi = place("a_hi", [P, KT, TOK], "act", dt=F32R)
    a_lo = place("a_lo", [P, KT, TOK], "act", 16 * KB_, F32R)
    y = place("y", [P, NB, D], "y")
    x = place("x", [P, NB, D], "x")
    o1 = place("o1", [P, NB, D], "x")
    ada_w = place("ada_w", [P, 2, ADA_HALF], "ada")
    ada_acc = place("ada_acc", [P, 2, 2, ADA_HALF], "ada", 8 * KB_)
    u_buf = place("u_buf", [P, NB, N], "tmp")
    conv = place("conv", [P, CK, TOK], "tmp", 4 * KB_)
    prod = place("prod", [P, 2, TOK], "tmp", 8 * KB_)
    row = place("row", [P, D], "tmp", 10 * KB_)
    p1 = place("p1", [P, NB, W_IN1], "act")
    sm1 = [place("sm1a", [P, 8, 3 * P], "y", 16 * KB_ - 12 * KB_), place("sm1b", [P, 8, 3 * P], "tmp")]
    pt1 = place("pt1", [P, 4, 3 * P], "tmp", 12 * KB_)
    assert 2 * W_IN1 * 4 <= (32 + 4) * KB_
    qk1 = place("qk1", [P, 26, TOK], "h")
    tab1 = place("tab1", [P, C_MASK - C_TRI], "h", 26 * KB_)
    cT = place("cT", [P, TOK], "h", 30 * KB_)
    TRI, ONE, ALI, CAU = 0, C_ONE - C_TRI, C_ALI - C_TRI, C_CAU - C_TRI
    p2 = place("p2", [P, NB, W_IN2], "ada")
    c2 = place("c2", [P, NB, N], "ada", 20 * KB_)
    q2t = place("q2t", [P, 8, TOK], "act")
    k2t = place("k2t", [P, KV2, 2 * TOK], "act", 8 * KB_)
    sm2 = place("sm2", [P, 2, 4, N], "act", 16 * KB_)
    o2 = place("o2", [P, NB, 1024], "y")
    pooled = place("pooled", [P, 8, TOK], "y", 8 * KB_)
    pool_a = place("pool_a", [P, NB, 4, TOK], "h")
    pool_w = place("pool_w", [P, 4, 2, PG], "h", 16 * KB_)
    pt2 = place("pt2", [P, 4, N], "tmp")
    tab2 = place("tab2", [P, C_END - C_MASK], "tmp", 8 * KB_)
    rot = place("rot", [P, 20, DH], "tmp", 13 * KB_)
    MASK2, COS2, SIN2 = 0, C_COS - C_MASK, C_SIN - C_MASK
    dup1 = place("dup1", [P, NB, 2, 2, DH], "tmp", 12 * KB_)
    dup2 = place("dup2", [P, 2 * NB, KV2, 2, DH], "tmp")
    final_row = place("final_row", [P, D], "ada")
    square_junk = place("square_junk", [P, D], "tmp")
    stage = place("stage", [P, 6, P], "y")

    ident = small("ident", [P, P])
    gains = small("gains", [P, 120])
    convw = small("convw", [P, 4, CTS // 1])
    bada = small("bada", [P, 96])
    adac = small("adac", [P, 8, KT])
    silu = small("silu", [P, 2, KT])
    comb = small("comb", [P, KT])
    ones_col = small("ones_col", [P, 1])
    ssq = small("ssq", [P, 4])
    rstd = small("rstd", [P, 4])
    mx = small("mx", [P, 2, 16])
    nm = small("nm", [P, 2, 16])
    rs = small("rs", [P, 2, 16])
    es = small("es", [P, 2, 16])
    sink1 = small("sink1", [P, HEADS])
    sink2 = small("sink2", [P, HEADS])
    bforget = small("bforget", [P, HEADS])
    z = small("z", [P, NB, HEADS])
    lf = small("lf", [P, NB, HEADS])
    ct8 = small("ct8", [P, NB, HEADS])
    grow = small("grow", [16, 2, P])

    G = ctx.enter_context(nc.psum_tensor("G", [P, 4, N], F32))
    T = ctx.enter_context(nc.psum_tensor("T", [P, 4, N], F32))

    def sem(name):
        return ctx.enter_context(nc.semaphore(name))

    x_in, table_in, vec_in, misc_in = sem("x_in"), sem("table_in"), sem("vec_in"), sem("misc_in")
    raw_full = [sem(f"raw_full{i}") for i in range(4)]
    hi_ready, lo_ready, step_done = sem("hi_ready"), sem("lo_ready"), sem("step_done")
    bank_evac = sem("bank_evac")
    turned, up_read = sem("turned"), sem("up_read")
    base_ready, tap1, gelu_done, conv_used, a_first, a_ready = (
        sem("base_ready"), sem("tap1"), sem("gelu_done"), sem("conv_used"), sem("a_first"), sem("a_ready"))
    vec_turned, cols_ready, silu_e, silu_ready = sem("vec_turned"), sem("cols_ready"), sem("silu_e"), sem("silu_ready")
    ada_full = [sem("ada_full0"), sem("ada_full1")]
    ada_used, ada_summed, ada_col, ada_zero = sem("ada_used"), sem("ada_summed"), sem("ada_col"), sem("ada_zero")
    squares, mean_ready, root_ready, rstd_ready = sem("squares"), sem("mean_ready"), sem("root_ready"), sem("rstd_ready")
    xn_ready, prep_turned, prep_tmp, prep_hi, h_ready = (
        sem("xn_ready"), sem("prep_turned"), sem("prep_tmp"), sem("prep_hi"), sem("h_ready"))
    comb_ready = sem("comb_ready")
    vchain, achain = sem("vchain"), sem("achain")
    row_full, x_again, ctx_in, tab1_in, tab2_in, pool_in, final_in = (
        sem("row_full"), sem("x_again"), sem("ctx_in"), sem("tab1_in"), sem("tab2_in"), sem("pool_in"), sem("final_in"))
    row_used, y_zero, s_max = sem("row_used"), sem("y_zero"), sem("s_max")
    z_ready, e_ready, e1_ready, l_ready, lf_ready, c_done, c_ready = (
        sem("z_ready"), sem("e_ready"), sem("e1_ready"), sem("l_ready"), sem("lf_ready"), sem("c_done"), sem("c_ready"))
    qk_turned, qk_act, qk_dve = sem("qk_turned"), sem("qk_act"), sem("qk_dve")
    s_ready, s_read, nm_ready, es_ready, p_ready, pt_turned, pt_ready, pt_used, o_evac = (
        sem("s_ready"), sem("s_read"), sem("nm_ready"), sem("es_ready"), sem("p_ready"), sem("pt_turned"),
        sem("pt_ready"), sem("pt_used"), sem("o_evac"))
    dup_ready, rope_done, pooled_mm, pooled_ev, mixed_mm, mixed_hi, mixed_lo = (
        sem("dup_ready"), sem("rope_done"), sem("pooled_mm"), sem("pooled_ev"), sem("mixed_mm"), sem("mixed_hi"), sem("mixed_lo"))
    g_turned, g_copied, g_stored = sem("g_turned"), sem("g_copied"), sem("g_stored")
    out_ready, out_stored = sem("out_ready"), sem("out_stored")

    ada_rows = nc.dram_tensor("ada_rows", (2, D), F32, kind="Internal").ap()

    def tiles(w):
        return w.rearrange("(t p) n -> p t n", p=P)

    w_in1, w_out1, w_down1 = tiles(a["w_in"][0]), tiles(a["w_out"][0]), tiles(a["w_down"][0])
    w_up1 = a["w_up"][0].rearrange("(t p) (two f) -> p t two f", p=P, two=2)
    w_in2, w_out2 = tiles(a["w_in_2"][0]), tiles(a["w_out_2"][0])
    w_up2, w_down2 = tiles(a["w_mlp_up_2"][0]), tiles(a["w_mlp_down_2"][0])
    w_ada = tiles(a["w_ada_2"][0])

    def tokens(t):
        return t[0].rearrange("(b p) n -> p b n", p=P)

    C_C, C_CTX, PRE_MIX, GRP, PRE_FFN, NORM_A, NORM_M, POOL_S = [16 * i for i in range(8)]
    PREP = {"in1": (0, 4), "out1": (4, 4), "up1": (8, 4), "in2": (12, 4), "ctx": (16, 4), "out2": (20, 2), "up2": (22, 4)}
    NORMED = {"in1": 0, "out1": 4, "up1": 8, "in2": 12, "ctx": 16, "up2": 20}
    STAT = {"in1": 0, "out1": 1, "y1": 2, "up1": 3, "y2": 4, "in2": 5, "ctx": 6, "up2": 7, "final": 8}

    def tt(pair):
        return T[:, 2 * pair:2 * pair + 2, :].rearrange("p a (j n) -> p (a j) n", n=TOK)

    block = ctx.enter_context(nc.Block())

    @block.sync
    def _(sp):
        sp.dma_start(x[:], tokens(a["x"])).then_inc(x_in, 16)

        def load(l, src, d=0):
            if l >= 4:
                sp.wait_ge(lo_ready, 2 * l - 6 + 2 * d)
            for k in range(2):
                if len(src.shape) == 4:
                    dst, part = raw[:, l % 4, :, GV * k:GV * k + GV], src[:, :, k, :]
                else:
                    rows = slice(STEPK * k, STEPK * k + STEPK)
                    dst, part = raw[:, l % 4, rows, 0:src.shape[2]], src[:, rows, :]
                sp.dma_start(dst, part).then_inc(raw_full[l % 4], 16)

        def chunk(l, w, col, d=0, width=N, t0=0, loads=4):
            for k in range(loads):
                load(l + k, w[:, bass.ds(t0 + LOADK * k, LOADK), bass.ds(col, width)], d)

        def up_chunk(l, c, d=0):
            for k in range(4):
                load(l + k, w_up1[:, LOADK * k:LOADK * k + LOADK, :, bass.ds(c * GV, GV)], d)

        l0 = FIRST_LOAD["in1"]
        chunk(l0, w_in1, 0)
        with sp.Fori(0, 7) as i:
            chunk(l0 + 4, w_in1, i * N + N, i * 4)
        chunk(l0 + 32, w_in1, 8 * N, width=W_IN1 - 8 * N)
        l0 = FIRST_LOAD["out1"]
        with sp.Fori(0, 4) as i:
            chunk(l0, w_out1, i * N, i * 4)
        c0 = 0
        for g, n in zip("abc", UPS1):
            l0 = FIRST_LOAD["up1" + g]
            with sp.Fori(0, n) as i:
                up_chunk(l0, i + c0, i * 4)
            l0 = FIRST_LOAD["down1" + g]
            if n == 8:
                with sp.Fori(0, 4) as i:
                    chunk(l0, w_down1, i * N, i * 4, t0=2 * c0)
            else:
                for c in range(4):
                    chunk(l0 + 3 * c, w_down1, c * N, t0=2 * c0, loads=3)
            c0 += n
        l0 = FIRST_LOAD["in2"]
        for k, col in enumerate((0, N, U2, U2 + N, K2)):
            chunk(l0 + 4 * k, w_in2, col)
        l0 = FIRST_LOAD["out2"]
        with sp.Fori(0, 4) as i:
            chunk(l0, w_out2, i * N, i * 4)
        l0 = FIRST_LOAD["mlp2"]
        with sp.Fori(0, GROUPS2) as g:
            for c in range(4):
                chunk(l0 + 4 * c, w_up2, g * (4 * N) + c * N, g * 32)
            for c in range(4):
                for k in range(4):
                    load(l0 + 16 + 4 * c + k,
                         w_down2[:, bass.ds(g * KT + LOADK * k, LOADK), c * N:c * N + N], g * 32)
        for b in range(NB):
            sp.wait_ge(out_ready, b + 1)
            sp.dma_start(tokens(a["out"])[:, b, :], y[:, b, :]).then_inc(out_stored, 16)
        sp.wait_ge(out_stored, 16 * NB)

    @block.gpsimd
    def _(pool):
        def ada(q):
            part = ADA_ORDER[q][0]

            def tile(t, half, wait):
                if wait is not None:
                    pool.wait_ge(ada_used, wait)
                pool.dma_start(ada_w[:, half, :],
                               w_ada[:, bass.ds(t, 1), part * D + half * ADA_HALF:part * D + (half + 1) * ADA_HALF]
                               .rearrange("p a n -> p (a n)")).then_inc(ada_full[half], 16)

            if q == 0:
                tile(0, 0, None)
                tile(0, 1, None)
                with pool.Fori(1, KT) as t:
                    tile(t, 0, t * 2 - 1)
                    tile(t, 1, t * 2)
            else:
                with pool.Fori(0, KT) as t:
                    tile(t, 0, t * 2 + (32 * q - 1))
                    tile(t, 1, t * 2 + 32 * q)

        def load_row(src):
            pool.dma_start(row[:], src.broadcast_to([P, D])).then_inc(row_full, 16)

        ada(0)
        pool.wait_ge(bank_evac, FIRST_EVAC["out1"])
        pool.dma_start(tab1[:], a["table"][:, C_TRI:C_MASK]).then_inc(tab1_in, 16)

        def twice(dst, src, n):
            return pool.tensor_copy(dst, src.rearrange("p (g d) -> p g d", d=DH).unsqueeze(2).broadcast_to([P, n, 2, DH]))

        for b in range(NB):
            ins = twice(dup1[:, b], p1[:, b, KA:KA + 2 * DH], 2)
        ins.then_inc(dup_ready, 1)
        pool.wait_ge(o_evac, 4)
        load_row(a["post_mix_g"])
        ada(1)
        pool.wait_ge(h_ready, PREP["out1"][0] + 4)
        pool.dma_start(x[:], tokens(a["x"])).then_inc(x_again, 16)
        pool.wait_ge(row_used, 1)
        load_row(a["post_ffn_g"])
        for q in range(2, 6):
            ada(q)
        pool.wait_ge(g_copied, 1)
        pool.dma_start(ada_rows.rearrange("r (t p) -> t r p", p=P), grow[:]).then_inc(g_stored, 16)
        pool.wait_ge(h_ready, PREP["in2"][0] + 4)
        pool.dma_start(y[:], tokens(a["ctx_2"])).then_inc(ctx_in, 16)
        pool.wait_ge(row_used, 2)
        pool.wait_ge(h_ready, PREP["ctx"][0] + 4)
        pool.dma_start(tab2[:], a["table"][:, C_MASK:C_END]).then_inc(tab2_in, 16)
        pool.wait_ge(bank_evac, FIRST_EVAC["out2"])
        pool.dma_start(pool_a[:], a["pool_table"].rearrange("p b (g t) -> p b g t", g=4)).then_inc(pool_in, 16)
        pool.dma_start(pool_w[:], a["pool_w_2"][0].rearrange("g (c p) d -> p g c d", p=P)).then_inc(pool_in, 16)
        for b in range(NB):
            twice(dup2[:, NB + b], c2[:, b, 0:KV2 * DH], KV2)
        pool.wait_ge(rope_done, NB)
        for b in range(NB):
            ins = twice(dup2[:, b], p2[:, b, K2:K2 + KV2 * DH], KV2)
        ins.then_inc(dup_ready, 1)
        pool.wait_ge(g_stored, 16)
        pool.wait_ge(o_evac, 6)
        pool.wait_ge(mixed_lo, 8)
        load_row(ada_rows[0:1, :])
        pool.dma_start(final_row[:], a["final_norm_w_2"].rearrange("(a n) -> a n", a=1).broadcast_to([P, D])).then_inc(final_in, 16)
        pool.wait_ge(row_used, 3)
        load_row(ada_rows[1:2, :])

    @block.scalar
    def _(act):
        chain = [0]

        def link(ins):
            chain[0] += 1
            ins.then_inc(achain, 1)
            act.wait_ge(achain, chain[0])

        act.dma_start(ident[:], a["table"][:, C_ID:C_ID + P]).then_inc(table_in, 16)
        rows = [a["c_2"][0], a["c_ctx_2"], a["pre_mix_g"][0], a["grp_swa_g"][0], a["grp_fox_g"][0], a["pre_ffn_g"][0],
                a["norm_attn_w_2"][0], a["norm_mlp_w_2"][0], a["pool_scale_2"][0]]
        r0 = 0
        for v in rows:
            n = v.shape[0] // P
            act.dma_start(stage[r0:r0 + n, 0, :], v.rearrange("(t p) -> t p", p=P)).then_inc(vec_in, 16)
            r0 += n
        assert r0 == 120
        for k in range(3):
            act.dma_start(stage[0:CTS, 1 + k, :], a["conv_w"][0, k].rearrange("(t p) -> t p", p=P)).then_inc(vec_in, 16)
        act.dma_start(stage[0:CTS, 4, :], a["conv_b"][0].rearrange("(t p) -> t p", p=P)).then_inc(vec_in, 16)
        act.dma_start(stage[0:96, 5, :], a["b_ada_2"][0].rearrange("(t p) -> t p", p=P)).then_inc(vec_in, 16)
        act.dma_start(sink1[:], a["sinks"].broadcast_to([P, HEADS])).then_inc(misc_in, 16)
        act.dma_start(sink2[:], a["attn_sink_2"].broadcast_to([P, HEADS])).then_inc(misc_in, 16)
        act.dma_start(bforget[:], a["b_forget"].broadcast_to([P, HEADS])).then_inc(misc_in, 16)

        def stats(k, src, junk=G):
            for n, part in enumerate(src):
                ins = act.activation(junk[:, :, :].rearrange("p a n -> p (a n)")[:, n * 1024:n * 1024 + part.shape[1]], part,
                                     ACT.Square, accum_out=ssq[:, 2 * n + 1:2 * n + 2])
            ins.then_inc(squares, 1)
            act.wait_ge(mean_ready, k + 1)
            act.activation(rstd[:, 0:2 * len(src)], ssq[:, 0:2 * len(src)], ACT.Sqrt).then_inc(root_ready, 1)

        def scale_rows(name, src, dst, groups, cols=None):
            if name in STAT:
                act.wait_ge(rstd_ready, STAT[name] + 1)
            for g in range(groups):
                for b in range(NB):
                    r = rstd[:, b:b + 1] if cols is None else rstd[:, 2 * (g // cols) + b:2 * (g // cols) + b + 1]
                    ins = act.activation(dst[:, b, g * N:(g + 1) * N], src[:, b, g * N:(g + 1) * N], ACT.Copy, scale=r)
                ins.then_inc(xn_ready, 1)

        def split_prep(name, hi):
            n0, n = PREP[name]
            for g in range(n):
                act.wait_ge(prep_tmp, n0 + g + 1)
                tmp = (u_buf, conv)[g % 2][:].rearrange("p a b -> p (a b)")
                act.activation(hi[:, 4 * g:4 * g + 4, :].rearrange("p a b -> p (a b)"), tmp, ACT.Copy).then_inc(prep_hi, 1)

        def hi(s, d=0):
            if s % 2 == 0:
                act.wait_ge(raw_full[s // 2 % 4], 32 * (s // 8 + 1) + d * 4)
            if s >= 4:
                act.wait_ge(step_done, s - 3 + d)
            act.activation(w_hi[:, s % 4], raw[:, s // 2 % 4, STEPK * (s % 2):STEPK * (s % 2) + STEPK, :],
                           ACT.Copy).then_inc(hi_ready, 1)

        def his(s, n, d=0):
            for k in range(n):
                if s + k < STEPS:
                    hi(s + k, d)

        def body(s, d=0, post=None, n=8):
            his(s + 3, 3, d)
            if post:
                post[0]()
            his(s + 6, 1, d)
            if post:
                post[1]()
            his(s + 7, n - 4, d)

        def evac(dst, parity, func=ACT.Copy, width=N, s=None, d=0):
            act.wait_ge(step_done, s + d)
            for b in range(NB):
                act.activation(dst(b), G[:, 2 * parity + b, 0:width], func).then_inc(bank_evac, 1)

        act.wait_ge(x_in, 16)
        stats(0, [x[:, 1, :]])
        scale_rows("in1", x, x, 4)
        act.wait_ge(cols_ready, 1)
        act.activation(silu[:].rearrange("p a b -> p (a b)"), gains[:, 0:32], ACT.Exp, scale=-1.0).then_inc(silu_e, 1)
        split_prep("in1", h_hi)
        his(0, 3)

        s0 = 2 * FIRST_LOAD["in1"]
        with act.Fori(0, 4) as i:
            for c in range(2):
                body(s0 + 8 * c, i * 16)
                evac(lambda b: p1[:, b, bass.ds(i * (2 * N) + c * N, N)], c, s=s0 + 8 * c + 8, d=i * 16)
        body(s0 + 64)
        evac(lambda b: p1[:, b, 8 * N:W_IN1], 0, width=W_IN1 - 8 * N, s=s0 + 72)

        act.wait_ge(z_ready, 1)
        act.activation(lf[:], z[:], ACT.Exp, scale=-1.0).then_inc(e_ready, 1)
        act.wait_ge(e1_ready, 1)
        act.activation(lf[:], lf[:], ACT.Ln).then_inc(l_ready, 1)
        for g in range(7):
            act.wait_ge(qk_turned, g + 1)
            act.activation(qk1[:, 4 * g:4 * g + 2, :], tt(g % 2)[:, 0:2, :], ACT.Copy).then_inc(qk_act, 1)
        for b in range(4):
            act.wait_ge(nm_ready, b + 1)
            if b < 2:
                act.activation(es[:, b, :], es[:, b, :], ACT.Exp).then_inc(es_ready, 1)
            for i in range(8):
                n = 8 * b + i
                act.activation(sm1[b % 2][:, i, 0:P], sm1[b % 2][:, i, 0:P], ACT.Exp, scale=SCALE,
                               bias=nm[:, b % 2, 2 * i:2 * i + 1], accum_out=rs[:, b % 2, 2 * i:2 * i + 1])
                act.activation(sm1[b % 2][:, i, P:3 * P], sm1[b % 2][:, i, P:3 * P], ACT.Exp, scale=SCALE,
                               bias=nm[:, b % 2, 2 * i + 1:2 * i + 2],
                               accum_out=rs[:, b % 2, 2 * i + 1:2 * i + 2]).then_inc(p_ready, 1)
            for i in range(8):
                n = 8 * b + i
                act.wait_ge(pt_turned, n + 1)
                if n >= 4:
                    act.wait_ge(pt_used, n - 3)
                act.activation(pt1[:, n % 4, :], T[:, n % 2, 0:3 * P], ACT.Copy).then_inc(pt_ready, 1)
        act.wait_ge(o_evac, 4)
        stats(1, [o1[:, 1, 0:1024], o1[:, 1, 1024:2048]])
        scale_rows("out1", o1, o1, 4, cols=2)
        split_prep("out1", h_hi)

        s0 = 2 * FIRST_LOAD["out1"]
        with act.Fori(0, 2) as i:
            for c in range(2):
                body(s0 + 8 * c, i * 16)
                evac(lambda b: y[:, b, bass.ds(i * (2 * N) + c * N, N)], c, s=s0 + 8 * c + 8, d=i * 16)
        act.wait_ge(bank_evac, FIRST_EVAC["up1a"])
        stats(2, [y[:, 1, :]])
        act.wait_ge(row_used, 1)
        stats(3, [x[:, 1, :]])
        scale_rows("up1", x, y, 4)
        split_prep("up1", h_hi)

        def up_evac(c, e, d, func):
            evac(lambda b: u_buf[:, b, :], c % 2, func, s=e, d=d)

        def post1(u, tile, du=0, dt=0):
            def taps():
                act.wait_ge(turned, u + 1 + du)
                if u >= 1:
                    act.wait_ge(conv_used, u + du)
                for j in range(CK):
                    t = (tile + j) if j < 2 else (CT1 + tile + j - 2)
                    ins = act.activation(conv[:, j, :], tt(0)[:, j, :], ACT.Identity,
                                         scale=convw[:, 2, bass.ds(t + dt, 1)], bias=convw[:, 3, bass.ds(t + dt, 1)])
                ins.then_inc(base_ready, 1)

            def gelu():
                act.wait_ge(up_read, u + 1 + du)
                act.activation(conv[:, 0:2, :], conv[:, 0:2, :], ACT.Gelu_apprx_tanh).then_inc(gelu_done, 1)

            return taps, gelu

        tile = 0
        for g, n in zip("abc", UPS1):
            s0, u0 = 2 * FIRST_LOAD["up1" + g], UP0["up1" + g]
            body(s0)
            up_evac(0, s0 + 8, 0, ACT.Copy)
            body(s0 + 8, 0, post1(u0, tile))
            up_evac(1, s0 + 16, 0, ACT.Copy)
            with act.Fori(0, n // 2 - 1) as i:
                for c in range(2):
                    body(s0 + 16 + 8 * c, i * 16, post1(u0 + 1 + c, tile + 2 + 2 * c, i * 2, i * 4))
                    up_evac(c, s0 + 24 + 8 * c, i * 16, ACT.Copy)
            tile += 2 * n
            s0, per = 2 * FIRST_LOAD["down1" + g], 8 if n == 8 else 6
            body(s0, 0, post1(u0 + n - 1, tile - 2), per)
            for c in range(1, 4):
                body(s0 + per * c, n=per)
        act.wait_ge(bank_evac, FIRST_EVAC["in2"])
        stats(4, [y[:, 1, :]])
        act.wait_ge(row_used, 2)
        stats(5, [x[:, 1, :]])
        scale_rows("in2", x, y, 4)
        split_prep("in2", h_hi)

        s0 = 2 * FIRST_LOAD["in2"]
        for k, col in enumerate((0, N, U2, U2 + N)):
            body(s0 + 8 * k)
            evac(lambda b: p2[:, b, col:col + N], k % 2, s=s0 + 8 * k + 8)
            if k == 0:
                act.wait_ge(ctx_in, 16)
                stats(6, [y[:, 1, :]], T)
                scale_rows("ctx", y, y, 4)
            if k == 1:
                split_prep("ctx", a_hi)
        body(s0 + 32)
        act.wait_ge(step_done, s0 + 40)
        for b in range(NB):
            act.activation(p2[:, b, K2:K2 + N], G[:, b, :], ACT.Copy).then_inc(bank_evac, 1)
            act.activation(c2[:, b, :], G[:, 2 + b, :], ACT.Copy).then_inc(bank_evac, 1)

        for g in range(4):
            act.wait_ge(qk_turned, 7 + g + 1)
            dst = q2t[:, 4 * g:4 * g + 2, :] if g < 2 else k2t[:, 2 * (g - 2), :].rearrange("p (a n) -> p a n", a=2)
            act.activation(dst, tt((7 + g) % 2)[:, 0:2, :], ACT.Copy).then_inc(qk_act, 1)
        for b in range(8):
            act.wait_ge(nm_ready, 4 + b + 1)
            half, q0 = b // 4, 4 * (b % 4)
            act.activation(es[:, half, q0:q0 + 4], es[:, half, q0:q0 + 4], ACT.Exp).then_inc(es_ready, 1)
            for i in range(4):
                act.activation(sm2[:, b % 2, i, :], sm2[:, b % 2, i, :], ACT.Exp, scale=SCALE,
                               bias=nm[:, half, q0 + i:q0 + i + 1],
                               accum_out=rs[:, half, q0 + i:q0 + i + 1]).then_inc(p_ready, 1)
            for i in range(4):
                n = 32 + 4 * b + i
                act.wait_ge(pt_turned, n + 1)
                act.wait_ge(pt_used, n - 3)
                act.activation(pt2[:, n % 4, :], T[:, n % 2, :], ACT.Copy).then_inc(pt_ready, 1)
        for g in range(4):
            act.wait_ge(pooled_mm, g + 1)
            act.activation(pooled[:, 2 * g:2 * g + 2, :], G[:, g, :].rearrange("p (a n) -> p a n", a=2),
                           ACT.Copy).then_inc(pooled_ev, 1)
        split_prep("out2", h_hi)

        s0 = 2 * FIRST_LOAD["out2"]
        with act.Fori(0, 2) as i:
            for c in range(2):
                body(s0 + 8 * c, i * 16)
                evac(lambda b: y[:, b, bass.ds(i * (2 * N) + c * N, N)], c, s=s0 + 8 * c + 8, d=i * 16)
        act.wait_ge(row_used, 3)
        stats(7, [x[:, 1, :]])
        scale_rows("up2", x, y, 4)
        split_prep("up2", h_hi)

        s0, u0 = 2 * FIRST_LOAD["mlp2"], UP0["mlp2"]

        def post2(u, du):
            def square():
                act.wait_ge(turned, u + 1 + du)
                act.wait_ge(a_ready, u + du)
                act.activation(conv[:], tt(0), ACT.Square).then_inc(up_read, 1)

            return square, lambda: None

        def group2(s, u, d, du):
            for c in range(4):
                body(s + 8 * c, d, post2(u + c - 1, du) if c else None)
                up_evac(c, s + 8 * c + 8, d, ACT.Relu)
            for c in range(4):
                body(s + 32 + 8 * c, d, None if c else post2(u + 3, du))

        with act.Fori(0, GROUPS2 - 1) as g:
            group2(s0, u0, g * 64, g * 4)
        group2(s0 + 64 * (GROUPS2 - 1), u0 + 4 * (GROUPS2 - 1), 0, 0)
        act.wait_ge(row_used, 4)
        stats(8, [x[:, 1, :]])

    @block.vector
    def _(dve):
        chain = [0]

        def link(ins):
            chain[0] += 1
            ins.then_inc(vchain, 1)
            dve.wait_ge(vchain, chain[0])

        def lo(s, d=0):
            if s >= STEPS:
                return
            dve.wait_ge(hi_ready, s + 1 + d)
            dve.tensor_tensor(w_lo[:, s % 4], raw[:, s // 2 % 4, STEPK * (s % 2):STEPK * (s % 2) + STEPK, :],
                              w_hi[:, s % 4].bitcast(F32), ALU.subtract).then_inc(lo_ready, 1)

        def los(s, n, d=0):
            for k in range(n):
                lo(s + k, d)

        def ada_op(q, k, d=0, dt=0):
            half = k % 2
            n = 32 * q + k
            dve.wait_ge(ada_full[half], 16 * (n // 2 + 1) + dt * 16)
            dve.wait_ge(ada_used, n + d)
            conds = 2 if ADA_ORDER[q][1] else 1
            for c in range(conds):
                ins = dve.scalar_tensor_tensor(out=ada_acc[:, c, half, :], in0=ada_w[:, half, :],
                                               scalar=silu[:, c, bass.ds(dt + k // 2, 1)],
                                               in1=ada_acc[:, c, half, :], op0=ALU.mult, op1=ALU.add)
            ins.then_inc(ada_used, 1)

        def ada_zeros():
            dve.memset(ada_acc[:], 0.0).then_inc(ada_zero, 1)

        def ada_finish(q):
            dve.wait_ge(ada_summed, q + 1)
            part, both = ADA_ORDER[q]
            dve.tensor_tensor(adac[:, part, :], T[:, 3, 0:KT], bada[:, KT * part:KT * part + KT], ALU.add)
            if both:
                dve.tensor_tensor(adac[:, 6 + part, :], T[:, 3, KT:2 * KT], bada[:, KT * part:KT * part + KT], ALU.add)
            dve.memset(ada_acc[:], 0.0).then_inc(ada_col, 1)
            dve.wait_ge(ada_col, q + 1)

        def stats(k, src, width):
            for n, part in enumerate(src):
                ins = dve.tensor_tensor_reduce(square_junk[:, n * 1024:n * 1024 + part.shape[1]], part, part,
                                               1.0, 0.0, ALU.mult, ALU.add, ssq[:, 2 * n:2 * n + 1])
            ins.then_inc(squares, 1)
            dve.wait_ge(squares, 2 * k + 2)
            w = 2 * len(src)
            dve.tensor_scalar(ssq[:, 0:w], ssq[:, 0:w], 1.0 / width, EPS, ALU.mult, ALU.add).then_inc(mean_ready, 1)
            dve.wait_ge(root_ready, k + 1)
            dve.reciprocal(rstd[:, 0:w], rstd[:, 0:w]).then_inc(rstd_ready, 1)
            dve.wait_ge(rstd_ready, k + 1)

        def prep(name, gain, hi, lo_out, shift=None):
            n0, n = PREP[name]

            def rest(g):
                dve.wait_ge(prep_hi, n0 + g + 1)
                tmp = (u_buf, conv)[g % 2][:].rearrange("p a b -> p (a b)")
                dve.tensor_tensor(lo_out[:, 4 * g:4 * g + 4, :].rearrange("p a b -> p (a b)"), tmp,
                                  hi[:, 4 * g:4 * g + 4, :].rearrange("p a b -> p (a b)").bitcast(F32),
                                  ALU.subtract).then_inc(h_ready, 1)

            for g in range(n):
                dve.wait_ge(prep_turned, n0 + g + 1)
                if g >= 2:
                    dve.wait_ge(h_ready, n0 + g - 1)
                tmp = (u_buf, conv)[g % 2][:].rearrange("p a b -> p (a b)").rearrange("p (j n) -> p j n", n=TOK)
                for j in range(4):
                    k = 4 * g + j
                    if gain is None:
                        ins = dve.tensor_copy(tmp[:, j, :], tt(g % 2)[:, j, :])
                    elif shift is None:
                        ins = dve.tensor_scalar(tmp[:, j, :], tt(g % 2)[:, j, :], gain[:, k:k + 1], None, ALU.mult)
                    else:
                        ins = dve.tensor_scalar(tmp[:, j, :], tt(g % 2)[:, j, :], gain[:, k:k + 1],
                                                shift[:, k:k + 1], ALU.mult, ALU.add)
                ins.then_inc(prep_tmp, 1)
                if g >= 1:
                    rest(g - 1)
            rest(n - 1)

        dve.memset(ones_col[:], 1.0)
        ada_zeros()
        dve.wait_ge(vec_turned, 1)
        dve.tensor_copy(gains[:], T[:, 0, 0:120])
        dve.tensor_copy(convw[:].rearrange("p a b -> p (a b)"), T[:, 1, 0:4 * CTS])
        dve.tensor_copy(bada[:], T[:, 2, 0:96]).then_inc(cols_ready, 1)
        dve.wait_ge(cols_ready, 1)
        dve.wait_ge(x_in, 16)
        stats(0, [x[:, 0, :]], D)
        dve.wait_ge(silu_e, 1)
        flat = silu[:].rearrange("p a b -> p (a b)")
        link(dve.tensor_scalar(flat, flat, 1.0, None, ALU.add))
        link(dve.reciprocal(flat, flat))
        link(dve.tensor_tensor(flat, flat, gains[:, 0:32], ALU.mult))
        prep("in1", gains[:, PRE_MIX:], h_hi, h_lo)
        los(0, 3)
        dve.wait_ge(ada_zero, 1)

        s0 = 2 * FIRST_LOAD["in1"]
        with dve.Fori(0, 8) as i:
            for k in range(8):
                lo(s0 + 3 + k, i * 8)
                if k % 2 == 1:
                    half = (k // 2) % 2
                    dve.wait_ge(ada_full[half], 16 + i * 32 + 16 * (k // 4))
                    for c in range(2):
                        ins = dve.scalar_tensor_tensor(out=ada_acc[:, c, half, :], in0=ada_w[:, half, :],
                                                       scalar=silu[:, c, bass.ds(i * 2 + k // 4, 1)],
                                                       in1=ada_acc[:, c, half, :], op0=ALU.mult, op1=ALU.add)
                    ins.then_inc(ada_used, 1)
                    dve.wait_ge(ada_used, i * 4 + k // 2 + 1)
        los(s0 + 67, 8)
        ada_finish(0)

        dve.wait_ge(bank_evac, FIRST_EVAC["out1"])
        dve.wait_ge(misc_in, 48)
        for b in range(NB):
            ins = dve.tensor_tensor(ct8[:, b, :], p1[:, b, FB:FB + HEADS], bforget[:], ALU.add)
        link(ins)
        link(dve.tensor_scalar(z[:], ct8[:], -1.0, None, ALU.mult))
        dve.tensor_tensor(z[:], z[:], ct8[:], ALU.max).then_inc(z_ready, 1)
        link(dve.tensor_scalar(ct8[:], ct8[:], 0.0, None, ALU.min))
        dve.wait_ge(e_ready, 1)
        dve.tensor_scalar(lf[:], lf[:], 1.0, None, ALU.add).then_inc(e1_ready, 1)
        dve.wait_ge(l_ready, 1)
        dve.tensor_tensor(lf[:], ct8[:], lf[:], ALU.subtract).then_inc(lf_ready, 1)
        dve.wait_ge(c_done, 1)
        dve.tensor_scalar(ct8[:], G[:, 0, 0:2 * HEADS].rearrange("p (b h) -> p b h", b=NB), 1 / SCALE, None, ALU.mult)
        link(dve.memset(cT[:], 0.0))
        dve.tensor_scalar(cT[0:HEADS, :], G[0:HEADS, 1, 0:TOK], -1 / SCALE, None, ALU.mult).then_inc(c_ready, 1)
        for g in range(6):
            dve.wait_ge(qk_turned, g + 1)
            dve.tensor_copy(qk1[:, 4 * g + 2:4 * g + 4, :], tt(g % 2)[:, 2:4, :]).then_inc(qk_dve, 1)
        dve.wait_ge(tab1_in, 16)
        slopes = 2.0 ** (-8.0 * np.arange(1, HEADS + 1) / HEADS)
        dve.wait_ge(c_ready, 1)

        def scores(b):
            if b >= 2:
                dve.wait_ge(pt_turned, 8 * (b - 1))
            for i in range(8):
                n = 8 * b + i
                bank = G[:, n % 4, :]
                dst = sm1[b % 2][:, i, :]
                dve.wait_ge(s_ready, n + 1)
                if b < 2:
                    ins = dve.scalar_tensor_tensor(out=dst, in0=tab1[:, ALI:ALI + 3 * P], scalar=float(slopes[n] / SCALE),
                                                   in1=bank[:, 0:3 * P], op0=ALU.mult, op1=ALU.add)
                else:
                    dve.scalar_tensor_tensor(out=dst[:, 0:P], in0=bank[:, 0:P], scalar=ct8[:, 0, n - 16:n - 15],
                                             in1=tab1[:, CAU:CAU + P], op0=ALU.add, op1=ALU.add)
                    ins = dve.scalar_tensor_tensor(out=dst[:, P:3 * P], in0=bank[:, P:3 * P],
                                                   scalar=ct8[:, 1, n - 16:n - 15], in1=tab1[:, CAU + P:CAU + 3 * P],
                                                   op0=ALU.add, op1=ALU.add)
                ins.then_inc(s_read, 1)
                if i >= 1:
                    maxima(b, i - 1)
            maxima(b, 7)
            dve.wait_ge(s_max, 8 * b + 8)

        def maxima(b, i):
            dve.wait_ge(s_read, 8 * b + i + 1)
            buf = sm1[b % 2]
            dve.reduce_max(mx[:, b % 2, 2 * i:2 * i + 1], buf[:, i, 0:P], AX_X)
            dve.reduce_max(mx[:, b % 2, 2 * i + 1:2 * i + 2], buf[:, i, P:3 * P], AX_X).then_inc(s_max, 1)

        def sinks(b):
            m, n_ = mx[:, b % 2, :], nm[:, b % 2, :]
            if b >= 2:
                dve.tensor_scalar(n_, m, -SCALE, None, ALU.mult).then_inc(nm_ready, 1)
                return
            link(dve.tensor_scalar(m, m, SCALE, None, ALU.mult))
            s = sink1[:, 8 * b:8 * b + 8].unsqueeze(2).broadcast_to([P, 8, 2])
            m3 = m.rearrange("p (h b) -> p h b", b=2)
            link(dve.tensor_tensor(m3, m3, s, ALU.max))
            dve.tensor_tensor(es[:, b, :].rearrange("p (h b) -> p h b", b=2), s, m3, ALU.subtract)
            dve.tensor_scalar(n_, m, -1.0, None, ALU.mult).then_inc(nm_ready, 1)

        def outputs(b):
            dve.wait_ge(pt_used, 8 * b + 8)
            r = rs[:, b % 2, :]
            if b < 2:
                dve.wait_ge(es_ready, b + 1)
                link(dve.tensor_tensor(r, r, es[:, b, :], ALU.add))
            link(dve.reciprocal(r, r))
            for k in range(NB):
                f = r.rearrange("p (h b) -> p h b", b=2)[:, :, k:k + 1].broadcast_to([P, 8, DH])
                ins = dve.tensor_tensor(o1[:, k, N * b:N * b + N].rearrange("p (h d) -> p h d", d=DH),
                                        T[:, 2 + k, :].rearrange("p (h d) -> p h d", d=DH), f, ALU.mult)
            ins.then_inc(o_evac, 1)

        scores(0)
        sinks(0)
        for b in range(4):
            if b < 3:
                scores(b + 1)
                sinks(b + 1)
            outputs(b)
        dve.wait_ge(o_evac, 4)
        stats(1, [o1[:, 0, 0:1024], o1[:, 0, 1024:2048]], 1024)
        prep("out1", gains[:, GRP:], h_hi, h_lo)

        s0 = 2 * FIRST_LOAD["out1"]
        with dve.Fori(0, 4) as i:
            for k in range(8):
                lo(s0 + 3 + k, i * 8)
                ada_op(1, k, i * 8, i * 4)
        ada_finish(1)

        def residual(k, scale, e):
            if e is not None:
                dve.wait_ge(bank_evac, e)
            for b in range(NB):
                s = rstd[:, b:b + 1] if scale else 1.0
                ins = dve.scalar_tensor_tensor(out=y[:, b, :], in0=y[:, b, :], scalar=s, in1=row[:],
                                               op0=ALU.mult, op1=ALU.mult)
            link(ins)
            dve.tensor_tensor(x[:].rearrange("p b n -> p (b n)"), x[:].rearrange("p b n -> p (b n)"),
                              y[:].rearrange("p b n -> p (b n)"), ALU.add).then_inc(row_used, 1)
            dve.wait_ge(row_used, k + 1)

        dve.wait_ge(bank_evac, FIRST_EVAC["up1a"])
        stats(2, [y[:, 0, :]], D)
        dve.wait_ge(row_full, 16)
        dve.wait_ge(x_again, 16)
        residual(0, True, None)
        stats(3, [x[:, 0, :]], D)
        prep("up1", gains[:, PRE_FFN:], h_hi, h_lo)
        dve.wait_ge(prep_turned, PREP["up1"][0] + 4)
        dve.memset(y[:], 0.0).then_inc(y_zero, 1)
        dve.wait_ge(y_zero, 1)

        def body(s, d=0, post=None, n=8, adas=()):
            adas = list(adas)
            for k in range(n):
                lo(s + 3 + k, d)
                if post and k == 2:
                    post[0]()
                elif post and k == 3:
                    post[1]()
                elif not post or k >= 4:
                    left = n - k if not post else n - max(k, 4)
                    for _ in range(-(-len(adas) // left)):
                        ada_op(*adas.pop(0))

        def post1(u, tile, a_tile, du=0, dt=0):
            def taps():
                dve.wait_ge(base_ready, u + 1 + du)
                for tap in (1, 0):
                    k = 2 - tap
                    for j in range(CK):
                        t = (tile + j) if j < 2 else (CT1 + tile + j - 2)
                        ins = dve.scalar_tensor_tensor(out=conv[:, j, k:TOK], in0=tt(0)[:, j, 0:TOK - k],
                                                       scalar=convw[:, tap, bass.ds(t + dt, 1)], in1=conv[:, j, k:TOK],
                                                       op0=ALU.mult, op1=ALU.add)
                    if tap:
                        ins.then_inc(tap1, 1)
                        dve.wait_ge(tap1, u + 1 + du)
                ins.then_inc(up_read, 1)

            def product():
                hi, lo_ = (t[:, bass.ds(a_tile + dt, 2), :] for t in (a_hi, a_lo))
                dve.wait_ge(gelu_done, u + 1 + du)
                dve.tensor_tensor(prod[:], conv[:, 0:2, :], conv[:, 2:4, :], ALU.mult).then_inc(conv_used, 1)
                dve.wait_ge(conv_used, u + 1 + du)
                dve.tensor_copy(hi, prod[:]).then_inc(a_first, 1)
                dve.wait_ge(a_first, u + 1 + du)
                dve.tensor_tensor(lo_, prod[:], hi.bitcast(F32), ALU.subtract).then_inc(a_ready, 1)

            return taps, product

        def down_evac(c, e, d=0):
            dve.wait_ge(step_done, e + d)
            for b in range(NB):
                dve.tensor_tensor(y[:, b, c * N:c * N + N], y[:, b, c * N:c * N + N], G[:, 2 * (c % 2) + b, :],
                                  ALU.add).then_inc(bank_evac, 1)

        tile = 0
        for g, n, q_up, q_down, fin_up, fin_down in (("a", 8, 2, 3, None, 2), ("b", 8, 4, 5, 3, 4),
                                                     ("c", 6, None, None, 5, None)):
            s0, u0 = 2 * FIRST_LOAD["up1" + g], UP0["up1" + g]
            body(s0)
            if fin_up is not None:
                ada_finish(fin_up)
            if q_up is not None:
                for k in range(4):
                    ada_op(q_up, k)
            with dve.Fori(0, n - 1) as i:
                body(s0 + 8, i * 8, post1(u0, tile, 0, i, i * 2),
                     adas=[(q_up, 4 + k, i * 4, i * 2) for k in range(4)] if q_up is not None else ())
            tile += 2 * n
            s0, per = 2 * FIRST_LOAD["down1" + g], 8 if n == 8 else 6
            body(s0, 0, post1(u0 + n - 1, tile - 2, 2 * n - 2), per)
            down_evac(0, s0 + per)
            if fin_down is not None:
                ada_finish(fin_down)
            done = 0
            for c, tiles_of_ada in ((0, 3), (1, 10), (2, 10), (3, 9)):
                adas = [(q_down, done + k) for k in range(tiles_of_ada)] if q_down is not None else []
                done += tiles_of_ada
                if c == 0:
                    for args in adas:
                        ada_op(*args)
                else:
                    body(s0 + per * c, n=per, adas=adas)
                    down_evac(c, s0 + per * c + per)

        dve.wait_ge(bank_evac, FIRST_EVAC["in2"])
        stats(4, [y[:, 0, :]], D)
        dve.wait_ge(row_full, 32)
        residual(1, True, None)
        stats(5, [x[:, 0, :]], D)

        def combine(norm, part):
            link(dve.tensor_scalar(comb[:], adac[:, part, :], 1.0, None, ALU.add))
            link(dve.tensor_tensor(comb[:], comb[:], gains[:, norm:norm + KT], ALU.mult))

        dve.wait_ge(g_turned, 1)
        dve.tensor_copy(grow[:].rearrange("t r p -> t (r p)"), T[0:16, 3, 0:2 * P]).then_inc(g_copied, 1)
        combine(NORM_A, 1)
        prep("in2", comb, h_hi, h_lo, adac[:, 0, :])

        s0 = 2 * FIRST_LOAD["in2"]
        for k in range(4):
            los(s0 + 8 * k + 3, 8)
            if k == 0:
                dve.wait_ge(ctx_in, 16)
                stats(6, [y[:, 0, :]], D)
            if k == 1:
                combine(NORM_A, 7)
                prep("ctx", comb, a_hi, a_lo, adac[:, 6, :])
        los(s0 + 35, 8)

        dve.wait_ge(bank_evac, FIRST_EVAC["out2"])
        dve.wait_ge(tab2_in, 16)
        cos = tab2[:, COS2:COS2 + 2 * DH].rearrange("p (b d) -> p b d", b=NB)
        sin = tab2[:, SIN2:SIN2 + 2 * DH].rearrange("p (b r s d) -> p b r s d", b=NB, r=2, s=2)
        for b in range(NB):
            qk = p2[:, b, 0:K2 + 256].rearrange("p (h d) -> p h d", d=DH)
            qk5 = p2[:, b, 0:K2 + 256].rearrange("p (h r s d) -> p h r s d", r=2, s=2, d=16)
            rot5 = rot[:].rearrange("p h (r s d) -> p h r s d", r=2, s=2)
            for s in range(2):
                ins = dve.tensor_tensor(rot5[:, :, :, s, :], qk5[:, :, :, 1 - s, :],
                                        sin[:, b, :, s, :].unsqueeze(1).broadcast_to([P, 20, 2, 16]), ALU.mult)
            link(ins)
            link(dve.tensor_tensor(qk, qk, cos[:, b, :].unsqueeze(1).broadcast_to([P, 20, DH]), ALU.mult))
            ins = dve.tensor_tensor(qk, qk, rot[:], ALU.add)
            ins.then_inc(rope_done, 1)
            dve.wait_ge(rope_done, b + 1)
        for g in range(4):
            dve.wait_ge(qk_turned, 7 + g + 1)
            dst = q2t[:, 4 * g + 2:4 * g + 4, :] if g < 2 else k2t[:, 2 * (g - 2) + 1, :].rearrange("p (a n) -> p a n", a=2)
            dve.tensor_copy(dst, tt((7 + g) % 2)[:, 2:4, :]).then_inc(qk_dve, 1)

        def scores2(b):
            half, q0 = b // 4, 4 * (b % 4)
            if b >= 2:
                dve.wait_ge(pt_turned, 32 + 4 * (b - 1))
            for i in range(4):
                n = 32 + 4 * b + i
                dve.wait_ge(s_ready, n + 1)
                dve.tensor_tensor(sm2[:, b % 2, i, :], G[:, n % 4, :], tab2[:, MASK2 + N * (i % 2):MASK2 + N * (i % 2) + N],
                                  ALU.add).then_inc(s_read, 1)
                dve.wait_ge(s_read, n + 1)
                dve.reduce_max(mx[:, half, q0 + i:q0 + i + 1], sm2[:, b % 2, i, :], AX_X).then_inc(s_max, 1)
            dve.wait_ge(s_max, 32 + 4 * b + 4)
            m = mx[:, half, q0:q0 + 4]
            link(dve.tensor_scalar(m, m, SCALE, None, ALU.mult))
            s = sink2[:, 2 * b:2 * b + 2].unsqueeze(2).broadcast_to([P, 2, 2])
            m3 = m.rearrange("p (h b) -> p h b", b=2)
            link(dve.tensor_tensor(m3, m3, s, ALU.max))
            dve.tensor_tensor(es[:, half, q0:q0 + 4].rearrange("p (h b) -> p h b", b=2), s, m3, ALU.subtract)
            dve.tensor_scalar(nm[:, half, q0:q0 + 4], m, -1.0, None, ALU.mult).then_inc(nm_ready, 1)

        def outputs2(half):
            dve.wait_ge(pt_used, 32 + 16 * half + 16)
            dve.wait_ge(es_ready, 2 + 4 * half + 4)
            r = rs[:, half, :]
            link(dve.tensor_tensor(r, r, es[:, half, :], ALU.add))
            link(dve.reciprocal(r, r))
            for k in range(NB):
                f = r.rearrange("p (h b) -> p h b", b=2)[:, :, k:k + 1].broadcast_to([P, 8, DH])
                ins = dve.tensor_tensor(o2[:, k, N * half:N * half + N].rearrange("p (h d) -> p h d", d=DH),
                                        T[:, 2 + k, :].rearrange("p (h d) -> p h d", d=DH), f, ALU.mult)
            ins.then_inc(o_evac, 1)

        scores2(0)
        for b in range(8):
            if b < 7:
                scores2(b + 1)
            if b % 4 == 3:
                outputs2(b // 4)
        for j in range(8):
            dve.wait_ge(mixed_mm, j + 1)
            tmp = (rot, rot)[0][:].rearrange("p h d -> p (h d)")[:, TOK * (j % 2):TOK * (j % 2) + TOK]
            link(dve.tensor_scalar(tmp, G[:, j % 4, 0:TOK], gains[:, POOL_S + j:POOL_S + j + 1], None, ALU.mult))
            dve.tensor_copy(h_hi[:, 8 + j, :], tmp).then_inc(mixed_hi, 1)
            dve.wait_ge(mixed_hi, j + 1)
            dve.tensor_tensor(h_lo[:, 8 + j, :], tmp, h_hi[:, 8 + j, :].bitcast(F32), ALU.subtract).then_inc(mixed_lo, 1)
        prep("out2", None, h_hi, h_lo)

        s0 = 2 * FIRST_LOAD["out2"]
        with dve.Fori(0, 4) as i:
            los(s0 + 3, 8, i * 8)
        dve.wait_ge(row_full, 48)
        residual(2, False, FIRST_EVAC["mlp2"])
        stats(7, [x[:, 0, :]], D)
        combine(NORM_M, 4)
        prep("up2", comb, h_hi, h_lo, adac[:, 3, :])
        dve.wait_ge(prep_turned, PREP["up2"][0] + 4)
        dve.memset(y[:], 0.0).then_inc(y_zero, 1)
        dve.wait_ge(y_zero, 2)

        def post2(u, c, du):
            def split():
                dve.wait_ge(up_read, u + 1 + du)
                dve.tensor_copy(a_hi[:, 4 * c:4 * c + 4, :], conv[:]).then_inc(a_first, 1)
                dve.wait_ge(a_first, u + 1 + du)
                dve.tensor_tensor(a_lo[:, 4 * c:4 * c + 4, :], conv[:], a_hi[:, 4 * c:4 * c + 4, :].bitcast(F32),
                                  ALU.subtract).then_inc(a_ready, 1)

            return lambda: None, split

        def group2(s, u, d, du):
            for c in range(4):
                body(s + 8 * c, d, post2(u + c - 1, c - 1, du) if c else None)
            for c in range(4):
                body(s + 32 + 8 * c, d, None if c else post2(u + 3, 3, du))
                down_evac(c, s + 32 + 8 * c + 8, d)

        s0, u0 = 2 * FIRST_LOAD["mlp2"], UP0["mlp2"]
        with dve.Fori(0, GROUPS2 - 1) as g:
            group2(s0, u0, g * 64, g * 4)
        group2(s0 + 64 * (GROUPS2 - 1), u0 + 4 * (GROUPS2 - 1), 0, 0)

        dve.wait_ge(row_full, 64)
        dve.wait_ge(bank_evac, FIRST_EVAC["mlp2"] + 64)
        residual(3, False, None)
        stats(8, [x[:, 0, :]], D)
        dve.wait_ge(final_in, 16)
        for b in range(NB):
            dve.scalar_tensor_tensor(out=y[:, b, :], in0=x[:, b, :], scalar=rstd[:, b:b + 1], in1=final_row[:],
                                     op0=ALU.mult, op1=ALU.mult).then_inc(out_ready, 1)

    @block.tensor
    def _(pe):
        def step(s, parity, acts, kt, first, last, ready=None, d=0, width=N, also=None):
            pe.wait_ge(hi_ready, s + 1 + d)
            pe.wait_ge(lo_ready, s + 1 + d)
            if ready is not None:
                pe.wait_ge(*ready)
            for j in range(STEPK):
                wh, wl = w_hi[:, s % 4, j, 0:width], w_lo[:, s % 4, j, 0:width]
                for n, (hi, lo) in enumerate(acts):
                    for b in range(NB):
                        out = G[:, 2 * (parity if n == 0 else 1) + b, 0:width]
                        ah, al = hi[:, kt + j, b * P:b * P + P], lo[:, kt + j, b * P:b * P + P]
                        f, l = first and j == 0, last and j == STEPK - 1
                        pe.matmul(out, ah, wh, start=f, stop=False)
                        pe.matmul(out, ah, wl, start=False, stop=False)
                        mm = pe.matmul(out, al, wh, start=False, stop=l)
            mm.then_inc(step_done, 1)

        def steps(s, k0, k1, parity, acts, ready, e=None, d=0, de=0, per=8, width=N):
            if k0 == 0 and e is not None and not (isinstance(e, int) and e <= 0):
                pe.wait_ge(bank_evac, e + de)
            for k in range(k0, k1):
                step(s + k, parity, acts, STEPK * k, k == 0, k == per - 1, ready(k), d, width)

        def prepped(name):
            n0 = PREP[name][0]
            return lambda k: (h_ready, n0 + k // 2 + 1)

        H, A = [(h_hi, h_lo)], [(a_hi, a_lo)]

        def turn_prep(name, src):
            n0, n = PREP[name]
            for g in range(n):
                if name in NORMED:
                    pe.wait_ge(xn_ready, NORMED[name] + g + 1)
                if n0 + g >= 2:
                    pe.wait_ge(prep_tmp, n0 + g - 1)
                for j in range(4):
                    for b in range(NB):
                        mm = pe.transpose(tt(g % 2)[:, j, b * P:b * P + P], src[:, b, (4 * g + j) * P:(4 * g + j + 1) * P],
                                          ident[:])
                mm.then_inc(prep_turned, 1)

        def ada_sum(q):
            pe.wait_ge(ada_used, 32 * q + 32)
            if q >= 1:
                pe.wait_ge(ada_col, q)
            for c in range(2 if ADA_ORDER[q][1] else 1):
                for t in range(KT):
                    mm = pe.matmul(T[:, 3, KT * c + t:KT * c + t + 1],
                                   ada_acc[:, c, t // 8, (t % 8) * P:(t % 8 + 1) * P], ones_col[:],
                                   start=True, stop=True)
            mm.then_inc(ada_summed, 1)

        pe.wait_ge(table_in, 16)
        pe.wait_ge(vec_in, 16 * 14)
        pe.transpose(T[:, 0, 0:120], stage[0:120, 0, :], ident[0:120, 0:120])
        for k in range(4):
            pe.transpose(T[:, 1, k * CTS:(k + 1) * CTS], stage[0:CTS, 1 + k, :], ident[0:CTS, 0:CTS])
        pe.transpose(T[:, 2, 0:96], stage[0:96, 5, :], ident[0:96, 0:96]).then_inc(vec_turned, 1)
        pe.wait_ge(cols_ready, 1)
        turn_prep("in1", x)

        s0, r = 2 * FIRST_LOAD["in1"], prepped("in1")
        steps(s0, 0, 8, 0, H, r)
        steps(s0 + 8, 0, 8, 1, H, r)
        with pe.Fori(0, 3) as i:
            for c in range(2):
                steps(s0 + 16 + 8 * c, 0, 8, c, H, r, 2 * (c + 1), i * 16, i * 4)
        steps(s0 + 64, 0, 8, 0, H, r, 14, width=W_IN1 - 8 * N)
        ada_sum(0)

        pe.wait_ge(ada_col, 1)
        pe.wait_ge(tab1_in, 16)
        pe.wait_ge(lf_ready, 1)
        tri, one = tab1[:, TRI:TRI + P], tab1[:, ONE:ONE + P]
        pe.matmul(G[:, 0, 0:HEADS], tri, lf[:, 0, :], start=True, stop=True)
        pe.matmul(G[:, 0, HEADS:2 * HEADS], one, lf[:, 0, :], start=True, stop=False)
        pe.matmul(G[:, 0, HEADS:2 * HEADS], tri, lf[:, 1, :], start=False, stop=True)
        pe.matmul(G[0:HEADS, 1, 0:TOK], lf[:, 0, :], tab1[:, TRI:TRI + TOK], start=True, stop=False)
        pe.matmul(G[0:HEADS, 1, P:TOK], lf[:, 1, :], tri, start=False, stop=True).then_inc(c_done, 1)

        pe.wait_ge(dup_ready, 1)
        QK = ([QA + P * t for t in range(8)] + [-1, -2] + [QB + P * t for t in range(8)]
              + [KB + P * t for t in range(8)])

        for g in range(7):
            if g >= 2:
                pe.wait_ge(qk_act, g - 1)
                pe.wait_ge(qk_dve, g - 1)
            for j, col in enumerate(QK[4 * g:4 * g + 4]):
                for b in range(NB):
                    src = p1[:, b, col:col + P] if col >= 0 else dup1[:, b, -1 - col].rearrange("p a d -> p (a d)")
                    mm = pe.transpose(tt(g % 2)[:, j, b * P:b * P + P], src, ident[:])
            mm.then_inc(qk_turned, 1)
        pe.wait_ge(qk_act, 7)
        pe.wait_ge(qk_dve, 6)
        pe.wait_ge(c_ready, 1)

        def scores(b):
            for i in range(8):
                n = 8 * b + i
                h = n % HEADS
                q, k = (h // 2, 8 + h // 8) if b < 2 else (10 + h // 2, 18 + h // 2)
                rows = slice(DH * (h % 2), DH * (h % 2) + DH)
                if n >= 4:
                    pe.wait_ge(s_read, n - 3)
                fox = b >= 2
                for blk, (c0, w) in enumerate(((0, P), (P, 2 * P))):
                    out = G[:, n % 4, c0:c0 + w]
                    mm = pe.matmul(out, qk1[rows, q, P * blk:P * blk + P], qk1[rows, k, 0:w], start=True, stop=not fox)
                    if fox:
                        mm = pe.matmul(out, ident[:, h:h + 1].broadcast_to([P, P]), cT[:, 0:w],
                                       start=False, stop=True)
                mm.then_inc(s_ready, 1)

        def turn_p(n, src, width):
            pe.wait_ge(p_ready, n + 1)
            if n >= 2:
                pe.wait_ge(pt_ready, n - 1)
            for j in range(width // P):
                mm = pe.transpose(T[:, n % 2, P * j:P * j + P], src[:, P * j:P * j + P], ident[:])
            mm.then_inc(pt_turned, 1)

        def pv1(n):
            pe.wait_ge(pt_ready, n + 1)
            i, h = n % 8, n % HEADS
            if i == 0 and n >= 8:
                pe.wait_ge(o_evac, n // 8)
            v = VA + DH * (h // 8) if n < HEADS else VB + DH * h
            pe.matmul(T[:, 2, DH * i:DH * i + DH], pt1[:, n % 4, 0:P], p1[:, 0, v:v + DH], start=True, stop=True)
            pe.matmul(T[:, 3, DH * i:DH * i + DH], pt1[:, n % 4, P:2 * P], p1[:, 0, v:v + DH], start=True, stop=False)
            pe.matmul(T[:, 3, DH * i:DH * i + DH], pt1[:, n % 4, 2 * P:3 * P], p1[:, 1, v:v + DH],
                      start=False, stop=True).then_inc(pt_used, 1)

        scores(0)
        for b in range(4):
            if b < 3:
                scores(b + 1)
            for i in range(8):
                turn_p(8 * b + i, sm1[b % 2][:, i, :], 3 * P)
                if i >= 1:
                    pv1(8 * b + i - 1)
            pv1(8 * b + 7)
        pe.wait_ge(o_evac, 4)
        turn_prep("out1", o1)

        s0, e0, r = 2 * FIRST_LOAD["out1"], FIRST_EVAC["out1"], prepped("out1")
        with pe.Fori(0, 2) as i:
            for c in range(2):
                steps(s0 + 8 * c, 0, 8, c, H, r, e0 + 2 * (c - 1), i * 16, i * 4)
        ada_sum(1)
        pe.wait_ge(ada_col, 2)
        turn_prep("up1", y)

        def turn_up(u, e, d=0, du=0, de=0):
            pe.wait_ge(bank_evac, e + de)
            if u >= 1:
                pe.wait_ge(up_read, u + du)
            for j in range(CK):
                for b in range(NB):
                    mm = pe.transpose(tt(0)[:, j, b * P:b * P + P], u_buf[:, b, P * j:P * j + P], ident[:])
            mm.then_inc(turned, 1)

        for g, n, fin_up, fin_down in (("a", 8, None, 2), ("b", 8, 3, 4), ("c", 6, 5, None)):
            s0, e0, u0, r = 2 * FIRST_LOAD["up1" + g], FIRST_EVAC["up1" + g], UP0["up1" + g], prepped("up1")
            sd, ed = 2 * FIRST_LOAD["down1" + g], FIRST_EVAC["down1" + g]
            per = 8 if n == 8 else 6

            def ready(k, u0=u0):
                return a_ready, u0 + k + 1

            def up_pair(s, e, u, d, de, du, tail=False, finish=None):
                for c in range(2):
                    steps(s + 8 * c, 2, 8, c, H, r, d=d)
                    if tail and c == 1:
                        steps(sd, 0, 2, 0, A, ready, ed - 2, per=per)
                    else:
                        steps(s + 8 * c + 8, 0, 2, 1 - c, H, r, e + 2 * c, d, de)
                    turn_up(u + c, e + 2 * c + 2, d, du, de)
                    if c == 0 and finish is not None:
                        ada_sum(finish)

            steps(s0, 0, 2, 0, H, r, e0 - 2 if g != "a" else e0)
            up_pair(s0, e0, u0, 0, 0, 0, finish=fin_up)
            with pe.Fori(0, n // 2 - 2) as i:
                up_pair(s0 + 16, e0 + 4, u0 + 2, i * 16, i * 4, i * 2)
            up_pair(s0 + 8 * n - 16, e0 + 2 * n - 4, u0 + n - 2, 0, 0, 0, tail=True)
            for c in range(4):
                steps(sd + per * c, 2 if c == 0 else 0, per, c % 2, A, ready, ed + 2 * (c - 1), per=per)
                if c == 0 and fin_down is not None:
                    ada_sum(fin_down)
        pe.wait_ge(ada_col, 6)
        for n, part in enumerate((2, 5)):
            mm = pe.transpose(T[0:KT, 3, P * n:P * n + P], adac[:, part, :], ident[:])
        mm.then_inc(g_turned, 1)
        pe.wait_ge(g_copied, 1)
        turn_prep("in2", y)

        s0, e0, r = 2 * FIRST_LOAD["in2"], FIRST_EVAC["in2"], prepped("in2")
        for k in range(4):
            steps(s0 + 8 * k, 0, 8, k % 2, H, r, e0 + 2 * (k - 1))
            if k == 1:
                turn_prep("ctx", y)
        pe.wait_ge(bank_evac, e0 + 8)
        for k in range(8):
            step(s0 + 32 + k, 0, H + A, STEPK * k, k == 0, k == 7, (h_ready, PREP["ctx"][0] + k // 2 + 1))
        pe.wait_ge(bank_evac, FIRST_EVAC["out2"])

        pe.wait_ge(rope_done, 2)
        pe.wait_ge(dup_ready, 2)
        for g in range(4):
            pe.wait_ge(qk_act, 7 + g - 1)
            pe.wait_ge(qk_dve, 6 + g - 1)
            for j in range(4):
                for b in range(NB):
                    out = tt((7 + g) % 2)[:, j, b * P:b * P + P]
                    if g < 2:
                        src = p2[:, b, Q2 + P * (4 * g + j):Q2 + P * (4 * g + j + 1)]
                    else:
                        kv = 2 * (g - 2) + j // 2
                        src = dup2[:, NB * (j % 2) + b, kv].rearrange("p a d -> p (a d)")
                    mm = pe.transpose(out, src, ident[:])
            mm.then_inc(qk_turned, 1)
        pe.wait_ge(qk_act, 11)
        pe.wait_ge(qk_dve, 10)

        def scores2(b):
            for i in range(4):
                n = 32 + 4 * b + i
                h, blk = 2 * b + i // 2, i % 2
                rows = slice(DH * (h % 2), DH * (h % 2) + DH)
                pe.wait_ge(s_read, n - 3)
                pe.matmul(G[:, n % 4, :], q2t[rows, h // 2, P * blk:P * blk + P], k2t[rows, h // 4, :],
                          start=True, stop=True).then_inc(s_ready, 1)

        def pv2(n):
            pe.wait_ge(pt_ready, n + 1)
            m = n - 32
            h, blk = m // 2, m % 2
            if m == 16:
                pe.wait_ge(o_evac, 5)
            out = T[:, 2 + blk, DH * (h % 8):DH * (h % 8) + DH]
            kv = DH * (h // 4)
            for j in range(4):
                v = p2[:, j, V2 + kv:V2 + kv + DH] if j < 2 else c2[:, j - 2, 256 + kv:256 + kv + DH]
                mm = pe.matmul(out, pt2[:, n % 4, P * j:P * j + P], v, start=j == 0, stop=j == 3)
            mm.then_inc(pt_used, 1)

        scores2(0)
        for b in range(8):
            if b < 7:
                scores2(b + 1)
            for i in range(4):
                n = 32 + 4 * b + i
                turn_p(n, sm2[:, b % 2, i, :], N)
                if i >= 1:
                    pv2(n - 1)
            pv2(32 + 4 * b + 3)

        pe.wait_ge(pool_in, 32)
        pe.wait_ge(s_read, 64)
        for g in range(4):
            for c in range(2):
                for b in range(NB):
                    mm = pe.matmul(G[:, g, TOK * c:TOK * c + TOK], p2[:, b, U2 + PG * g + P * c:U2 + PG * g + P * c + P],
                                   pool_a[:, b, g, :], start=b == 0, stop=b == NB - 1)
            mm.then_inc(pooled_mm, 1)
        pe.wait_ge(pooled_ev, 4)
        for j in range(8):
            g, dt = j // 2, j % 2
            if j >= 4:
                pe.wait_ge(mixed_lo, j - 3)
            for c in range(2):
                mm = pe.matmul(G[:, j % 4, 0:TOK], pool_w[:, g, c, P * dt:P * dt + P], pooled[:, 2 * g + c, :],
                               start=c == 0, stop=c == 1)
            mm.then_inc(mixed_mm, 1)
        pe.wait_ge(o_evac, 6)
        pe.wait_ge(mixed_lo, 8)
        turn_prep("out2", o2)

        s0, e0, n0 = 2 * FIRST_LOAD["out2"], FIRST_EVAC["out2"], PREP["out2"][0]

        def r(k):
            return h_ready, n0 + min(k // 2, 1) + 1

        with pe.Fori(0, 2) as i:
            for c in range(2):
                steps(s0 + 8 * c, 0, 8, c, H, r, e0 + 2 * (c - 1), i * 16, i * 4)
        turn_prep("up2", y)

        s0, e0, u0, r = 2 * FIRST_LOAD["mlp2"], FIRST_EVAC["mlp2"], UP0["mlp2"], prepped("up2")
        with pe.Fori(0, GROUPS2) as g:
            d, de, du = g * 64, g * 16, g * 4

            def ready(k):
                return a_ready, u0 + k // 2 + 1 + du

            steps(s0, 0, 2, 0, H, r, e0 - 2, d, de)
            for c in range(4):
                steps(s0 + 8 * c, 2, 8, c % 2, H, r, d=d)
                if c < 3:
                    steps(s0 + 8 * c + 8, 0, 2, (c + 1) % 2, H, r, e0 + 2 * c, d, de)
                else:
                    steps(s0 + 32, 0, 2, 0, A, ready, e0 + 6, d, de)
                turn_up(u0 + c, e0 + 2 * c + 2, d, du, de)
            for c in range(4):
                steps(s0 + 32 + 8 * c, 2 if c == 0 else 0, 8, c % 2, A, ready, e0 + 8 + 2 * (c - 1), d, de)

    ctx.close()


NAMES = ["x", "pre_mix_g", "w_in", "b_forget", "sinks", "grp_swa_g", "grp_fox_g", "w_out", "post_mix_g", "pre_ffn_g",
         "w_up", "conv_w", "conv_b", "w_down", "post_ffn_g", "c_2", "ctx_2", "c_ctx_2", "norm_attn_w_2", "norm_mlp_w_2",
         "w_ada_2", "b_ada_2", "w_in_2", "attn_sink_2", "pool_w_2", "pool_scale_2", "w_out_2", "w_mlp_up_2",
         "w_mlp_down_2", "final_norm_w_2"]


def kernel(**inputs):
    import concourse.bacc as bacc
    from concourse.bass_utils import run_bass_kernel_spmd

    nc = bacc.Bacc("TRN2", target_bir_lowering=False, num_devices=1)
    table, pool_table = constants()
    arrays, aps = {}, {}
    for name, value in [(n, inputs[n]) for n in NAMES] + [("table", table), ("pool_table", pool_table)]:
        value = np.ascontiguousarray(value)
        arrays["in_" + name] = value
        aps[name] = nc.dram_tensor("in_" + name, value.shape, mybir.dt.from_np(value.dtype), kind="ExternalInput").ap()
    aps["out"] = nc.dram_tensor("out", (1, TOK, D), F32, kind="ExternalOutput").ap()
    build(nc, aps)
    result = run_bass_kernel_spmd(nc, [arrays], core_ids=[0])
    return result.results[0]["out"]
```

```python
from contextlib import ExitStack

import numpy as np

import concourse.bass as bass
from concourse import mybir

F32 = mybir.dt.float32
F32R = mybir.dt.float32r
ALU = mybir.AluOpType
ACT = mybir.ActivationFunctionType
AX_X = mybir.AxisListType.X

P = 128
TOK = 256
NB = TOK // P
D = 2048
KT = D // P
DH = 64
SCALE = DH ** -0.5
EPS = 1e-6
N = 512
CK = N // P
LOADK = 4
STEPK = 2

HEADS = 16
W_IN1 = 4368
QA, KA, VA, QB, KB, VB, FB = 0, 1024, 1152, 1280, 2304, 3328, 4352
FF1 = 5632
GV = N // 2
CT1 = FF1 // P
CTS = 2 * CT1
UPS1 = (8, 8, 6)
W_IN2 = 2560
Q2, K2, V2, U2 = 0, 1024, 1280, 1536
KV2 = 4
FF2 = 8192
GROUPS2 = 4
WINDOWS = (2, 4, 8, 16)
PG = 256
ADA_HALF = 1024
ADA_ORDER = ((0, (0, 1)), (5, (0,)), (2, (0,)), (3, (0,)), (1, (1, 2)), (4, (0,)))
ADA_RUNS = ((0, 0, 32), (1, 0, 32), (2, 0, 32), (4, 0, 16), (3, 0, 32), (4, 16, 16), (5, 0, 32))
ADA_BASE = [sum(r[2] for r in ADA_RUNS[:n]) for n in range(len(ADA_RUNS))]
ADA_END = [max(b + r[2] for b, r in zip(ADA_BASE, ADA_RUNS) if r[0] == q) for q in range(len(ADA_ORDER))]
NEG = -1e30

C_ID, C_TRI, C_ONE, C_ALI, C_CAU, C_MASK, C_COS, C_SIN, C_END = 0, 128, 256, 384, 768, 1152, 2176, 2304, 2432

PHASES = [("in1", 9, 4), ("out1", 4, 4), ("up1a", 8, 4), ("down1a", 4, 4), ("up1b", 8, 4), ("down1b", 4, 4),
          ("up1c", 6, 4), ("down1c", 4, 3), ("in2", 5, 4), ("out2", 4, 4), ("mlp2", 32, 4)]
FIRST_LOAD, FIRST_EVAC = {}, {}
_l = _e = 0
for _name, _n, _per in PHASES:
    FIRST_LOAD[_name], FIRST_EVAC[_name] = _l, _e
    _l += _n * _per
    _e += 2 * _n + (2 if _name == "in2" else 0)
LOADS = _l
STEPS = 2 * LOADS
UP0 = {"up1a": 0, "up1b": 8, "up1c": 16, "mlp2": 22}


def constants():
    t = np.zeros((P, C_END), np.float32)
    p = np.arange(P)[:, None]
    c = np.arange(TOK)[None, :]
    t[:, C_ID:C_ID + P] = p == c[:, :P]
    t[:, C_TRI:C_TRI + P] = p <= c[:, :P]
    t[:, C_ONE:C_ONE + P] = 1.0
    t[:, C_ALI:C_ALI + P] = np.where(c[:, :P] <= p, c[:, :P] - p, NEG)
    far = P + p - c
    t[:, C_ALI + P:C_ALI + 3 * P] = np.where((far >= 0) & (far < P), -far, NEG)
    t[:, C_CAU:C_CAU + P] = np.where(c[:, :P] <= p, 0.0, NEG)
    t[:, C_CAU + P:C_CAU + 3 * P] = np.where(far >= 0, 0.0, NEG)
    freq = (10000.0 ** (-np.arange(0, 32, 2, dtype=np.float32) / np.float32(32))).astype(np.float32)
    for b in range(NB):
        q = b * P + p
        t[:, C_MASK + b * N:C_MASK + b * N + TOK] = np.where(np.abs(q - c) <= 128, 0.0, NEG)
        for rc, pos in enumerate((q // 64, q % 64)):
            ang = (pos.astype(np.float32) * freq[None, :]).astype(np.float32)
            for half in range(2):
                at = b * DH + rc * 32 + half * 16
                t[:, C_COS + at:C_COS + at + 16] = np.cos(ang)
                t[:, C_SIN + at:C_SIN + at + 16] = np.sin(ang) * (-1.0 if half == 0 else 1.0)
    pool = np.zeros((TOK, len(WINDOWS), TOK), np.float32)
    s, q = np.arange(TOK)[:, None], np.arange(TOK)[None, :]
    for g, w in enumerate(WINDOWS):
        lo, hi = np.clip(q - w // 2, 0, TOK), np.clip(q - w // 2 + w, 0, TOK)
        pool[:, g, :] = ((s >= lo) & (s < hi)) / (hi - lo).astype(np.float32) - (s == q)
    return t, np.ascontiguousarray(pool.reshape(NB, P, len(WINDOWS) * TOK).transpose(1, 0, 2))


def build(nc, a):
    ctx = ExitStack()
    base = (nc.sbuf_base + 63) // 64 * 64
    top = [base]
    at = {}

    def region(name, size):
        at[name] = top[0]
        top[0] += size

    KB_ = 1024
    region("raw", 32 * KB_)
    region("whi", 16 * KB_)
    region("wlo", 16 * KB_)
    region("h", 32 * KB_)
    region("act", 32 * KB_)
    region("y", 16 * KB_)
    region("x", 16 * KB_)
    region("ada", 24 * KB_)
    region("tmp", 18 * KB_)
    region("small", nc.sbuf_usable_end - top[0])
    small_at = [at["small"]]

    def place(name, shape, where, off=0, dt=F32):
        return nc.alloc_sbuf_tensor_at(name, shape, dt, offset=at[where] + off)

    def small(name, shape):
        t = nc.alloc_sbuf_tensor_at(name, shape, F32, offset=small_at[0])
        size = 4
        for n in shape[1:]:
            size *= n
        small_at[0] += (size + 31) // 32 * 32
        assert small_at[0] <= nc.sbuf_usable_end
        return t

    raw = place("raw", [P, 4, LOADK, N], "raw")
    w_hi = place("w_hi", [P, 4, STEPK, N], "whi", dt=F32R)
    w_lo = place("w_lo", [P, 4, STEPK, N], "wlo", dt=F32R)
    h_hi = place("h_hi", [P, KT, TOK], "h", dt=F32R)
    h_lo = place("h_lo", [P, KT, TOK], "h", 16 * KB_, F32R)
    a_hi = place("a_hi", [P, KT, TOK], "act", dt=F32R)
    a_lo = place("a_lo", [P, KT, TOK], "act", 16 * KB_, F32R)
    y = place("y", [P, NB, D], "y")
    x = place("x", [P, NB, D], "x")
    o1 = place("o1", [P, NB, D], "x")
    ada_w = place("ada_w", [P, 2, ADA_HALF], "ada")
    ada_acc = place("ada_acc", [P, 2, 2, ADA_HALF], "ada", 8 * KB_)
    ada_third = place("ada_third", [P, 2, ADA_HALF], "tmp", 10 * KB_)
    u_buf = place("u_buf", [P, NB, N], "tmp")
    conv = place("conv", [P, CK, TOK], "tmp", 4 * KB_)
    prod = place("prod", [P, 2, TOK], "tmp", 8 * KB_)
    row = place("row", [P, D], "tmp", 10 * KB_)
    p1 = place("p1", [P, NB, W_IN1], "act")
    sm1 = [place("sm1a", [P, 8, 3 * P], "y", 16 * KB_ - 12 * KB_), place("sm1b", [P, 8, 3 * P], "tmp")]
    pt1 = place("pt1", [P, 2, 3 * P], "tmp", 12 * KB_)
    junk1 = place("junk1", [P, N], "tmp", 15 * KB_)
    assert 2 * W_IN1 * 4 <= (32 + 4) * KB_
    qk1 = place("qk1", [P, 26, TOK], "h")
    tab1 = place("tab1", [P, C_MASK - C_TRI], "h", 26 * KB_)
    cT = place("cT", [P, TOK], "h", 30 * KB_)
    TRI, ONE, ALI, CAU = 0, C_ONE - C_TRI, C_ALI - C_TRI, C_CAU - C_TRI
    p2 = place("p2", [P, NB, W_IN2], "ada")
    c2 = place("c2", [P, NB, N], "ada", 20 * KB_)
    q2t = place("q2t", [P, 8, TOK], "act")
    k2t = place("k2t", [P, KV2, 2 * TOK], "act", 8 * KB_)
    sm2 = place("sm2", [P, 2, 4, N], "act", 16 * KB_)
    o2 = place("o2", [P, NB, 1024], "y")
    pooled = place("pooled", [P, 8, TOK], "y", 8 * KB_)
    pool_a = place("pool_a", [P, NB, 4, TOK], "h")
    pool_w = place("pool_w", [P, 4, 2, PG], "h", 16 * KB_)
    pt2 = place("pt2", [P, 4, N], "tmp")
    tab2 = place("tab2", [P, C_END - C_MASK], "tmp", 8 * KB_)
    rot = place("rot", [P, 20, DH], "tmp", 13 * KB_)
    MASK2, COS2, SIN2 = 0, C_COS - C_MASK, C_SIN - C_MASK
    dup1 = place("dup1", [P, NB, 2, 2, DH], "tmp", 12 * KB_)
    dup2 = place("dup2", [P, 2 * NB, KV2, 2, DH], "tmp")
    final_row = place("final_row", [P, D], "ada")
    junk = place("junk", [P, N], "tmp", 8 * KB_)
    stage = place("stage", [P, 6, P], "y", 4 * KB_)

    ident = small("ident", [P, P])
    gains = small("gains", [P, 120])
    convw = small("convw", [P, 4, CTS // 1])
    bada = small("bada", [P, 96])
    adac = small("adac", [P, 8, KT])
    silu = small("silu", [P, 2, KT])
    comb = small("comb", [P, KT])
    ones_col = small("ones_col", [P, 1])
    ones_again = small("ones_again", [P, 1])
    ssq = small("ssq", [P, 8])
    rstd = small("rstd", [P, 4])
    rstdx = small("rstdx", [P, NB])
    sq = small("sq", [P, NB, 4])
    mx = small("mx", [P, 2, 16])
    nm = small("nm", [P, 2, 16])
    rs = small("rs", [P, 2, 16])
    es = small("es", [P, 2, 16])
    sink1 = small("sink1", [P, HEADS])
    sink2 = small("sink2", [P, HEADS])
    bforget = small("bforget", [P, HEADS])
    z = small("z", [P, NB, HEADS])
    lf = small("lf", [P, NB, HEADS])
    ct8 = small("ct8", [P, NB, HEADS])
    grow = small("grow", [16, 2, P])

    G = ctx.enter_context(nc.psum_tensor("G", [P, 4, N], F32))
    T = ctx.enter_context(nc.psum_tensor("T", [P, 4, N], F32))

    def sem(name):
        return ctx.enter_context(nc.semaphore(name))

    x_in = [sem(f"x_in{g}") for g in range(4)]
    table_in, vec_in, vec2_in, misc_in = sem("table_in"), sem("vec_in"), sem("vec2_in"), sem("misc_in")
    raw_full = [sem(f"raw_full{i}") for i in range(4)]
    hi_ready, lo_ready, step_done = sem("hi_ready"), sem("lo_ready"), sem("step_done")
    bank_evac = sem("bank_evac")
    turned, up_read = sem("turned"), sem("up_read")
    base_ready, tap1, gelu_done, conv_used, a_first, a_ready = (
        sem("base_ready"), sem("tap1"), sem("gelu_done"), sem("conv_used"), sem("a_first"), sem("a_ready"))
    vec_turned, vec2_turned, cols_ready, cols2_ready, silu_e, silu_ready = sem("vec_turned"), sem("vec2_turned"), sem("cols_ready"), sem("cols2_ready"), sem("silu_e"), sem("silu_ready")
    ada_full = [sem("ada_full0"), sem("ada_full1")]
    ada_used, ada_summed, ada_col, ada_zero = sem("ada_used"), sem("ada_summed"), sem("ada_col"), sem("ada_zero")
    squared, mean_ready, root_ready, rstd_ready = sem("squared"), sem("mean_ready"), sem("root_ready"), sem("rstd_ready")
    xn_act, xn_dve, prep_turned, tmp_act, tmp_dve, prep_hi, h_ready = (
        sem("xn_act"), sem("xn_dve"), sem("prep_turned"), sem("tmp_act"), sem("tmp_dve"), sem("prep_hi"), sem("h_ready"))
    x_new = sem("x_new")
    comb_ready = sem("comb_ready")
    vchain, achain = sem("vchain"), sem("achain")
    row_full, x_again, ctx_in, tab1_in, tab2_in, pool_in, final_in = (
        sem("row_full"), sem("x_again"), sem("ctx_in"), sem("tab1_in"), sem("tab2_in"), sem("pool_in"), sem("final_in"))
    y_zero, s_max = sem("y_zero"), sem("s_max")
    z_ready, e_ready, e1_ready, l_ready, lf_ready, c_done, c_ready = (
        sem("z_ready"), sem("e_ready"), sem("e1_ready"), sem("l_ready"), sem("lf_ready"), sem("c_done"), sem("c_ready"))
    qk_turned, qk_act, qk_dve = sem("qk_turned"), sem("qk_act"), sem("qk_dve")
    s_ready, s_read, nm_ready, es_ready, p_ready, pt_turned, pt_ready, pt_used, o_evac = (
        sem("s_ready"), sem("s_read"), sem("nm_ready"), sem("es_ready"), sem("p_ready"), sem("pt_turned"),
        sem("pt_ready"), sem("pt_used"), sem("o_evac"))
    dup_ready, rope_done, pooled_mm, pooled_ev, mixed_mm, mixed_hi, mixed_lo = (
        sem("dup_ready"), sem("rope_done"), sem("pooled_mm"), sem("pooled_ev"), sem("mixed_mm"), sem("mixed_hi"), sem("mixed_lo"))
    g_turned, g_copied, g_stored = sem("g_turned"), sem("g_copied"), sem("g_stored")
    out_ready, out_stored = sem("out_ready"), sem("out_stored")

    ada_rows = nc.dram_tensor("ada_rows", (2, D), F32, kind="Internal").ap()

    def tiles(w):
        return w.rearrange("(t p) n -> p t n", p=P)

    w_in1, w_out1, w_down1 = tiles(a["w_in"][0]), tiles(a["w_out"][0]), tiles(a["w_down"][0])
    w_up1 = a["w_up"][0].rearrange("(t p) (two f) -> p t two f", p=P, two=2)
    w_in2, w_out2 = tiles(a["w_in_2"][0]), tiles(a["w_out_2"][0])
    w_up2, w_down2 = tiles(a["w_mlp_up_2"][0]), tiles(a["w_mlp_down_2"][0])
    w_ada = tiles(a["w_ada_2"][0])

    def tokens(t):
        return t[0].rearrange("(b p) n -> p b n", p=P)

    C_C, C_CTX, PRE_MIX, GRP, PRE_FFN, NORM_A, NORM_M, POOL_S = [16 * i for i in range(8)]
    PREP = {"in1": (0, 4), "out1": (4, 4), "up1": (8, 4), "in2": (12, 4), "ctx": (16, 4), "out2": (20, 2), "up2": (22, 4)}
    NORMED = {"out1": 0, "in2": 4, "ctx": 8, "up2": 12}
    X_NEW = {"up1": 0, "in2": 4, "out2": 8, "final": 12}
    STAT = {"in1": 0, "out1": 1, "y1": 2, "up1": 3, "y2": 4, "in2": 5, "ctx": 6, "up2": 7, "final": 8}
    SQUARED = {"in1": 8, "out1": 16, "y1": 24, "up1": 32, "y2": 40, "in2": 48, "ctx": 56, "up2": 64, "final": 72}

    def pipeline(n, pre, gain, fin):
        for t in range(n + 2):
            if t < n and pre:
                pre(t)
            if 1 <= t <= n:
                gain(t - 1)
            if t >= 2:
                fin(t - 2)

    def accs(q):
        return [ada_third[:] if i == 2 else ada_acc[:, i] for i in ADA_ORDER[q][1]]

    def tt(pair):
        return T[:, 2 * pair:2 * pair + 2, :].rearrange("p a (j n) -> p (a j) n", n=TOK)

    block = ctx.enter_context(nc.Block())

    @block.sync
    def _(sp):
        for g in range(4):
            sp.dma_start(x[:, :, g * N:g * N + N], tokens(a["x"])[:, :, g * N:g * N + N]).then_inc(x_in[g], 16)

        def load(l, src, d=0):
            if l >= 4:
                sp.wait_ge(lo_ready, 2 * l - 6 + 2 * d)
            for k in range(2):
                if len(src.shape) == 4:
                    dst, part = raw[:, l % 4, :, GV * k:GV * k + GV], src[:, :, k, :]
                else:
                    rows = slice(STEPK * k, STEPK * k + STEPK)
                    dst, part = raw[:, l % 4, rows, 0:src.shape[2]], src[:, rows, :]
                sp.dma_start(dst, part).then_inc(raw_full[l % 4], 16)

        def chunk(l, w, col, d=0, width=N, t0=0, loads=4):
            for k in range(loads):
                load(l + k, w[:, bass.ds(t0 + LOADK * k, LOADK), bass.ds(col, width)], d)

        def up_chunk(l, c, d=0):
            for k in range(4):
                load(l + k, w_up1[:, LOADK * k:LOADK * k + LOADK, :, bass.ds(c * GV, GV)], d)

        l0 = FIRST_LOAD["in1"]
        chunk(l0, w_in1, 0)
        with sp.Fori(0, 7) as i:
            chunk(l0 + 4, w_in1, i * N + N, i * 4)
        chunk(l0 + 32, w_in1, 8 * N, width=W_IN1 - 8 * N)
        l0 = FIRST_LOAD["out1"]
        with sp.Fori(0, 4) as i:
            chunk(l0, w_out1, i * N, i * 4)
        c0 = 0
        for g, n in zip("abc", UPS1):
            l0 = FIRST_LOAD["up1" + g]
            with sp.Fori(0, n) as i:
                up_chunk(l0, i + c0, i * 4)
            l0 = FIRST_LOAD["down1" + g]
            if n == 8:
                with sp.Fori(0, 4) as i:
                    chunk(l0, w_down1, i * N, i * 4, t0=2 * c0)
            else:
                for c in range(4):
                    chunk(l0 + 3 * c, w_down1, c * N, t0=2 * c0, loads=3)
            c0 += n
        l0 = FIRST_LOAD["in2"]
        for k, col in enumerate((0, N, U2, U2 + N, K2)):
            chunk(l0 + 4 * k, w_in2, col)
        l0 = FIRST_LOAD["out2"]
        with sp.Fori(0, 4) as i:
            chunk(l0, w_out2, i * N, i * 4)
        l0 = FIRST_LOAD["mlp2"]
        with sp.Fori(0, GROUPS2) as g:
            for c in range(4):
                chunk(l0 + 4 * c, w_up2, g * (4 * N) + c * N, g * 32)
            for c in range(4):
                for k in range(4):
                    load(l0 + 16 + 4 * c + k,
                         w_down2[:, bass.ds(g * KT + LOADK * k, LOADK), c * N:c * N + N], g * 32)
        for g in range(4):
            sp.wait_ge(out_ready, g + 1)
            sp.dma_start(tokens(a["out"])[:, :, g * N:g * N + N], y[:, :, g * N:g * N + N]).then_inc(out_stored, 16)
        sp.wait_ge(out_stored, 16 * 4)

    @block.gpsimd
    def _(pool):
        for k in range(3):
            pool.dma_start(stage[0:CTS, 1 + k, :], a["conv_w"][0, k].rearrange("(t p) -> t p", p=P)).then_inc(vec2_in, 16)
        pool.dma_start(stage[0:CTS, 4, :], a["conv_b"][0].rearrange("(t p) -> t p", p=P)).then_inc(vec2_in, 16)
        pool.dma_start(stage[0:96, 5, :], a["b_ada_2"][0].rearrange("(t p) -> t p", p=P)).then_inc(vec2_in, 16)

        def ada(run):
            q, first, count = ADA_RUNS[run]
            part, n = ADA_ORDER[q][0], ADA_BASE[run]

            def tile(t, half, wait):
                if wait is not None:
                    pool.wait_ge(ada_used, wait)
                pool.dma_start(ada_w[:, half, :],
                               w_ada[:, bass.ds(t + first // 2, 1), part * D + half * ADA_HALF:part * D + (half + 1) * ADA_HALF]
                               .rearrange("p a n -> p (a n)")).then_inc(ada_full[half], 16)

            if run == 0:
                tile(0, 0, None)
                tile(0, 1, None)
                with pool.Fori(1, count // 2) as t:
                    tile(t, 0, t * 2 - 1)
                    tile(t, 1, t * 2)
            else:
                with pool.Fori(0, count // 2) as t:
                    tile(t, 0, t * 2 + (n - 1))
                    tile(t, 1, t * 2 + n)

        def load_row(src):
            pool.dma_start(row[:], src.broadcast_to([P, D])).then_inc(row_full, 16)

        ada(0)
        pool.wait_ge(bank_evac, FIRST_EVAC["out1"])
        pool.dma_start(tab1[:], a["table"][:, C_TRI:C_MASK]).then_inc(tab1_in, 16)

        def twice(dst, src, n):
            return pool.tensor_copy(dst, src.rearrange("p (g d) -> p g d", d=DH).unsqueeze(2).broadcast_to([P, n, 2, DH]))

        for b in range(NB):
            ins = twice(dup1[:, b], p1[:, b, KA:KA + 2 * DH], 2)
        ins.then_inc(dup_ready, 1)
        pool.wait_ge(o_evac, 4)
        pool.wait_ge(squared, SQUARED["out1"])
        load_row(a["post_mix_g"])
        ada(1)
        pool.wait_ge(prep_turned, PREP["out1"][0] + 4)
        pool.dma_start(x[:], tokens(a["x"])).then_inc(x_again, 16)
        for run in range(2, 6):
            ada(run)
        ada(6)
        pool.wait_ge(ada_col, 5)
        load_row(a["post_ffn_g"])
        pool.wait_ge(g_copied, 1)
        pool.dma_start(ada_rows.rearrange("r (t p) -> t r p", p=P), grow[:]).then_inc(g_stored, 16)
        pool.wait_ge(h_ready, PREP["in2"][0] + 4)
        pool.dma_start(y[:], tokens(a["ctx_2"])).then_inc(ctx_in, 16)
        pool.wait_ge(h_ready, PREP["ctx"][0] + 4)
        pool.dma_start(tab2[:], a["table"][:, C_MASK:C_END]).then_inc(tab2_in, 16)
        pool.wait_ge(bank_evac, FIRST_EVAC["out2"])
        pool.dma_start(pool_a[:], a["pool_table"].rearrange("p b (g t) -> p b g t", g=4)).then_inc(pool_in, 16)
        pool.dma_start(pool_w[:], a["pool_w_2"][0].rearrange("g (c p) d -> p g c d", p=P)).then_inc(pool_in, 16)
        for b in range(NB):
            twice(dup2[:, NB + b], c2[:, b, 0:KV2 * DH], KV2)
        pool.wait_ge(rope_done, NB)
        for b in range(NB):
            ins = twice(dup2[:, b], p2[:, b, K2:K2 + KV2 * DH], KV2)
        ins.then_inc(dup_ready, 1)
        pool.wait_ge(g_stored, 16)
        pool.wait_ge(o_evac, 6)
        pool.wait_ge(mixed_lo, 8)
        load_row(ada_rows[0:1, :])
        pool.dma_start(final_row[:], a["final_norm_w_2"].rearrange("(a n) -> a n", a=1).broadcast_to([P, D])).then_inc(final_in, 16)
        pool.wait_ge(bank_evac, FIRST_EVAC["mlp2"])
        load_row(ada_rows[1:2, :])

    @block.scalar
    def _(act):
        chain = [0]

        def link(ins):
            chain[0] += 1
            ins.then_inc(achain, 1)
            act.wait_ge(achain, chain[0])

        act.dma_start(ident[:], a["table"][:, C_ID:C_ID + P]).then_inc(table_in, 16)
        rows = [a["c_2"][0], a["c_ctx_2"], a["pre_mix_g"][0], a["grp_swa_g"][0], a["grp_fox_g"][0], a["pre_ffn_g"][0],
                a["norm_attn_w_2"][0], a["norm_mlp_w_2"][0], a["pool_scale_2"][0]]
        r0 = 0
        for v in rows:
            n = v.shape[0] // P
            act.dma_start(stage[r0:r0 + n, 0, :], v.rearrange("(t p) -> t p", p=P)).then_inc(vec_in, 16)
            r0 += n
        assert r0 == 120
        act.dma_start(sink1[:], a["sinks"].broadcast_to([P, HEADS])).then_inc(misc_in, 16)
        act.dma_start(sink2[:], a["attn_sink_2"].broadcast_to([P, HEADS])).then_inc(misc_in, 16)
        act.dma_start(bforget[:], a["b_forget"].broadcast_to([P, HEADS])).then_inc(misc_in, 16)

        taken = [0]

        def squares(g, src, out=junk):
            for b in range(NB):
                if taken[0]:
                    act.wait_ge(squared, taken[0])
                act.activation(out[:], src(b), ACT.Square, accum_out=sq[:, b, g:g + 1]).then_inc(squared, 1)
                taken[0] += 1

        def root(name, w=NB):
            act.wait_ge(mean_ready, STAT[name] + 1)
            act.activation(ssq[:, 4:4 + w], ssq[:, 0:w], ACT.Sqrt).then_inc(root_ready, 1)

        def scale_rows(name, src, dst, r=lambda g: rstdx[:, 0:1]):
            def scale(g):
                act.activation(dst[:, 0, g * N:(g + 1) * N], src[:, 0, g * N:(g + 1) * N], ACT.Copy,
                               scale=r(g)).then_inc(xn_act, 1)
            act.wait_ge(rstd_ready, STAT[name] + 1)
            return scale

        def prep(name, gain, hi, shift=None, pre=None):
            n0, n = PREP[name]

            def scale(g):
                act.wait_ge(prep_turned, n0 + g + 1)
                if g >= 2:
                    act.wait_ge(h_ready, n0 + g - 1)
                for j in range(2):
                    k = 4 * g + j
                    out = (u_buf, conv)[g % 2][:].rearrange("p a b -> p (a b)")[:, TOK * j:TOK * j + TOK]
                    if gain is None:
                        ins = act.activation(out, tt(g % 2)[:, j, :], ACT.Copy)
                    elif shift is None:
                        ins = act.activation(out, tt(g % 2)[:, j, :], ACT.Copy, scale=gain[:, k:k + 1])
                    else:
                        ins = act.activation(out, tt(g % 2)[:, j, :], ACT.Identity, scale=gain[:, k:k + 1],
                                             bias=shift[:, k:k + 1])
                ins.then_inc(tmp_act, 1)

            def part(g):
                act.wait_ge(tmp_act, n0 + g + 1)
                act.wait_ge(tmp_dve, n0 + g + 1)
                tmp = (u_buf, conv)[g % 2][:].rearrange("p a b -> p (a b)")
                act.activation(hi[:, 4 * g:4 * g + 4, :].rearrange("p a b -> p (a b)"), tmp, ACT.Copy).then_inc(prep_hi, 1)

            pipeline(n, pre, scale, part)

        def hi(s, d=0):
            if s % 2 == 0:
                act.wait_ge(raw_full[s // 2 % 4], 32 * (s // 8 + 1) + d * 4)
            if s >= 4:
                act.wait_ge(step_done, s - 3 + d)
            act.activation(w_hi[:, s % 4], raw[:, s // 2 % 4, STEPK * (s % 2):STEPK * (s % 2) + STEPK, :],
                           ACT.Copy).then_inc(hi_ready, 1)

        def his(s, n, d=0):
            for k in range(n):
                if s + k < STEPS:
                    hi(s + k, d)

        def body(s, d=0, post=None, n=8):
            his(s + 3, 3, d)
            if post:
                post[0]()
            his(s + 6, 1, d)
            if post:
                post[1]()
            his(s + 7, n - 4, d)

        def evac(dst, parity, func=ACT.Copy, width=N, s=None, d=0, scaled=False):
            act.wait_ge(step_done, s + d)
            for b in range(NB):
                scale = rstdx[:, b:b + 1] if scaled else 1.0
                act.activation(dst(b), G[:, 2 * parity + b, 0:width], func, scale=scale).then_inc(bank_evac, 1)

        act.wait_ge(cols_ready, 1)
        act.activation(silu[:].rearrange("p a b -> p (a b)"), gains[:, 0:32], ACT.Exp, scale=-1.0).then_inc(silu_e, 1)

        def first_squares(g):
            act.wait_ge(x_in[g], 16)
            squares(g, lambda b: x[:, b, g * N:g * N + N])

        his(0, 1)
        prep("in1", gains[:, PRE_MIX:], h_hi, pre=first_squares)
        his(1, 2)
        root("in1")
        act.wait_ge(rstd_ready, STAT["in1"] + 1)

        s0 = 2 * FIRST_LOAD["in1"]
        with act.Fori(0, 4) as i:
            for c in range(2):
                body(s0 + 8 * c, i * 16)
                evac(lambda b: p1[:, b, bass.ds(i * (2 * N) + c * N, N)], c, s=s0 + 8 * c + 8, d=i * 16,
                     scaled=True)
        body(s0 + 64)
        evac(lambda b: p1[:, b, 8 * N:W_IN1], 0, width=W_IN1 - 8 * N, s=s0 + 72, scaled=True)

        act.wait_ge(z_ready, 1)
        act.activation(lf[:], z[:], ACT.Exp, scale=-1.0).then_inc(e_ready, 1)
        act.wait_ge(e1_ready, 1)
        act.activation(lf[:], lf[:], ACT.Ln).then_inc(l_ready, 1)
        for g in range(7):
            act.wait_ge(qk_turned, g + 1)
            act.activation(qk1[:, 4 * g:4 * g + 2, :], tt(g % 2)[:, 0:2, :], ACT.Copy).then_inc(qk_act, 1)
        for b in range(4):
            act.wait_ge(nm_ready, b + 1)
            if b < 2:
                act.activation(es[:, b, :], es[:, b, :], ACT.Exp).then_inc(es_ready, 1)
            for i in range(8):
                n = 8 * b + i
                act.activation(sm1[b % 2][:, i, 0:P], sm1[b % 2][:, i, 0:P], ACT.Exp, scale=SCALE,
                               bias=nm[:, b % 2, 2 * i:2 * i + 1], accum_out=rs[:, b % 2, 2 * i:2 * i + 1])
                act.activation(sm1[b % 2][:, i, P:3 * P], sm1[b % 2][:, i, P:3 * P], ACT.Exp, scale=SCALE,
                               bias=nm[:, b % 2, 2 * i + 1:2 * i + 2],
                               accum_out=rs[:, b % 2, 2 * i + 1:2 * i + 2]).then_inc(p_ready, 1)
            for i in range(8):
                n = 8 * b + i
                act.wait_ge(pt_turned, n + 1)
                if n >= 2:
                    act.wait_ge(pt_used, n - 1)
                act.activation(pt1[:, n % 2, :], T[:, n % 2, 0:3 * P], ACT.Copy).then_inc(pt_ready, 1)
            if b >= 1:
                act.wait_ge(o_evac, b)
                squares(b - 1, lambda k: o1[:, k, (b - 1) * N:b * N], junk1)
        act.wait_ge(o_evac, 4)
        squares(3, lambda k: o1[:, k, 3 * N:4 * N], junk1)
        root("out1", 2 * NB)
        prep("out1", gains[:, GRP:], h_hi, pre=scale_rows("out1", o1, o1, lambda g: rstd[:, g // 2:g // 2 + 1]))

        s0 = 2 * FIRST_LOAD["out1"]
        for c in range(4):
            body(s0 + 8 * c)
            act.wait_ge(step_done, s0 + 8 * c + 8)
            squares(c, lambda b: G[:, 2 * (c % 2) + b, :])
        root("y1")

        def new_squares(name):
            def take(g):
                act.wait_ge(x_new, X_NEW[name] + g + 1)
                squares(g, lambda b: x[:, b, g * N:g * N + N])
            return take

        prep("up1", gains[:, PRE_FFN:], h_hi, pre=new_squares("up1"))
        root("up1")
        act.wait_ge(rstd_ready, STAT["up1"] + 1)

        def up_evac(c, e, d, func):
            evac(lambda b: u_buf[:, b, :], c % 2, func, s=e, d=d, scaled=func == ACT.Copy)

        def post1(u, tile, du=0, dt=0):
            def taps():
                act.wait_ge(turned, u + 1 + du)
                if u >= 1:
                    act.wait_ge(conv_used, u + du)
                for j in range(CK):
                    t = (tile + j) if j < 2 else (CT1 + tile + j - 2)
                    ins = act.activation(conv[:, j, :], tt(0)[:, j, :], ACT.Identity,
                                         scale=convw[:, 2, bass.ds(t + dt, 1)], bias=convw[:, 3, bass.ds(t + dt, 1)])
                ins.then_inc(base_ready, 1)

            def gelu():
                act.wait_ge(up_read, u + 1 + du)
                act.activation(conv[:, 0:2, :], conv[:, 0:2, :], ACT.Gelu_apprx_tanh).then_inc(gelu_done, 1)

            return taps, gelu

        tile = 0
        for g, n in zip("abc", UPS1):
            s0, u0 = 2 * FIRST_LOAD["up1" + g], UP0["up1" + g]
            body(s0)
            up_evac(0, s0 + 8, 0, ACT.Copy)
            body(s0 + 8, 0, post1(u0, tile))
            up_evac(1, s0 + 16, 0, ACT.Copy)
            with act.Fori(0, n // 2 - 1) as i:
                for c in range(2):
                    body(s0 + 16 + 8 * c, i * 16, post1(u0 + 1 + c, tile + 2 + 2 * c, i * 2, i * 4))
                    up_evac(c, s0 + 24 + 8 * c, i * 16, ACT.Copy)
            tile += 2 * n
            s0, per = 2 * FIRST_LOAD["down1" + g], 8 if n == 8 else 6
            body(s0, 0, post1(u0 + n - 1, tile - 2), per)
            for c in range(1, 4):
                body(s0 + per * c, n=per)
                if n == 6:
                    act.wait_ge(bank_evac, FIRST_EVAC["down1c"] + 2 * c)
                    squares(c - 1, lambda b: y[:, b, (c - 1) * N:c * N])
        act.wait_ge(bank_evac, FIRST_EVAC["in2"])
        squares(3, lambda b: y[:, b, 3 * N:4 * N])
        root("y2")
        for g in range(4):
            new_squares("in2")(g)
        root("in2")
        prep("in2", comb, h_hi, adac[:, 0, :], scale_rows("in2", x, y))

        s0 = 2 * FIRST_LOAD["in2"]
        for k, col in enumerate((0, N, U2, U2 + N)):
            body(s0 + 8 * k)
            evac(lambda b: p2[:, b, col:col + N], k % 2, s=s0 + 8 * k + 8)
            if k == 0:
                act.wait_ge(ctx_in, 16)
                for g in range(4):
                    squares(g, lambda b: y[:, b, g * N:g * N + N])
            if k == 1:
                root("ctx")
                prep("ctx", comb, a_hi, adac[:, 6, :], scale_rows("ctx", y, y, lambda g: rstd[:, 0:1]))
        body(s0 + 32)
        act.wait_ge(step_done, s0 + 40)
        for b in range(NB):
            act.activation(p2[:, b, K2:K2 + N], G[:, b, :], ACT.Copy).then_inc(bank_evac, 1)
            act.activation(c2[:, b, :], G[:, 2 + b, :], ACT.Copy).then_inc(bank_evac, 1)

        for g in range(4):
            act.wait_ge(qk_turned, 7 + g + 1)
            dst = q2t[:, 4 * g:4 * g + 2, :] if g < 2 else k2t[:, 2 * (g - 2), :].rearrange("p (a n) -> p a n", a=2)
            act.activation(dst, tt((7 + g) % 2)[:, 0:2, :], ACT.Copy).then_inc(qk_act, 1)
        for b in range(8):
            act.wait_ge(nm_ready, 4 + b + 1)
            half, q0 = b // 4, 4 * (b % 4)
            act.activation(es[:, half, q0:q0 + 4], es[:, half, q0:q0 + 4], ACT.Exp).then_inc(es_ready, 1)
            for i in range(4):
                act.activation(sm2[:, b % 2, i, :], sm2[:, b % 2, i, :], ACT.Exp, scale=SCALE,
                               bias=nm[:, half, q0 + i:q0 + i + 1],
                               accum_out=rs[:, half, q0 + i:q0 + i + 1]).then_inc(p_ready, 1)
            for i in range(4):
                n = 32 + 4 * b + i
                act.wait_ge(pt_turned, n + 1)
                act.wait_ge(pt_used, n - 3)
                act.activation(pt2[:, n % 4, :], T[:, n % 2, :], ACT.Copy).then_inc(pt_ready, 1)
        for g in range(4):
            act.wait_ge(pooled_mm, g + 1)
            act.activation(pooled[:, 2 * g:2 * g + 2, :], G[:, g, :].rearrange("p (a n) -> p a n", a=2),
                           ACT.Copy).then_inc(pooled_ev, 1)
        prep("out2", None, h_hi)

        s0 = 2 * FIRST_LOAD["out2"]
        for c in range(4):
            body(s0 + 8 * c)
            if c:
                new_squares("out2")(c - 1)
        new_squares("out2")(3)
        root("up2")
        prep("up2", comb, h_hi, adac[:, 3, :], scale_rows("up2", x, y))

        s0, u0 = 2 * FIRST_LOAD["mlp2"], UP0["mlp2"]

        def post2(u, du):
            def square():
                act.wait_ge(turned, u + 1 + du)
                act.wait_ge(a_ready, u + du)
                act.activation(conv[:], tt(0), ACT.Square).then_inc(up_read, 1)

            return square, lambda: None

        def group2(s, u, d, du, last=False):
            for c in range(4):
                body(s + 8 * c, d, post2(u + c - 1, du) if c else None)
                up_evac(c, s + 8 * c + 8, d, ACT.Relu)
            for c in range(4):
                body(s + 32 + 8 * c, d, None if c else post2(u + 3, du))
                if last and c:
                    new_squares("final")(c - 1)
            if last:
                new_squares("final")(3)
                root("final")

        with act.Fori(0, GROUPS2 - 1) as g:
            group2(s0, u0, g * 64, g * 4)
        group2(s0 + 64 * (GROUPS2 - 1), u0 + 4 * (GROUPS2 - 1), 0, 0, True)

    @block.vector
    def _(dve):
        chain = [0]

        def link(ins):
            chain[0] += 1
            ins.then_inc(vchain, 1)
            dve.wait_ge(vchain, chain[0])

        def lo(s, d=0):
            if s >= STEPS:
                return
            dve.wait_ge(hi_ready, s + 1 + d)
            dve.tensor_tensor(w_lo[:, s % 4], raw[:, s // 2 % 4, STEPK * (s % 2):STEPK * (s % 2) + STEPK, :],
                              w_hi[:, s % 4].bitcast(F32), ALU.subtract).then_inc(lo_ready, 1)

        def los(s, n, d=0):
            for k in range(n):
                lo(s + k, d)

        def ada_op(run, k, d=0, dt=0):
            q, first, _ = ADA_RUNS[run]
            half, n = k % 2, ADA_BASE[run] + k
            dve.wait_ge(ada_full[half], 16 * (n // 2 + 1) + dt * 16)
            if n:
                dve.wait_ge(ada_used, n + d)
            for c, acc in enumerate(accs(q)):
                ins = dve.scalar_tensor_tensor(out=acc[:, half, :], in0=ada_w[:, half, :],
                                               scalar=silu[:, c, bass.ds(dt + (first + k) // 2, 1)],
                                               in1=acc[:, half, :], op0=ALU.mult, op1=ALU.add)
            ins.then_inc(ada_used, 1)

        def ada_zeros():
            dve.memset(ada_acc[:], 0.0).then_inc(ada_zero, 1)

        def ada_finish(q):
            dve.wait_ge(ada_summed, q + 1)
            part, bufs = ADA_ORDER[q]
            dve.tensor_tensor(adac[:, part, :], T[:, 3, 0:KT], bada[:, KT * part:KT * part + KT], ALU.add)
            if len(bufs) == 2:
                dve.tensor_tensor(adac[:, 6 + part, :], T[:, 3, KT:2 * KT], bada[:, KT * part:KT * part + KT], ALU.add)
            if q >= 4:
                dve.memset(ones_again[:], 1.0).then_inc(ada_col, 1)
            else:
                dve.memset(ada_acc[:, 0:len(bufs)], 0.0).then_inc(ada_col, 1)
            dve.wait_ge(ada_col, q + 1)

        def root(name, dst, width=D, w=NB):
            k = STAT[name]
            dve.wait_ge(squared, SQUARED[name])
            link(dve.tensor_reduce(ssq[:, 0:w], sq[:].rearrange("p b (h c) -> p (b h) c", c=NB * 4 // w), AX_X, ALU.add))
            dve.tensor_scalar(ssq[:, 0:w], ssq[:, 0:w], 1.0 / width, EPS, ALU.mult, ALU.add).then_inc(mean_ready, 1)
            dve.wait_ge(root_ready, k + 1)
            dve.reciprocal(dst[:, 0:w], ssq[:, 4:4 + w]).then_inc(rstd_ready, 1)
            dve.wait_ge(rstd_ready, k + 1)

        def scale_rows(src, dst, r=lambda g: rstdx[:, 1:2]):
            def scale(g):
                dve.tensor_scalar(dst[:, 1, g * N:(g + 1) * N], src[:, 1, g * N:(g + 1) * N], r(g), None,
                                  ALU.mult).then_inc(xn_dve, 1)
            return scale

        def prep(name, gain, hi, lo_out, shift=None, pre=None):
            n0, n = PREP[name]

            def scale(g):
                dve.wait_ge(prep_turned, n0 + g + 1)
                if g >= 2:
                    dve.wait_ge(h_ready, n0 + g - 1)
                for j in range(2, 4):
                    k = 4 * g + j
                    out = (u_buf, conv)[g % 2][:].rearrange("p a b -> p (a b)")[:, TOK * j:TOK * j + TOK]
                    if gain is None:
                        ins = dve.tensor_copy(out, tt(g % 2)[:, j, :])
                    elif shift is None:
                        ins = dve.tensor_scalar(out, tt(g % 2)[:, j, :], gain[:, k:k + 1], None, ALU.mult)
                    else:
                        ins = dve.tensor_scalar(out, tt(g % 2)[:, j, :], gain[:, k:k + 1], shift[:, k:k + 1],
                                                ALU.mult, ALU.add)
                ins.then_inc(tmp_dve, 1)

            def rest(g):
                dve.wait_ge(prep_hi, n0 + g + 1)
                tmp = (u_buf, conv)[g % 2][:].rearrange("p a b -> p (a b)")
                dve.tensor_tensor(lo_out[:, 4 * g:4 * g + 4, :].rearrange("p a b -> p (a b)"), tmp,
                                  hi[:, 4 * g:4 * g + 4, :].rearrange("p a b -> p (a b)").bitcast(F32),
                                  ALU.subtract).then_inc(h_ready, 1)

            pipeline(n, pre, scale, rest)

        dve.memset(ones_col[:], 1.0)
        ada_zeros()
        dve.wait_ge(vec_turned, 1)
        dve.tensor_copy(gains[:], T[:, 3, 0:120]).then_inc(cols_ready, 1)
        dve.wait_ge(cols_ready, 1)
        lo(0)
        prep("in1", gains[:, PRE_MIX:], h_hi, h_lo)
        los(1, 2)
        root("in1", rstdx)
        dve.wait_ge(silu_e, 1)
        flat = silu[:].rearrange("p a b -> p (a b)")
        link(dve.tensor_scalar(flat, flat, 1.0, None, ALU.add))
        link(dve.reciprocal(flat, flat))
        link(dve.tensor_tensor(flat, flat, gains[:, 0:32], ALU.mult))
        dve.wait_ge(ada_zero, 1)

        s0 = 2 * FIRST_LOAD["in1"]
        with dve.Fori(0, 8) as i:
            for k in range(8):
                lo(s0 + 3 + k, i * 8)
                if k % 2 == 1:
                    half = (k // 2) % 2
                    dve.wait_ge(ada_full[half], 16 + i * 32 + 16 * (k // 4))
                    for c in range(2):
                        ins = dve.scalar_tensor_tensor(out=ada_acc[:, c, half, :], in0=ada_w[:, half, :],
                                                       scalar=silu[:, c, bass.ds(i * 2 + k // 4, 1)],
                                                       in1=ada_acc[:, c, half, :], op0=ALU.mult, op1=ALU.add)
                    ins.then_inc(ada_used, 1)
                    dve.wait_ge(ada_used, i * 4 + k // 2 + 1)
        los(s0 + 67, 8)
        dve.wait_ge(vec2_turned, 1)
        dve.tensor_copy(convw[:].rearrange("p a b -> p (a b)"), T[:, 1, 0:4 * CTS])
        dve.tensor_copy(bada[:], T[:, 2, 0:96]).then_inc(cols2_ready, 1)
        dve.wait_ge(cols2_ready, 1)
        ada_finish(0)

        dve.wait_ge(bank_evac, FIRST_EVAC["out1"])
        dve.wait_ge(misc_in, 48)
        for b in range(NB):
            ins = dve.tensor_tensor(ct8[:, b, :], p1[:, b, FB:FB + HEADS], bforget[:], ALU.add)
        link(ins)
        link(dve.tensor_scalar(z[:], ct8[:], -1.0, None, ALU.mult))
        dve.tensor_tensor(z[:], z[:], ct8[:], ALU.max).then_inc(z_ready, 1)
        link(dve.tensor_scalar(ct8[:], ct8[:], 0.0, None, ALU.min))
        dve.wait_ge(e_ready, 1)
        dve.tensor_scalar(lf[:], lf[:], 1.0, None, ALU.add).then_inc(e1_ready, 1)
        dve.wait_ge(l_ready, 1)
        dve.tensor_tensor(lf[:], ct8[:], lf[:], ALU.subtract).then_inc(lf_ready, 1)
        dve.wait_ge(c_done, 1)
        dve.tensor_scalar(ct8[:], G[:, 0, 0:2 * HEADS].rearrange("p (b h) -> p b h", b=NB), 1 / SCALE, None, ALU.mult)
        link(dve.memset(cT[:], 0.0))
        dve.tensor_scalar(cT[0:HEADS, :], G[0:HEADS, 1, 0:TOK], -1 / SCALE, None, ALU.mult).then_inc(c_ready, 1)
        for g in range(6):
            dve.wait_ge(qk_turned, g + 1)
            dve.tensor_copy(qk1[:, 4 * g + 2:4 * g + 4, :], tt(g % 2)[:, 2:4, :]).then_inc(qk_dve, 1)
        dve.wait_ge(tab1_in, 16)
        slopes = 2.0 ** (-8.0 * np.arange(1, HEADS + 1) / HEADS)
        dve.wait_ge(c_ready, 1)

        def scores(b):
            if b >= 2:
                dve.wait_ge(pt_turned, 8 * (b - 1))
            for i in range(8):
                n = 8 * b + i
                bank = G[:, n % 4, :]
                dst = sm1[b % 2][:, i, :]
                dve.wait_ge(s_ready, n + 1)
                if b < 2:
                    ins = dve.scalar_tensor_tensor(out=dst, in0=tab1[:, ALI:ALI + 3 * P], scalar=float(slopes[n] / SCALE),
                                                   in1=bank[:, 0:3 * P], op0=ALU.mult, op1=ALU.add)
                else:
                    dve.scalar_tensor_tensor(out=dst[:, 0:P], in0=bank[:, 0:P], scalar=ct8[:, 0, n - 16:n - 15],
                                             in1=tab1[:, CAU:CAU + P], op0=ALU.add, op1=ALU.add)
                    ins = dve.scalar_tensor_tensor(out=dst[:, P:3 * P], in0=bank[:, P:3 * P],
                                                   scalar=ct8[:, 1, n - 16:n - 15], in1=tab1[:, CAU + P:CAU + 3 * P],
                                                   op0=ALU.add, op1=ALU.add)
                ins.then_inc(s_read, 1)
                if i >= 1:
                    maxima(b, i - 1)
            maxima(b, 7)
            dve.wait_ge(s_max, 8 * b + 8)

        def maxima(b, i):
            dve.wait_ge(s_read, 8 * b + i + 1)
            buf = sm1[b % 2]
            dve.reduce_max(mx[:, b % 2, 2 * i:2 * i + 1], buf[:, i, 0:P], AX_X)
            dve.reduce_max(mx[:, b % 2, 2 * i + 1:2 * i + 2], buf[:, i, P:3 * P], AX_X).then_inc(s_max, 1)

        def sinks(b):
            m, n_ = mx[:, b % 2, :], nm[:, b % 2, :]
            if b >= 2:
                dve.tensor_scalar(n_, m, -SCALE, None, ALU.mult).then_inc(nm_ready, 1)
                return
            link(dve.tensor_scalar(m, m, SCALE, None, ALU.mult))
            s = sink1[:, 8 * b:8 * b + 8].unsqueeze(2).broadcast_to([P, 8, 2])
            m3 = m.rearrange("p (h b) -> p h b", b=2)
            link(dve.tensor_tensor(m3, m3, s, ALU.max))
            dve.tensor_tensor(es[:, b, :].rearrange("p (h b) -> p h b", b=2), s, m3, ALU.subtract)
            dve.tensor_scalar(n_, m, -1.0, None, ALU.mult).then_inc(nm_ready, 1)

        def outputs(b):
            dve.wait_ge(pt_used, 8 * b + 8)
            r = rs[:, b % 2, :]
            if b < 2:
                dve.wait_ge(es_ready, b + 1)
                link(dve.tensor_tensor(r, r, es[:, b, :], ALU.add))
            link(dve.reciprocal(r, r))
            for k in range(NB):
                f = r.rearrange("p (h b) -> p h b", b=2)[:, :, k:k + 1].broadcast_to([P, 8, DH])
                ins = dve.tensor_tensor(o1[:, k, N * b:N * b + N].rearrange("p (h d) -> p h d", d=DH),
                                        T[:, 2 + k, :].rearrange("p (h d) -> p h d", d=DH), f, ALU.mult)
            ins.then_inc(o_evac, 1)

        scores(0)
        sinks(0)
        for b in range(4):
            if b < 3:
                scores(b + 1)
                sinks(b + 1)
            outputs(b)
        dve.wait_ge(o_evac, 4)
        root("out1", rstd, 1024, 2 * NB)
        prep("out1", gains[:, GRP:], h_hi, h_lo,
             pre=scale_rows(o1, o1, lambda g: rstd[:, 2 + g // 2:3 + g // 2]))

        s0 = 2 * FIRST_LOAD["out1"]
        dve.wait_ge(row_full, 16)
        for c in range(4):
            for k in range(8):
                lo(s0 + 8 * c + 3 + k)
                ada_op(1, 8 * c + k)
            dve.wait_ge(squared, SQUARED["out1"] + 2 * c + 2)
            for b in range(NB):
                dve.tensor_tensor(y[:, b, c * N:c * N + N], G[:, 2 * (c % 2) + b, :], row[:, c * N:c * N + N],
                                  ALU.mult).then_inc(bank_evac, 1)

        root("y1", rstd)
        dve.wait_ge(x_again, 16)

        def residual(name):
            def add(g):
                for b in range(NB):
                    ins = dve.scalar_tensor_tensor(out=x[:, b, g * N:g * N + N], in0=y[:, b, g * N:g * N + N],
                                                   scalar=rstd[:, b:b + 1], in1=x[:, b, g * N:g * N + N],
                                                   op0=ALU.mult, op1=ALU.add)
                ins.then_inc(x_new, 1)
            return add

        prep("up1", gains[:, PRE_FFN:], h_hi, h_lo, pre=residual("up1"))
        dve.memset(y[:], 0.0).then_inc(y_zero, 1)
        ada_finish(1)
        dve.memset(ada_third[:], 0.0).then_inc(y_zero, 1)
        dve.wait_ge(y_zero, 2)
        root("up1", rstdx)

        def body(s, d=0, post=None, n=8, adas=()):
            adas = list(adas)
            for k in range(n):
                lo(s + 3 + k, d)
                if post and k == 2:
                    post[0]()
                elif post and k == 3:
                    post[1]()
                elif not post or k >= 4:
                    left = n - k if not post else n - max(k, 4)
                    for _ in range(-(-len(adas) // left)):
                        ada_op(*adas.pop(0))

        def post1(u, tile, a_tile, du=0, dt=0):
            def taps():
                dve.wait_ge(base_ready, u + 1 + du)
                for tap in (1, 0):
                    k = 2 - tap
                    for j in range(CK):
                        t = (tile + j) if j < 2 else (CT1 + tile + j - 2)
                        ins = dve.scalar_tensor_tensor(out=conv[:, j, k:TOK], in0=tt(0)[:, j, 0:TOK - k],
                                                       scalar=convw[:, tap, bass.ds(t + dt, 1)], in1=conv[:, j, k:TOK],
                                                       op0=ALU.mult, op1=ALU.add)
                    if tap:
                        ins.then_inc(tap1, 1)
                        dve.wait_ge(tap1, u + 1 + du)
                ins.then_inc(up_read, 1)

            def product():
                hi, lo_ = (t[:, bass.ds(a_tile + dt, 2), :] for t in (a_hi, a_lo))
                dve.wait_ge(gelu_done, u + 1 + du)
                dve.tensor_tensor(prod[:], conv[:, 0:2, :], conv[:, 2:4, :], ALU.mult).then_inc(conv_used, 1)
                dve.wait_ge(conv_used, u + 1 + du)
                dve.tensor_copy(hi, prod[:]).then_inc(a_first, 1)
                dve.wait_ge(a_first, u + 1 + du)
                dve.tensor_tensor(lo_, prod[:], hi.bitcast(F32), ALU.subtract).then_inc(a_ready, 1)

            return taps, product

        def down_evac(c, e, d=0):
            dve.wait_ge(step_done, e + d)
            for b in range(NB):
                dve.tensor_tensor(y[:, b, c * N:c * N + N], y[:, b, c * N:c * N + N], G[:, 2 * (c % 2) + b, :],
                                  ALU.add).then_inc(bank_evac, 1)

        def times_row(c):
            dve.wait_ge(squared, SQUARED["up1"] + 2 * c + 2)
            cols = slice(c * N, c * N + N)
            link(dve.tensor_tensor(y[:, :, cols], y[:, :, cols], row[:, cols].unsqueeze(1).broadcast_to([P, NB, N]),
                                   ALU.mult))

        tile = 0
        for g, n, run_up, run_down, fin_up, fin_down in (("a", 8, 2, 3, None, 2), ("b", 8, 4, 5, None, 3),
                                                         ("c", 6, 6, None, 4, 5)):
            s0, u0 = 2 * FIRST_LOAD["up1" + g], UP0["up1" + g]
            first, each = (4, 4) if n == 8 else (7, 5)
            body(s0, adas=[(run_up, k) for k in range(first)])
            if fin_up is not None:
                ada_finish(fin_up)
            if n == 8:
                with dve.Fori(0, n - 1) as i:
                    body(s0 + 8, i * 8, post1(u0, tile, 0, i, i * 2),
                         adas=[(run_up, first + k, i * each, i * (each // 2)) for k in range(each)])
            else:
                for c in range(1, n):
                    body(s0 + 8 * c, 0, post1(u0 + c - 1, tile + 2 * c - 2, 2 * c - 2),
                         adas=[(run_up, first + each * (c - 1) + k) for k in range(each)])
            tile += 2 * n
            s0, per = 2 * FIRST_LOAD["down1" + g], 8 if n == 8 else 6
            if n == 6:
                dve.wait_ge(row_full, 32)
            for c in range(4):
                body(s0 + per * c, 0, post1(u0 + n - 1, tile - 2, 2 * n - 2) if c == 0 else None, per,
                     adas=[(run_down, 4 * c + k) for k in range(4)] if run_down is not None else ())
                down_evac(c, s0 + per * c + per)
                if c == 0:
                    ada_finish(fin_down)
                if n == 6 and c:
                    times_row(c - 1)
        times_row(3)
        root("y2", rstd)
        for g in range(4):
            residual("in2")(g)
        root("in2", rstdx)

        def combine(norm, part):
            link(dve.tensor_scalar(comb[:], adac[:, part, :], 1.0, None, ALU.add))
            link(dve.tensor_tensor(comb[:], comb[:], gains[:, norm:norm + KT], ALU.mult))

        dve.wait_ge(g_turned, 1)
        dve.tensor_copy(grow[:].rearrange("t r p -> t (r p)"), T[0:16, 3, 0:2 * P]).then_inc(g_copied, 1)
        combine(NORM_A, 1)
        prep("in2", comb, h_hi, h_lo, adac[:, 0, :], scale_rows(x, y))

        s0 = 2 * FIRST_LOAD["in2"]
        for k in range(4):
            los(s0 + 8 * k + 3, 8)
            if k == 1:
                root("ctx", rstd)
                combine(NORM_A, 7)
                prep("ctx", comb, a_hi, a_lo, adac[:, 6, :], scale_rows(y, y, lambda g: rstd[:, 1:2]))
        los(s0 + 35, 8)

        dve.wait_ge(bank_evac, FIRST_EVAC["out2"])
        dve.wait_ge(tab2_in, 16)
        cos = tab2[:, COS2:COS2 + 2 * DH].rearrange("p (b d) -> p b d", b=NB)
        sin = tab2[:, SIN2:SIN2 + 2 * DH].rearrange("p (b r s d) -> p b r s d", b=NB, r=2, s=2)
        for b in range(NB):
            qk = p2[:, b, 0:K2 + 256].rearrange("p (h d) -> p h d", d=DH)
            qk5 = p2[:, b, 0:K2 + 256].rearrange("p (h r s d) -> p h r s d", r=2, s=2, d=16)
            rot5 = rot[:].rearrange("p h (r s d) -> p h r s d", r=2, s=2)
            for s in range(2):
                ins = dve.tensor_tensor(rot5[:, :, :, s, :], qk5[:, :, :, 1 - s, :],
                                        sin[:, b, :, s, :].unsqueeze(1).broadcast_to([P, 20, 2, 16]), ALU.mult)
            link(ins)
            link(dve.tensor_tensor(qk, qk, cos[:, b, :].unsqueeze(1).broadcast_to([P, 20, DH]), ALU.mult))
            ins = dve.tensor_tensor(qk, qk, rot[:], ALU.add)
            ins.then_inc(rope_done, 1)
            dve.wait_ge(rope_done, b + 1)
        for g in range(4):
            dve.wait_ge(qk_turned, 7 + g + 1)
            dst = q2t[:, 4 * g + 2:4 * g + 4, :] if g < 2 else k2t[:, 2 * (g - 2) + 1, :].rearrange("p (a n) -> p a n", a=2)
            dve.tensor_copy(dst, tt((7 + g) % 2)[:, 2:4, :]).then_inc(qk_dve, 1)

        def scores2(b):
            half, q0 = b // 4, 4 * (b % 4)
            if b >= 2:
                dve.wait_ge(pt_turned, 32 + 4 * (b - 1))
            for i in range(4):
                n = 32 + 4 * b + i
                dve.wait_ge(s_ready, n + 1)
                dve.tensor_tensor(sm2[:, b % 2, i, :], G[:, n % 4, :], tab2[:, MASK2 + N * (i % 2):MASK2 + N * (i % 2) + N],
                                  ALU.add).then_inc(s_read, 1)
                dve.wait_ge(s_read, n + 1)
                dve.reduce_max(mx[:, half, q0 + i:q0 + i + 1], sm2[:, b % 2, i, :], AX_X).then_inc(s_max, 1)
            dve.wait_ge(s_max, 32 + 4 * b + 4)
            m = mx[:, half, q0:q0 + 4]
            link(dve.tensor_scalar(m, m, SCALE, None, ALU.mult))
            s = sink2[:, 2 * b:2 * b + 2].unsqueeze(2).broadcast_to([P, 2, 2])
            m3 = m.rearrange("p (h b) -> p h b", b=2)
            link(dve.tensor_tensor(m3, m3, s, ALU.max))
            dve.tensor_tensor(es[:, half, q0:q0 + 4].rearrange("p (h b) -> p h b", b=2), s, m3, ALU.subtract)
            dve.tensor_scalar(nm[:, half, q0:q0 + 4], m, -1.0, None, ALU.mult).then_inc(nm_ready, 1)

        def outputs2(half):
            dve.wait_ge(pt_used, 32 + 16 * half + 16)
            dve.wait_ge(es_ready, 2 + 4 * half + 4)
            r = rs[:, half, :]
            link(dve.tensor_tensor(r, r, es[:, half, :], ALU.add))
            link(dve.reciprocal(r, r))
            for k in range(NB):
                f = r.rearrange("p (h b) -> p h b", b=2)[:, :, k:k + 1].broadcast_to([P, 8, DH])
                ins = dve.tensor_tensor(o2[:, k, N * half:N * half + N].rearrange("p (h d) -> p h d", d=DH),
                                        T[:, 2 + k, :].rearrange("p (h d) -> p h d", d=DH), f, ALU.mult)
            ins.then_inc(o_evac, 1)

        scores2(0)
        for b in range(8):
            if b < 7:
                scores2(b + 1)
            if b % 4 == 3:
                outputs2(b // 4)
        for j in range(8):
            dve.wait_ge(mixed_mm, j + 1)
            tmp = (rot, rot)[0][:].rearrange("p h d -> p (h d)")[:, TOK * (j % 2):TOK * (j % 2) + TOK]
            link(dve.tensor_scalar(tmp, G[:, j % 4, 0:TOK], gains[:, POOL_S + j:POOL_S + j + 1], None, ALU.mult))
            dve.tensor_copy(h_hi[:, 8 + j, :], tmp).then_inc(mixed_hi, 1)
            dve.wait_ge(mixed_hi, j + 1)
            dve.tensor_tensor(h_lo[:, 8 + j, :], tmp, h_hi[:, 8 + j, :].bitcast(F32), ALU.subtract).then_inc(mixed_lo, 1)
        prep("out2", None, h_hi, h_lo)

        s0 = 2 * FIRST_LOAD["out2"]
        dve.wait_ge(row_full, 48)
        for c in range(4):
            los(s0 + 8 * c + 3, 8)
            cols = slice(c * N, c * N + N)
            dve.wait_ge(step_done, s0 + 8 * c + 8)
            for b in range(NB):
                dve.tensor_tensor(y[:, b, cols], G[:, 2 * (c % 2) + b, :], row[:, cols], ALU.mult).then_inc(bank_evac, 1)
            dve.wait_ge(bank_evac, FIRST_EVAC["out2"] + 2 * c + 2)
            dve.tensor_tensor(x[:, :, cols], x[:, :, cols], y[:, :, cols], ALU.add).then_inc(x_new, 1)
        dve.wait_ge(x_new, X_NEW["final"])
        root("up2", rstdx)
        combine(NORM_M, 4)
        prep("up2", comb, h_hi, h_lo, adac[:, 3, :], scale_rows(x, y))
        dve.wait_ge(prep_turned, PREP["up2"][0] + 4)
        dve.memset(y[:], 0.0).then_inc(y_zero, 1)
        dve.wait_ge(y_zero, 3)

        def post2(u, c, du):
            def split():
                dve.wait_ge(up_read, u + 1 + du)
                dve.tensor_copy(a_hi[:, 4 * c:4 * c + 4, :], conv[:]).then_inc(a_first, 1)
                dve.wait_ge(a_first, u + 1 + du)
                dve.tensor_tensor(a_lo[:, 4 * c:4 * c + 4, :], conv[:], a_hi[:, 4 * c:4 * c + 4, :].bitcast(F32),
                                  ALU.subtract).then_inc(a_ready, 1)

            return lambda: None, split

        def group2(s, u, d, du, last=False):
            for c in range(4):
                body(s + 8 * c, d, post2(u + c - 1, c - 1, du) if c else None)
            for c in range(4):
                body(s + 32 + 8 * c, d, None if c else post2(u + 3, 3, du))
                down_evac(c, s + 32 + 8 * c + 8, d)
                if last:
                    cols = slice(c * N, c * N + N)
                    dve.wait_ge(bank_evac, FIRST_EVAC["mlp2"] + 16 * GROUPS2 - 8 + 2 * c + 2)
                    link(dve.tensor_tensor(y[:, :, cols], y[:, :, cols],
                                           row[:, cols].unsqueeze(1).broadcast_to([P, NB, N]), ALU.mult))
                    dve.tensor_tensor(x[:, :, cols], x[:, :, cols], y[:, :, cols], ALU.add).then_inc(x_new, 1)

        s0, u0 = 2 * FIRST_LOAD["mlp2"], UP0["mlp2"]
        with dve.Fori(0, GROUPS2 - 1) as g:
            group2(s0, u0, g * 64, g * 4)
        dve.wait_ge(row_full, 64)
        group2(s0 + 64 * (GROUPS2 - 1), u0 + 4 * (GROUPS2 - 1), 0, 0, True)

        root("final", rstdx)
        dve.wait_ge(final_in, 16)
        for g in range(4):
            cols = slice(g * N, g * N + N)
            for b in range(NB):
                ins = dve.scalar_tensor_tensor(out=y[:, b, cols], in0=x[:, b, cols], scalar=rstdx[:, b:b + 1],
                                               in1=final_row[:, cols], op0=ALU.mult, op1=ALU.mult)
            ins.then_inc(out_ready, 1)

    @block.tensor
    def _(pe):
        def step(s, parity, acts, kt, first, last, ready=None, d=0, width=N, also=None):
            pe.wait_ge(hi_ready, s + 1 + d)
            pe.wait_ge(lo_ready, s + 1 + d)
            if ready is not None:
                pe.wait_ge(*ready)
            for j in range(STEPK):
                wh, wl = w_hi[:, s % 4, j, 0:width], w_lo[:, s % 4, j, 0:width]
                for n, (hi, lo) in enumerate(acts):
                    for b in range(NB):
                        out = G[:, 2 * (parity if n == 0 else 1) + b, 0:width]
                        ah, al = hi[:, kt + j, b * P:b * P + P], lo[:, kt + j, b * P:b * P + P]
                        f, l = first and j == 0, last and j == STEPK - 1
                        pe.matmul(out, ah, wh, start=f, stop=False)
                        pe.matmul(out, ah, wl, start=False, stop=False)
                        mm = pe.matmul(out, al, wh, start=False, stop=l)
            mm.then_inc(step_done, 1)

        def steps(s, k0, k1, parity, acts, ready, e=None, d=0, de=0, per=8, width=N):
            if k0 == 0 and e is not None and not (isinstance(e, int) and e <= 0):
                pe.wait_ge(bank_evac, e + de)
            for k in range(k0, k1):
                step(s + k, parity, acts, STEPK * k, k == 0, k == per - 1, ready(k), d, width)

        def prepped(name):
            n0 = PREP[name][0]
            return lambda k: (h_ready, n0 + k // 2 + 1)

        H, A = [(h_hi, h_lo)], [(a_hi, a_lo)]

        def turn_prep(name, src, waits=()):
            n0, n = PREP[name]
            for g in range(n):
                if name in NORMED:
                    pe.wait_ge(xn_act, NORMED[name] + g + 1)
                    pe.wait_ge(xn_dve, NORMED[name] + g + 1)
                if name == "up1":
                    pe.wait_ge(x_new, X_NEW[name] + g + 1)
                if name == "in1":
                    pe.wait_ge(x_in[g], 16)
                if n0 + g >= 2:
                    pe.wait_ge(tmp_act, n0 + g - 1)
                    pe.wait_ge(tmp_dve, n0 + g - 1)
                for j in range(4):
                    for b in range(NB):
                        mm = pe.transpose(tt(g % 2)[:, j, b * P:b * P + P], src[:, b, (4 * g + j) * P:(4 * g + j + 1) * P],
                                          ident[:])
                mm.then_inc(prep_turned, 1)

        def ada_sum(q):
            pe.wait_ge(ada_used, ADA_END[q])
            if q >= 1:
                pe.wait_ge(ada_col, q)
            for c, acc in enumerate(accs(q)):
                for t in range(KT):
                    mm = pe.matmul(T[:, 3, KT * c + t:KT * c + t + 1], acc[:, t // 8, (t % 8) * P:(t % 8 + 1) * P], ones_col[:],
                                   start=True, stop=True)
            mm.then_inc(ada_summed, 1)

        pe.wait_ge(table_in, 16)
        pe.wait_ge(vec_in, 16 * 9)
        pe.transpose(T[:, 3, 0:120], stage[0:120, 0, :], ident[0:120, 0:120]).then_inc(vec_turned, 1)
        pe.wait_ge(cols_ready, 1)
        turn_prep("in1", x)

        s0, r = 2 * FIRST_LOAD["in1"], prepped("in1")
        steps(s0, 0, 8, 0, H, r)
        steps(s0 + 8, 0, 8, 1, H, r)
        with pe.Fori(0, 3) as i:
            for c in range(2):
                steps(s0 + 16 + 8 * c, 0, 8, c, H, r, 2 * (c + 1), i * 16, i * 4)
        steps(s0 + 64, 0, 8, 0, H, r, 14, width=W_IN1 - 8 * N)
        pe.wait_ge(vec2_in, 16 * 5)
        for k in range(4):
            pe.transpose(T[:, 1, k * CTS:(k + 1) * CTS], stage[0:CTS, 1 + k, :], ident[0:CTS, 0:CTS])
        pe.transpose(T[:, 2, 0:96], stage[0:96, 5, :], ident[0:96, 0:96]).then_inc(vec2_turned, 1)
        ada_sum(0)

        pe.wait_ge(ada_col, 1)
        pe.wait_ge(tab1_in, 16)
        pe.wait_ge(lf_ready, 1)
        tri, one = tab1[:, TRI:TRI + P], tab1[:, ONE:ONE + P]
        pe.matmul(G[:, 0, 0:HEADS], tri, lf[:, 0, :], start=True, stop=True)
        pe.matmul(G[:, 0, HEADS:2 * HEADS], one, lf[:, 0, :], start=True, stop=False)
        pe.matmul(G[:, 0, HEADS:2 * HEADS], tri, lf[:, 1, :], start=False, stop=True)
        pe.matmul(G[0:HEADS, 1, 0:TOK], lf[:, 0, :], tab1[:, TRI:TRI + TOK], start=True, stop=False)
        pe.matmul(G[0:HEADS, 1, P:TOK], lf[:, 1, :], tri, start=False, stop=True).then_inc(c_done, 1)

        pe.wait_ge(dup_ready, 1)
        QK = ([QA + P * t for t in range(8)] + [-1, -2] + [QB + P * t for t in range(8)]
              + [KB + P * t for t in range(8)])

        for g in range(7):
            if g >= 2:
                pe.wait_ge(qk_act, g - 1)
                pe.wait_ge(qk_dve, g - 1)
            for j, col in enumerate(QK[4 * g:4 * g + 4]):
                for b in range(NB):
                    src = p1[:, b, col:col + P] if col >= 0 else dup1[:, b, -1 - col].rearrange("p a d -> p (a d)")
                    mm = pe.transpose(tt(g % 2)[:, j, b * P:b * P + P], src, ident[:])
            mm.then_inc(qk_turned, 1)
        pe.wait_ge(qk_act, 7)
        pe.wait_ge(qk_dve, 6)
        pe.wait_ge(c_ready, 1)

        def scores(b):
            for i in range(8):
                n = 8 * b + i
                h = n % HEADS
                q, k = (h // 2, 8 + h // 8) if b < 2 else (10 + h // 2, 18 + h // 2)
                rows = slice(DH * (h % 2), DH * (h % 2) + DH)
                if n >= 4:
                    pe.wait_ge(s_read, n - 3)
                fox = b >= 2
                for blk, (c0, w) in enumerate(((0, P), (P, 2 * P))):
                    out = G[:, n % 4, c0:c0 + w]
                    mm = pe.matmul(out, qk1[rows, q, P * blk:P * blk + P], qk1[rows, k, 0:w], start=True, stop=not fox)
                    if fox:
                        mm = pe.matmul(out, ident[:, h:h + 1].broadcast_to([P, P]), cT[:, 0:w],
                                       start=False, stop=True)
                mm.then_inc(s_ready, 1)

        def turn_p(n, src, width):
            pe.wait_ge(p_ready, n + 1)
            if n >= 2:
                pe.wait_ge(pt_ready, n - 1)
            for j in range(width // P):
                mm = pe.transpose(T[:, n % 2, P * j:P * j + P], src[:, P * j:P * j + P], ident[:])
            mm.then_inc(pt_turned, 1)

        def pv1(n):
            pe.wait_ge(pt_ready, n + 1)
            i, h = n % 8, n % HEADS
            if i == 0 and n >= 8:
                pe.wait_ge(o_evac, n // 8)
            v = VA + DH * (h // 8) if n < HEADS else VB + DH * h
            pe.matmul(T[:, 2, DH * i:DH * i + DH], pt1[:, n % 2, 0:P], p1[:, 0, v:v + DH], start=True, stop=True)
            pe.matmul(T[:, 3, DH * i:DH * i + DH], pt1[:, n % 2, P:2 * P], p1[:, 0, v:v + DH], start=True, stop=False)
            pe.matmul(T[:, 3, DH * i:DH * i + DH], pt1[:, n % 2, 2 * P:3 * P], p1[:, 1, v:v + DH],
                      start=False, stop=True).then_inc(pt_used, 1)

        scores(0)
        for b in range(4):
            if b < 3:
                scores(b + 1)
            for i in range(8):
                turn_p(8 * b + i, sm1[b % 2][:, i, :], 3 * P)
                if i >= 1:
                    pv1(8 * b + i - 1)
            pv1(8 * b + 7)
        pe.wait_ge(o_evac, 4)
        turn_prep("out1", o1)

        s0, e0, r = 2 * FIRST_LOAD["out1"], FIRST_EVAC["out1"], prepped("out1")
        with pe.Fori(0, 2) as i:
            for c in range(2):
                steps(s0 + 8 * c, 0, 8, c, H, r, e0 + 2 * (c - 1), i * 16, i * 4)
        turn_prep("up1", x)
        pe.wait_ge(tmp_act, PREP["up1"][0] + 4)
        pe.wait_ge(tmp_dve, PREP["up1"][0] + 4)
        ada_sum(1)

        def turn_up(u, e, d=0, du=0, de=0):
            pe.wait_ge(bank_evac, e + de)
            if u >= 1:
                pe.wait_ge(up_read, u + du)
            for j in range(CK):
                for b in range(NB):
                    mm = pe.transpose(tt(0)[:, j, b * P:b * P + P], u_buf[:, b, P * j:P * j + P], ident[:])
            mm.then_inc(turned, 1)

        for g, n, fin_up, fin_down in (("a", 8, None, 2), ("b", 8, None, 3), ("c", 6, 4, 5)):
            s0, e0, u0, r = 2 * FIRST_LOAD["up1" + g], FIRST_EVAC["up1" + g], UP0["up1" + g], prepped("up1")
            sd, ed = 2 * FIRST_LOAD["down1" + g], FIRST_EVAC["down1" + g]
            per = 8 if n == 8 else 6

            def ready(k, u0=u0):
                return a_ready, u0 + k + 1

            def up_pair(s, e, u, d, de, du, tail=False, finish=None):
                for c in range(2):
                    steps(s + 8 * c, 2, 8, c, H, r, d=d)
                    if tail and c == 1:
                        steps(sd, 0, 2, 0, A, ready, ed - 2, per=per)
                    else:
                        steps(s + 8 * c + 8, 0, 2, 1 - c, H, r, e + 2 * c, d, de)
                    turn_up(u + c, e + 2 * c + 2, d, du, de)
                    if c == 0 and finish is not None:
                        ada_sum(finish)

            steps(s0, 0, 2, 0, H, r, e0 - 2 if g != "a" else e0)
            up_pair(s0, e0, u0, 0, 0, 0, finish=fin_up)
            with pe.Fori(0, n // 2 - 2) as i:
                up_pair(s0 + 16, e0 + 4, u0 + 2, i * 16, i * 4, i * 2)
            up_pair(s0 + 8 * n - 16, e0 + 2 * n - 4, u0 + n - 2, 0, 0, 0, tail=True)
            for c in range(4):
                steps(sd + per * c, 2 if c == 0 else 0, per, c % 2, A, ready, ed + 2 * (c - 1), per=per)
                if c == 0 and fin_down is not None:
                    ada_sum(fin_down)
        pe.wait_ge(ada_col, 6)
        for n, part in enumerate((2, 5)):
            mm = pe.transpose(T[0:KT, 3, P * n:P * n + P], adac[:, part, :], ident[:])
        mm.then_inc(g_turned, 1)
        pe.wait_ge(g_copied, 1)
        turn_prep("in2", y)

        s0, e0, r = 2 * FIRST_LOAD["in2"], FIRST_EVAC["in2"], prepped("in2")
        for k in range(4):
            steps(s0 + 8 * k, 0, 8, k % 2, H, r, e0 + 2 * (k - 1))
            if k == 1:
                turn_prep("ctx", y)
        pe.wait_ge(bank_evac, e0 + 8)
        for k in range(8):
            step(s0 + 32 + k, 0, H + A, STEPK * k, k == 0, k == 7, (h_ready, PREP["ctx"][0] + k // 2 + 1))
        pe.wait_ge(bank_evac, FIRST_EVAC["out2"])

        pe.wait_ge(rope_done, 2)
        pe.wait_ge(dup_ready, 2)
        for g in range(4):
            pe.wait_ge(qk_act, 7 + g - 1)
            pe.wait_ge(qk_dve, 6 + g - 1)
            for j in range(4):
                for b in range(NB):
                    out = tt((7 + g) % 2)[:, j, b * P:b * P + P]
                    if g < 2:
                        src = p2[:, b, Q2 + P * (4 * g + j):Q2 + P * (4 * g + j + 1)]
                    else:
                        kv = 2 * (g - 2) + j // 2
                        src = dup2[:, NB * (j % 2) + b, kv].rearrange("p a d -> p (a d)")
                    mm = pe.transpose(out, src, ident[:])
            mm.then_inc(qk_turned, 1)
        pe.wait_ge(qk_act, 11)
        pe.wait_ge(qk_dve, 10)

        def scores2(b):
            for i in range(4):
                n = 32 + 4 * b + i
                h, blk = 2 * b + i // 2, i % 2
                rows = slice(DH * (h % 2), DH * (h % 2) + DH)
                pe.wait_ge(s_read, n - 3)
                pe.matmul(G[:, n % 4, :], q2t[rows, h // 2, P * blk:P * blk + P], k2t[rows, h // 4, :],
                          start=True, stop=True).then_inc(s_ready, 1)

        def pv2(n):
            pe.wait_ge(pt_ready, n + 1)
            m = n - 32
            h, blk = m // 2, m % 2
            if m == 16:
                pe.wait_ge(o_evac, 5)
            out = T[:, 2 + blk, DH * (h % 8):DH * (h % 8) + DH]
            kv = DH * (h // 4)
            for j in range(4):
                v = p2[:, j, V2 + kv:V2 + kv + DH] if j < 2 else c2[:, j - 2, 256 + kv:256 + kv + DH]
                mm = pe.matmul(out, pt2[:, n % 4, P * j:P * j + P], v, start=j == 0, stop=j == 3)
            mm.then_inc(pt_used, 1)

        scores2(0)
        for b in range(8):
            if b < 7:
                scores2(b + 1)
            for i in range(4):
                n = 32 + 4 * b + i
                turn_p(n, sm2[:, b % 2, i, :], N)
                if i >= 1:
                    pv2(n - 1)
            pv2(32 + 4 * b + 3)

        pe.wait_ge(pool_in, 32)
        pe.wait_ge(s_read, 64)
        for g in range(4):
            for c in range(2):
                for b in range(NB):
                    mm = pe.matmul(G[:, g, TOK * c:TOK * c + TOK], p2[:, b, U2 + PG * g + P * c:U2 + PG * g + P * c + P],
                                   pool_a[:, b, g, :], start=b == 0, stop=b == NB - 1)
            mm.then_inc(pooled_mm, 1)
        pe.wait_ge(pooled_ev, 4)
        for j in range(8):
            g, dt = j // 2, j % 2
            if j >= 4:
                pe.wait_ge(mixed_lo, j - 3)
            for c in range(2):
                mm = pe.matmul(G[:, j % 4, 0:TOK], pool_w[:, g, c, P * dt:P * dt + P], pooled[:, 2 * g + c, :],
                               start=c == 0, stop=c == 1)
            mm.then_inc(mixed_mm, 1)
        pe.wait_ge(o_evac, 6)
        pe.wait_ge(mixed_lo, 8)
        turn_prep("out2", o2)

        s0, e0, n0 = 2 * FIRST_LOAD["out2"], FIRST_EVAC["out2"], PREP["out2"][0]

        def r(k):
            return h_ready, n0 + min(k // 2, 1) + 1

        with pe.Fori(0, 2) as i:
            for c in range(2):
                steps(s0 + 8 * c, 0, 8, c, H, r, e0 + 2 * (c - 1), i * 16, i * 4)
        turn_prep("up2", y)

        s0, e0, u0, r = 2 * FIRST_LOAD["mlp2"], FIRST_EVAC["mlp2"], UP0["mlp2"], prepped("up2")
        with pe.Fori(0, GROUPS2) as g:
            d, de, du = g * 64, g * 16, g * 4

            def ready(k):
                return a_ready, u0 + k // 2 + 1 + du

            steps(s0, 0, 2, 0, H, r, e0 - 2, d, de)
            for c in range(4):
                steps(s0 + 8 * c, 2, 8, c % 2, H, r, d=d)
                if c < 3:
                    steps(s0 + 8 * c + 8, 0, 2, (c + 1) % 2, H, r, e0 + 2 * c, d, de)
                else:
                    steps(s0 + 32, 0, 2, 0, A, ready, e0 + 6, d, de)
                turn_up(u0 + c, e0 + 2 * c + 2, d, du, de)
            for c in range(4):
                steps(s0 + 32 + 8 * c, 2 if c == 0 else 0, 8, c % 2, A, ready, e0 + 8 + 2 * (c - 1), d, de)

    ctx.close()


NAMES = ["x", "pre_mix_g", "w_in", "b_forget", "sinks", "grp_swa_g", "grp_fox_g", "w_out", "post_mix_g", "pre_ffn_g",
         "w_up", "conv_w", "conv_b", "w_down", "post_ffn_g", "c_2", "ctx_2", "c_ctx_2", "norm_attn_w_2", "norm_mlp_w_2",
         "w_ada_2", "b_ada_2", "w_in_2", "attn_sink_2", "pool_w_2", "pool_scale_2", "w_out_2", "w_mlp_up_2",
         "w_mlp_down_2", "final_norm_w_2"]


def kernel(**inputs):
    import concourse.bacc as bacc
    from concourse.bass_utils import run_bass_kernel_spmd

    nc = bacc.Bacc("TRN2", target_bir_lowering=False, num_devices=1)
    table, pool_table = constants()
    arrays, aps = {}, {}
    for name, value in [(n, inputs[n]) for n in NAMES] + [("table", table), ("pool_table", pool_table)]:
        value = np.ascontiguousarray(value)
        arrays["in_" + name] = value
        aps[name] = nc.dram_tensor("in_" + name, value.shape, mybir.dt.from_np(value.dtype), kind="ExternalInput").ap()
    aps["out"] = nc.dram_tensor("out", (1, TOK, D), F32, kind="ExternalOutput").ap()
    build(nc, aps)
    result = run_bass_kernel_spmd(nc, [arrays], core_ids=[0])
    return result.results[0]["out"]
```

```python
from contextlib import ExitStack

import numpy as np

import concourse.bass as bass
from concourse import mybir

F32 = mybir.dt.float32
F32R = mybir.dt.float32r
ALU = mybir.AluOpType
ACT = mybir.ActivationFunctionType
AX_X = mybir.AxisListType.X

P = 128
TOK = 256
NB = TOK // P
D = 2048
KT = D // P
DH = 64
SCALE = DH ** -0.5
EPS = 1e-6
N = 512
CK = N // P
LOADK = 4
STEPK = 2

HEADS = 16
W_IN1 = 4368
QA, KA, VA, QB, KB, VB, FB = 0, 1024, 1152, 1280, 2304, 3328, 4352
FF1 = 5632
GV = N // 2
CT1 = FF1 // P
CTS = 2 * CT1
UPS1 = (8, 8, 6)
W_IN2 = 2560
Q2, K2, V2, U2 = 0, 1024, 1280, 1536
KV2 = 4
FF2 = 8192
GROUPS2 = 4
WINDOWS = (2, 4, 8, 16)
PG = 256
ADA_HALF = 1024
ADA_ORDER = ((0, (0, 1)), (5, (0,)), (2, (0,)), (3, (0,)), (1, (1, 2)), (4, (0,)))
ADA_RUNS = ((0, 0, 32), (1, 0, 16), (1, 16, 16), (2, 0, 32), (4, 0, 16), (3, 0, 32), (4, 16, 16), (5, 0, 32))
ADA_BASE = [sum(r[2] for r in ADA_RUNS[:n]) for n in range(len(ADA_RUNS))]
ADA_END = [max(b + r[2] for b, r in zip(ADA_BASE, ADA_RUNS) if r[0] == q) for q in range(len(ADA_ORDER))]
NEG = -1e30

C_ID, C_TRI, C_ONE, C_ALI, C_CAU, C_MASK, C_COS, C_SIN, C_END = 0, 128, 256, 384, 768, 1152, 2176, 2304, 2432

PHASES = [("in1", 9, 4), ("out1", 4, 4), ("up1a", 8, 4), ("down1a", 4, 4), ("up1b", 8, 4), ("down1b", 4, 4),
          ("up1c", 6, 4), ("down1c", 4, 3), ("in2", 5, 4), ("out2", 4, 4), ("mlp2", 32, 4)]
FIRST_LOAD, FIRST_EVAC = {}, {}
_l = _e = 0
for _name, _n, _per in PHASES:
    FIRST_LOAD[_name], FIRST_EVAC[_name] = _l, _e
    _l += _n * _per
    _e += 2 * _n + (2 if _name == "in2" else 0)
LOADS = _l
STEPS = 2 * LOADS
UP0 = {"up1a": 0, "up1b": 8, "up1c": 16, "mlp2": 22}


def constants():
    t = np.zeros((P, C_END), np.float32)
    p = np.arange(P)[:, None]
    c = np.arange(TOK)[None, :]
    t[:, C_ID:C_ID + P] = p == c[:, :P]
    t[:, C_TRI:C_TRI + P] = p <= c[:, :P]
    t[:, C_ONE:C_ONE + P] = 1.0
    t[:, C_ALI:C_ALI + P] = np.where(c[:, :P] <= p, c[:, :P] - p, NEG)
    far = P + p - c
    t[:, C_ALI + P:C_ALI + 3 * P] = np.where((far >= 0) & (far < P), -far, NEG)
    t[:, C_CAU:C_CAU + P] = np.where(c[:, :P] <= p, 0.0, NEG)
    t[:, C_CAU + P:C_CAU + 3 * P] = np.where(far >= 0, 0.0, NEG)
    freq = (10000.0 ** (-np.arange(0, 32, 2, dtype=np.float32) / np.float32(32))).astype(np.float32)
    for b in range(NB):
        q = b * P + p
        t[:, C_MASK + b * N:C_MASK + b * N + TOK] = np.where(np.abs(q - c) <= 128, 0.0, NEG)
        for rc, pos in enumerate((q // 64, q % 64)):
            ang = (pos.astype(np.float32) * freq[None, :]).astype(np.float32)
            for half in range(2):
                at = b * DH + rc * 32 + half * 16
                t[:, C_COS + at:C_COS + at + 16] = np.cos(ang)
                t[:, C_SIN + at:C_SIN + at + 16] = np.sin(ang) * (-1.0 if half == 0 else 1.0)
    pool = np.zeros((TOK, len(WINDOWS), TOK), np.float32)
    s, q = np.arange(TOK)[:, None], np.arange(TOK)[None, :]
    for g, w in enumerate(WINDOWS):
        lo, hi = np.clip(q - w // 2, 0, TOK), np.clip(q - w // 2 + w, 0, TOK)
        pool[:, g, :] = ((s >= lo) & (s < hi)) / (hi - lo).astype(np.float32) - (s == q)
    return t, np.ascontiguousarray(pool.reshape(NB, P, len(WINDOWS) * TOK).transpose(1, 0, 2))


def build(nc, a):
    ctx = ExitStack()
    base = (nc.sbuf_base + 63) // 64 * 64
    top = [base]
    at = {}

    def region(name, size):
        at[name] = top[0]
        top[0] += size

    KB_ = 1024
    region("raw", 32 * KB_)
    region("whi", 16 * KB_)
    region("wlo", 16 * KB_)
    region("h", 32 * KB_)
    region("act", 32 * KB_)
    region("y", 16 * KB_)
    region("x", 16 * KB_)
    region("ada", 24 * KB_)
    region("tmp", 18 * KB_)
    region("small", nc.sbuf_usable_end - top[0])
    small_at = [at["small"]]

    def place(name, shape, where, off=0, dt=F32):
        return nc.alloc_sbuf_tensor_at(name, shape, dt, offset=at[where] + off)

    def small(name, shape):
        t = nc.alloc_sbuf_tensor_at(name, shape, F32, offset=small_at[0])
        size = 4
        for n in shape[1:]:
            size *= n
        small_at[0] += (size + 31) // 32 * 32
        assert small_at[0] <= nc.sbuf_usable_end
        return t

    raw = place("raw", [P, 4, LOADK, N], "raw")
    w_hi = place("w_hi", [P, 4, STEPK, N], "whi", dt=F32R)
    w_lo = place("w_lo", [P, 4, STEPK, N], "wlo", dt=F32R)
    h_hi = place("h_hi", [P, KT, TOK], "h", dt=F32R)
    h_lo = place("h_lo", [P, KT, TOK], "h", 16 * KB_, F32R)
    a_hi = place("a_hi", [P, KT, TOK], "act", dt=F32R)
    a_lo = place("a_lo", [P, KT, TOK], "act", 16 * KB_, F32R)
    y = place("y", [P, NB, D], "y")
    x = place("x", [P, NB, D], "x")
    o1 = place("o1", [P, NB, D], "x")
    ada_w = place("ada_w", [P, 2, ADA_HALF], "ada")
    ada_acc = place("ada_acc", [P, 2, 2, ADA_HALF], "ada", 8 * KB_)
    ada_third = place("ada_third", [P, 2, ADA_HALF], "tmp", 10 * KB_)
    u_buf = place("u_buf", [P, NB, N], "tmp")
    conv = place("conv", [P, CK, TOK], "tmp", 4 * KB_)
    prod = place("prod", [P, 2, TOK], "tmp", 8 * KB_)
    row = place("row", [P, D], "tmp", 10 * KB_)
    p1 = place("p1", [P, NB, W_IN1], "act")
    sm1 = place("sm1", [P, 4, 3 * P], "y", 4 * KB_)
    pt1 = place("pt1", [P, 4, 3 * P], "y", 10 * KB_)
    slope_id = place("slope_id", [P, HEADS, P], "tmp")
    junk1 = place("junk1", [P, N], "tmp", 15 * KB_)
    assert 2 * W_IN1 * 4 <= (32 + 4) * KB_
    qk1 = place("qk1", [P, 26, TOK], "h")
    tab1 = place("tab1", [P, C_MASK - C_TRI], "h", 26 * KB_)
    cT = place("cT", [P, 3 * P], "h", 30 * KB_)
    TRI, ALI, CAU = 0, C_ALI - C_TRI, C_CAU - C_TRI
    slopes = 2.0 ** (-8.0 * np.arange(1, HEADS + 1) / HEADS)
    p2 = place("p2", [P, NB, W_IN2], "ada")
    c2 = place("c2", [P, NB, N], "ada", 20 * KB_)
    q2t = place("q2t", [P, 8, TOK], "y", 8 * KB_)
    k2t = place("k2t", [P, KV2, 2 * TOK], "act", 8 * KB_)
    sm2 = place("sm2", [P, 4, N], "act", 16 * KB_)
    o2 = place("o2", [P, NB, 1024], "y")
    pooled = place("pooled", [P, 8, TOK], "act")
    pool_a = place("pool_a", [P, NB, 4, TOK], "h")
    pool_w = place("pool_w", [P, 4, 2, PG], "h", 16 * KB_)
    pt2 = place("pt2", [P, 4, N], "tmp")
    tab2 = place("tab2", [P, C_END - C_MASK], "tmp", 8 * KB_)
    rot = place("rot", [P, 20, DH], "tmp", 13 * KB_)
    MASK2, COS2, SIN2 = 0, C_COS - C_MASK, C_SIN - C_MASK
    dup1 = place("dup1", [P, NB, 2, 2, DH], "tmp", 12 * KB_)
    dup2 = place("dup2", [P, 2 * NB, KV2, 2, DH], "tmp")
    final_row = place("final_row", [P, D], "ada")
    junk = place("junk", [P, N], "tmp", 8 * KB_)
    stage = place("stage", [P, 6, P], "y", 4 * KB_)

    ident = small("ident", [P, P])
    gains = small("gains", [P, 120])
    convw = small("convw", [P, 4, CTS])
    bada = small("bada", [P, 96])
    adac = small("adac", [P, 8, KT])
    silu = small("silu", [P, 2, KT])
    comb = small("comb", [P, KT])
    ones_col = small("ones_col", [P, 1])
    ones_again = small("ones_again", [P, 1])
    ssq = small("ssq", [P, 8])
    rstd = small("rstd", [P, 4])
    rstdx = small("rstdx", [P, NB])
    sq = small("sq", [P, NB, 4])
    mx = small("mx", [P, 4, 8])
    nm = small("nm", [P, 4, 8])
    rs = small("rs", [P, 4, 8])
    es = small("es", [P, 4, 8])
    sink1 = small("sink1", [P, HEADS])
    sink2 = small("sink2", [P, HEADS])
    nsink = small("nsink", [P, 2, HEADS])
    bforget = small("bforget", [P, HEADS])
    z = small("z", [P, NB, HEADS])
    lf = small("lf", [P, NB, HEADS])
    ct8 = small("ct8", [P, NB, HEADS])
    grow = small("grow", [16, 2, P])

    G = ctx.enter_context(nc.psum_tensor("G", [P, 4, N], F32))
    T = ctx.enter_context(nc.psum_tensor("T", [P, 4, N], F32))

    def sem(name):
        return ctx.enter_context(nc.semaphore(name))

    x_in = [sem(f"x_in{g}") for g in range(4)]
    table_in, vec_in, vec2_in, misc_in = sem("table_in"), sem("vec_in"), sem("vec2_in"), sem("misc_in")
    raw_full = [sem(f"raw_full{i}") for i in range(4)]
    hi_ready, lo_ready, step_done = sem("hi_ready"), sem("lo_ready"), sem("step_done")
    bank_evac = sem("bank_evac")
    turned, up_read = sem("turned"), sem("up_read")
    base_ready, tap1, gelu_done, conv_used, a_first, a_ready = (
        sem("base_ready"), sem("tap1"), sem("gelu_done"), sem("conv_used"), sem("a_first"), sem("a_ready"))
    vec_turned, vec2_turned, cols_ready, cols2_ready, silu_e = (
        sem("vec_turned"), sem("vec2_turned"), sem("cols_ready"), sem("cols2_ready"), sem("silu_e"))
    ada_full = [sem("ada_full0"), sem("ada_full1")]
    ada_used, ada_summed, ada_col, ada_zero = sem("ada_used"), sem("ada_summed"), sem("ada_col"), sem("ada_zero")
    squared, mean_ready, root_ready, rstd_ready = sem("squared"), sem("mean_ready"), sem("root_ready"), sem("rstd_ready")
    xn_act, xn_dve, prep_turned, tmp_act, tmp_dve, prep_hi, h_ready = (
        sem("xn_act"), sem("xn_dve"), sem("prep_turned"), sem("tmp_act"), sem("tmp_dve"), sem("prep_hi"), sem("h_ready"))
    x_new = sem("x_new")
    vchain = sem("vchain")
    row_full, x_again, ctx_in, tab1_in, tab2_in, pool_in, final_in = (
        sem("row_full"), sem("x_again"), sem("ctx_in"), sem("tab1_in"), sem("tab2_in"), sem("pool_in"), sem("final_in"))
    y_zero, s_max = sem("y_zero"), sem("s_max")
    z_ready, e_ready, e1_ready, l_ready, lf_ready, c_done, c_ready = (
        sem("z_ready"), sem("e_ready"), sem("e1_ready"), sem("l_ready"), sem("lf_ready"), sem("c_done"), sem("c_ready"))
    slope_ready = sem("slope_ready")
    qk_turned, qk_act, qk_dve = sem("qk_turned"), sem("qk_act"), sem("qk_dve")
    s_ready, es_in, nm_ready, es_ready, p_ready, pt_turned, pt_ready, pt_used, o_evac = (
        sem("s_ready"), sem("es_in"), sem("nm_ready"), sem("es_ready"), sem("p_ready"), sem("pt_turned"),
        sem("pt_ready"), sem("pt_used"), sem("o_evac"))
    dup_ready, rope_done, pooled_mm, pooled_ev, mixed_mm, mixed_hi, mixed_lo = (
        sem("dup_ready"), sem("rope_done"), sem("pooled_mm"), sem("pooled_ev"), sem("mixed_mm"), sem("mixed_hi"), sem("mixed_lo"))
    g_turned, g_copied, g_stored = sem("g_turned"), sem("g_copied"), sem("g_stored")
    out_ready, out_stored = sem("out_ready"), sem("out_stored")

    ada_rows = nc.dram_tensor("ada_rows", (2, D), F32, kind="Internal").ap()

    def tiles(w):
        return w.rearrange("(t p) n -> p t n", p=P)

    w_in1, w_out1, w_down1 = tiles(a["w_in"][0]), tiles(a["w_out"][0]), tiles(a["w_down"][0])
    w_up1 = a["w_up"][0].rearrange("(t p) (two f) -> p t two f", p=P, two=2)
    w_in2, w_out2 = tiles(a["w_in_2"][0]), tiles(a["w_out_2"][0])
    w_up2, w_down2 = tiles(a["w_mlp_up_2"][0]), tiles(a["w_mlp_down_2"][0])
    w_ada = tiles(a["w_ada_2"][0])

    def tokens(t):
        return t[0].rearrange("(b p) n -> p b n", p=P)

    C_C, C_CTX, PRE_MIX, GRP, PRE_FFN, NORM_A, NORM_M, POOL_S = [16 * i for i in range(8)]
    PREP = {"in1": (0, 4), "out1": (4, 4), "up1": (8, 4), "in2": (12, 4), "ctx": (16, 4), "out2": (20, 2), "up2": (22, 4)}
    NORMED = {"out1": 0, "in2": 4, "ctx": 8, "up2": 12}
    X_NEW = {"up1": 0, "in2": 4, "out2": 8, "final": 12}
    STAT = {"in1": 0, "out1": 1, "y1": 2, "up1": 3, "y2": 4, "in2": 5, "ctx": 6, "up2": 7, "final": 8}
    SQUARED = {"in1": 8, "out1": 16, "y1": 24, "up1": 32, "y2": 40, "in2": 48, "ctx": 56, "up2": 64, "final": 72}

    def pipeline(n, pre, gain, fin):
        for t in range(n + 2):
            if t < n and pre:
                pre(t)
            if 1 <= t <= n:
                gain(t - 1)
            if t >= 2:
                fin(t - 2)

    def twice(src, n):
        return src.rearrange("p (g d) -> p g d", d=DH).unsqueeze(2).broadcast_to([P, n, 2, DH])

    def accs(q):
        return [ada_third[:] if i == 2 else ada_acc[:, i] for i in ADA_ORDER[q][1]]

    def tt(pair):
        return T[:, 2 * pair:2 * pair + 2, :].rearrange("p a (j n) -> p (a j) n", n=TOK)

    block = ctx.enter_context(nc.Block())

    @block.sync
    def _(sp):
        for g in range(4):
            if g == 1:
                sp.wait_ge(vec_in, 16 * 9)
            sp.dma_start(x[:, :, g * N:g * N + N], tokens(a["x"])[:, :, g * N:g * N + N]).then_inc(x_in[g], 16)

        def load(l, src, d=0):
            if l >= 4:
                sp.wait_ge(lo_ready, 2 * l - 6 + 2 * d)
            for k in range(2):
                if len(src.shape) == 4:
                    dst, part = raw[:, l % 4, :, GV * k:GV * k + GV], src[:, :, k, :]
                else:
                    rows = slice(STEPK * k, STEPK * k + STEPK)
                    dst, part = raw[:, l % 4, rows, 0:src.shape[2]], src[:, rows, :]
                sp.dma_start(dst, part).then_inc(raw_full[l % 4], 16)

        def chunk(l, w, col, d=0, width=N, t0=0, loads=4):
            for k in range(loads):
                load(l + k, w[:, bass.ds(t0 + LOADK * k, LOADK), bass.ds(col, width)], d)

        def up_chunk(l, c, d=0):
            for k in range(4):
                load(l + k, w_up1[:, LOADK * k:LOADK * k + LOADK, :, bass.ds(c * GV, GV)], d)

        l0 = FIRST_LOAD["in1"]
        chunk(l0, w_in1, 0)
        with sp.Fori(0, 7) as i:
            chunk(l0 + 4, w_in1, i * N + N, i * 4)
        chunk(l0 + 32, w_in1, 8 * N, width=W_IN1 - 8 * N)
        l0 = FIRST_LOAD["out1"]
        with sp.Fori(0, 4) as i:
            chunk(l0, w_out1, i * N, i * 4)
        c0 = 0
        for g, n in zip("abc", UPS1):
            l0 = FIRST_LOAD["up1" + g]
            with sp.Fori(0, n) as i:
                up_chunk(l0, i + c0, i * 4)
            l0 = FIRST_LOAD["down1" + g]
            if n == 8:
                with sp.Fori(0, 4) as i:
                    chunk(l0, w_down1, i * N, i * 4, t0=2 * c0)
            else:
                for c in range(4):
                    chunk(l0 + 3 * c, w_down1, c * N, t0=2 * c0, loads=3)
            c0 += n
        l0 = FIRST_LOAD["in2"]
        for k, col in enumerate((0, N, K2, U2, U2 + N)):
            chunk(l0 + 4 * k, w_in2, col)
        l0 = FIRST_LOAD["out2"]
        with sp.Fori(0, 4) as i:
            chunk(l0, w_out2, i * N, i * 4)
        l0 = FIRST_LOAD["mlp2"]
        with sp.Fori(0, GROUPS2) as g:
            for c in range(4):
                chunk(l0 + 4 * c, w_up2, g * (4 * N) + c * N, g * 32)
            for c in range(4):
                for k in range(4):
                    load(l0 + 16 + 4 * c + k,
                         w_down2[:, bass.ds(g * KT + LOADK * k, LOADK), c * N:c * N + N], g * 32)
        for g in range(4):
            sp.wait_ge(out_ready, g + 1)
            sp.dma_start(tokens(a["out"])[:, :, g * N:g * N + N], y[:, :, g * N:g * N + N]).then_inc(out_stored, 16)
        sp.wait_ge(out_stored, 16 * 4)

    @block.gpsimd
    def _(pool):
        for k in range(3):
            pool.dma_start(stage[0:CTS, 1 + k, :], a["conv_w"][0, k].rearrange("(t p) -> t p", p=P)).then_inc(vec2_in, 16)
        pool.dma_start(stage[0:CTS, 4, :], a["conv_b"][0].rearrange("(t p) -> t p", p=P)).then_inc(vec2_in, 16)
        pool.dma_start(stage[0:96, 5, :], a["b_ada_2"][0].rearrange("(t p) -> t p", p=P)).then_inc(vec2_in, 16)
        pool.wait_ge(x_in[3], 16)

        def ada(run):
            q, first, count = ADA_RUNS[run]
            part, n = ADA_ORDER[q][0], ADA_BASE[run]

            def tile(t, half, wait):
                if wait is not None:
                    pool.wait_ge(ada_used, wait)
                pool.dma_start(ada_w[:, half, :],
                               w_ada[:, bass.ds(t + first // 2, 1), part * D + half * ADA_HALF:part * D + (half + 1) * ADA_HALF]
                               .rearrange("p a n -> p (a n)")).then_inc(ada_full[half], 16)

            if run == 0:
                tile(0, 0, None)
                tile(0, 1, None)
                with pool.Fori(1, count // 2) as t:
                    tile(t, 0, t * 2 - 1)
                    tile(t, 1, t * 2)
            else:
                with pool.Fori(0, count // 2) as t:
                    tile(t, 0, t * 2 + (n - 1))
                    tile(t, 1, t * 2 + n)

        def load_row(src):
            pool.dma_start(row[:], src.broadcast_to([P, D])).then_inc(row_full, 16)

        ada(0)
        pool.wait_ge(bank_evac, FIRST_EVAC["out1"])
        pool.dma_start(tab1[:], a["table"][:, C_TRI:C_MASK]).then_inc(tab1_in, 16)
        ada(1)
        pool.wait_ge(o_evac, 8)
        pool.wait_ge(squared, SQUARED["out1"])
        load_row(a["post_mix_g"])
        ada(2)
        pool.wait_ge(prep_turned, PREP["out1"][0] + 4)
        pool.dma_start(x[:], tokens(a["x"])).then_inc(x_again, 16)
        pool.wait_ge(x_new, X_NEW["up1"] + 4)
        pool.memset(y[:], 0.0).then_inc(y_zero, 1)
        pool.memset(ada_third[:], 0.0).then_inc(y_zero, 1)
        for run in range(3, 7):
            ada(run)
        ada(7)
        pool.wait_ge(ada_col, 5)
        load_row(a["post_ffn_g"])
        pool.wait_ge(g_copied, 1)
        pool.dma_start(ada_rows.rearrange("r (t p) -> t r p", p=P), grow[:]).then_inc(g_stored, 16)
        pool.wait_ge(h_ready, PREP["in2"][0] + 4)
        pool.dma_start(y[:], tokens(a["ctx_2"])).then_inc(ctx_in, 16)
        pool.wait_ge(h_ready, PREP["ctx"][0] + 4)
        pool.dma_start(tab2[:], a["table"][:, C_MASK:C_END]).then_inc(tab2_in, 16)
        pool.wait_ge(bank_evac, FIRST_EVAC["out2"])
        pool.dma_start(pool_a[:], a["pool_table"].rearrange("p b (g t) -> p b g t", g=4)).then_inc(pool_in, 16)
        pool.dma_start(pool_w[:], a["pool_w_2"][0].rearrange("g (c p) d -> p g c d", p=P)).then_inc(pool_in, 16)
        pool.wait_ge(g_stored, 16)
        pool.wait_ge(o_evac, 12)
        pool.wait_ge(mixed_lo, 8)
        load_row(ada_rows[0:1, :])
        pool.dma_start(final_row[:], a["final_norm_w_2"].rearrange("(a n) -> a n", a=1).broadcast_to([P, D])).then_inc(final_in, 16)
        pool.wait_ge(bank_evac, FIRST_EVAC["mlp2"])
        load_row(ada_rows[1:2, :])
        pool.wait_ge(prep_turned, PREP["up2"][0] + 4)
        pool.memset(y[:], 0.0).then_inc(y_zero, 1)

    @block.scalar
    def _(act):
        act.dma_start(ident[:], a["table"][:, C_ID:C_ID + P]).then_inc(table_in, 16)
        rows = [a["c_2"][0], a["c_ctx_2"], a["pre_mix_g"][0], a["grp_swa_g"][0], a["grp_fox_g"][0], a["pre_ffn_g"][0],
                a["norm_attn_w_2"][0], a["norm_mlp_w_2"][0], a["pool_scale_2"][0]]
        r0 = 0
        for v in rows:
            n = v.shape[0] // P
            act.dma_start(stage[r0:r0 + n, 0, :], v.rearrange("(t p) -> t p", p=P)).then_inc(vec_in, 16)
            r0 += n
        assert r0 == 120
        act.dma_start(sink1[:], a["sinks"].broadcast_to([P, HEADS])).then_inc(misc_in, 16)
        act.dma_start(sink2[:], a["attn_sink_2"].broadcast_to([P, HEADS])).then_inc(misc_in, 16)
        act.dma_start(bforget[:], a["b_forget"].broadcast_to([P, HEADS])).then_inc(misc_in, 16)

        taken = [0]

        def squares(g, src, out=junk):
            for b in range(NB):
                if taken[0]:
                    act.wait_ge(squared, taken[0])
                act.activation(out[:], src(b), ACT.Square, accum_out=sq[:, b, g:g + 1]).then_inc(squared, 1)
                taken[0] += 1

        def root(name, w=NB):
            act.wait_ge(mean_ready, STAT[name] + 1)
            act.activation(ssq[:, 4:4 + w], ssq[:, 0:w], ACT.Sqrt).then_inc(root_ready, 1)

        def scale_rows(name, src, dst, r=lambda g: rstdx[:, 0:1]):
            def scale(g):
                act.activation(dst[:, 0, g * N:(g + 1) * N], src[:, 0, g * N:(g + 1) * N], ACT.Copy,
                               scale=r(g)).then_inc(xn_act, 1)
            act.wait_ge(rstd_ready, STAT[name] + 1)
            return scale

        def prep(name, gain, hi, shift=None, pre=None):
            n0, n = PREP[name]

            def scale(g):
                act.wait_ge(prep_turned, n0 + g + 1)
                if g >= 2:
                    act.wait_ge(h_ready, n0 + g - 1)
                for j in range(2):
                    k = 4 * g + j
                    out = (u_buf, conv)[g % 2][:].rearrange("p a b -> p (a b)")[:, TOK * j:TOK * j + TOK]
                    if gain is None:
                        ins = act.activation(out, tt(g % 2)[:, j, :], ACT.Copy)
                    elif shift is None:
                        ins = act.activation(out, tt(g % 2)[:, j, :], ACT.Copy, scale=gain[:, k:k + 1])
                    else:
                        ins = act.activation(out, tt(g % 2)[:, j, :], ACT.Identity, scale=gain[:, k:k + 1],
                                             bias=shift[:, k:k + 1])
                ins.then_inc(tmp_act, 1)

            def part(g):
                act.wait_ge(tmp_act, n0 + g + 1)
                act.wait_ge(tmp_dve, n0 + g + 1)
                tmp = (u_buf, conv)[g % 2][:].rearrange("p a b -> p (a b)")
                act.activation(hi[:, 4 * g:4 * g + 4, :].rearrange("p a b -> p (a b)"), tmp, ACT.Copy).then_inc(prep_hi, 1)

            pipeline(n, pre, scale, part)

        def hi(s, d=0):
            if s % 2 == 0:
                act.wait_ge(raw_full[s // 2 % 4], 32 * (s // 8 + 1) + d * 4)
            if s >= 4:
                act.wait_ge(step_done, s - 3 + d)
            act.activation(w_hi[:, s % 4], raw[:, s // 2 % 4, STEPK * (s % 2):STEPK * (s % 2) + STEPK, :],
                           ACT.Copy).then_inc(hi_ready, 1)

        def his(s, n, d=0):
            for k in range(n):
                if s + k < STEPS:
                    hi(s + k, d)

        def body(s, d=0, post=None, n=8):
            his(s + 3, 3, d)
            if post:
                post[0]()
            his(s + 6, 1, d)
            if post:
                post[1]()
            his(s + 7, n - 4, d)

        def evac(dst, parity, func=ACT.Copy, width=N, s=None, d=0, scaled=False):
            act.wait_ge(step_done, s + d)
            for b in range(NB):
                scale = rstdx[:, b:b + 1] if scaled else 1.0
                act.activation(dst(b), G[:, 2 * parity + b, 0:width], func, scale=scale).then_inc(bank_evac, 1)

        act.wait_ge(cols_ready, 1)
        act.activation(silu[:].rearrange("p a b -> p (a b)"), gains[:, 0:32], ACT.Exp, scale=-1.0).then_inc(silu_e, 1)

        def first_squares(g):
            if g == 3:
                his(0, 1)
            act.wait_ge(x_in[g], 16)
            squares(g, lambda b: x[:, b, g * N:g * N + N])

        prep("in1", gains[:, PRE_MIX:], h_hi, pre=first_squares)
        his(1, 2)
        root("in1")
        act.wait_ge(rstd_ready, STAT["in1"] + 1)

        s0 = 2 * FIRST_LOAD["in1"]
        with act.Fori(0, 4) as i:
            for c in range(2):
                body(s0 + 8 * c, i * 16)
                evac(lambda b: p1[:, b, bass.ds(i * (2 * N) + c * N, N)], c, s=s0 + 8 * c + 8, d=i * 16,
                     scaled=True)
        for h in range(HEADS):
            act.activation(slope_id[:, h, :], ident[:], ACT.Copy, scale=float(slopes[h] / SCALE)).then_inc(slope_ready, 1)
        body(s0 + 64)
        evac(lambda b: p1[:, b, 8 * N:W_IN1], 0, width=W_IN1 - 8 * N, s=s0 + 72, scaled=True)

        act.wait_ge(bank_evac, FIRST_EVAC["out1"])
        for b in range(NB):
            ins = act.activation(dup1[:, b], twice(p1[:, b, KA:KA + 2 * DH], 2), ACT.Copy)
        ins.then_inc(dup_ready, 1)
        act.wait_ge(z_ready, 1)
        act.activation(lf[:], z[:], ACT.Exp, scale=-1.0).then_inc(e_ready, 1)
        act.wait_ge(e1_ready, 1)
        act.activation(lf[:], lf[:], ACT.Ln).then_inc(l_ready, 1)
        for g in range(7):
            act.wait_ge(qk_turned, g + 1)
            act.activation(qk1[:, 4 * g:4 * g + 2, :], tt(g % 2)[:, 0:2, :], ACT.Copy).then_inc(qk_act, 1)

        def exps1(n):
            b, i = n // 4, n % 4
            act.wait_ge(nm_ready, n + 1)
            if n >= 4:
                act.wait_ge(pt_turned, n - 3)
            if i == 0 and b >= 4:
                act.wait_ge(o_evac, b - 3)
            act.activation(sm1[:, n % 4, 0:P], G[:, n % 4, 0:P], ACT.Exp, scale=SCALE,
                           bias=nm[:, b % 4, 2 * i:2 * i + 1], accum_out=rs[:, b % 4, 2 * i:2 * i + 1])
            act.activation(sm1[:, n % 4, P:3 * P], G[:, n % 4, P:3 * P], ACT.Exp, scale=SCALE,
                           bias=nm[:, b % 4, 2 * i + 1:2 * i + 2],
                           accum_out=rs[:, b % 4, 2 * i + 1:2 * i + 2]).then_inc(p_ready, 1)
            if i == 3 and b < 4:
                act.wait_ge(es_in, b + 1)
                act.activation(es[:, b, :], es[:, b, :], ACT.Exp).then_inc(es_ready, 1)

        exps1(0)
        exps1(1)
        for n in range(2 * HEADS):
            if n + 2 < 2 * HEADS:
                exps1(n + 2)
            act.wait_ge(pt_turned, n + 1)
            if n >= 4:
                act.wait_ge(pt_used, n - 3)
            act.activation(pt1[:, n % 4, :], T[:, n % 2, 0:3 * P], ACT.Copy).then_inc(pt_ready, 1)
            if n >= 14 and n % 8 == 6:
                g = n // 8 - 1
                act.wait_ge(o_evac, 2 * g + 2)
                squares(g, lambda k: o1[:, k, g * N:g * N + N], junk1)
        act.wait_ge(o_evac, 8)
        squares(3, lambda k: o1[:, k, 3 * N:4 * N], junk1)
        root("out1", 2 * NB)
        prep("out1", gains[:, GRP:], h_hi, pre=scale_rows("out1", o1, o1, lambda g: rstd[:, g // 2:g // 2 + 1]))

        s0 = 2 * FIRST_LOAD["out1"]
        for c in range(4):
            body(s0 + 8 * c)
            act.wait_ge(step_done, s0 + 8 * c + 8)
            squares(c, lambda b: G[:, 2 * (c % 2) + b, :])
        root("y1")

        def new_squares(name):
            def take(g):
                act.wait_ge(x_new, X_NEW[name] + g + 1)
                squares(g, lambda b: x[:, b, g * N:g * N + N])
            return take

        prep("up1", gains[:, PRE_FFN:], h_hi, pre=new_squares("up1"))
        root("up1")
        act.wait_ge(rstd_ready, STAT["up1"] + 1)

        def up_evac(c, e, d, func):
            evac(lambda b: u_buf[:, b, :], c % 2, func, s=e, d=d, scaled=func == ACT.Copy)

        def post1(u, tile, du=0, dt=0):
            def taps():
                act.wait_ge(turned, u + 1 + du)
                if u >= 1:
                    act.wait_ge(conv_used, u + du)
                for j in range(CK):
                    t = (tile + j) if j < 2 else (CT1 + tile + j - 2)
                    ins = act.activation(conv[:, j, :], tt(0)[:, j, :], ACT.Identity,
                                         scale=convw[:, 2, bass.ds(t + dt, 1)], bias=convw[:, 3, bass.ds(t + dt, 1)])
                ins.then_inc(base_ready, 1)

            def gelu():
                act.wait_ge(up_read, u + 1 + du)
                act.activation(conv[:, 0:2, :], conv[:, 0:2, :], ACT.Gelu_apprx_tanh).then_inc(gelu_done, 1)

            return taps, gelu

        tile = 0
        for g, n in zip("abc", UPS1):
            s0, u0 = 2 * FIRST_LOAD["up1" + g], UP0["up1" + g]
            body(s0)
            up_evac(0, s0 + 8, 0, ACT.Copy)
            body(s0 + 8, 0, post1(u0, tile))
            up_evac(1, s0 + 16, 0, ACT.Copy)
            with act.Fori(0, n // 2 - 1) as i:
                for c in range(2):
                    body(s0 + 16 + 8 * c, i * 16, post1(u0 + 1 + c, tile + 2 + 2 * c, i * 2, i * 4))
                    up_evac(c, s0 + 24 + 8 * c, i * 16, ACT.Copy)
            tile += 2 * n
            s0, per = 2 * FIRST_LOAD["down1" + g], 8 if n == 8 else 6
            body(s0, 0, post1(u0 + n - 1, tile - 2), per)
            for c in range(1, 4):
                body(s0 + per * c, n=per)
                if n == 6:
                    act.wait_ge(bank_evac, FIRST_EVAC["down1c"] + 2 * c)
                    squares(c - 1, lambda b: y[:, b, (c - 1) * N:c * N])
        act.wait_ge(bank_evac, FIRST_EVAC["in2"])
        squares(3, lambda b: y[:, b, 3 * N:4 * N])
        root("y2")
        for g in range(4):
            new_squares("in2")(g)
        root("in2")
        prep("in2", comb, h_hi, adac[:, 0, :], scale_rows("in2", x, y))

        s0 = 2 * FIRST_LOAD["in2"]

        def turned_qk(g):
            act.wait_ge(qk_turned, 7 + g + 1)
            dst = q2t[:, 4 * g:4 * g + 2, :] if g < 2 else k2t[:, 2 * (g - 2), :].rearrange("p (a n) -> p a n", a=2)
            act.activation(dst, tt((7 + g) % 2)[:, 0:2, :], ACT.Copy).then_inc(qk_act, 1)

        def turned_k():
            turned_qk(2)
            turned_qk(3)

        for k, col in enumerate((0, N, K2, U2, U2 + N)):
            body(s0 + 8 * k, post=(turned_k, lambda: None) if k == 4 else None)
            evac(lambda b: p2[:, b, col:col + N], (0, 1, 0, 0, 1)[k], s=s0 + 8 * k + 8)
            if k == 2:
                evac(lambda b: c2[:, b, :], 1, s=s0 + 8 * k + 8)
                act.wait_ge(bank_evac, FIRST_EVAC["in2"] + 8)
                for b in range(NB):
                    ins = act.activation(dup2[:, NB + b], twice(c2[:, b, 0:KV2 * DH], KV2), ACT.Copy)
                ins.then_inc(dup_ready, 1)
            if k == 3:
                turned_qk(0)
                turned_qk(1)
            if k == 0:
                act.wait_ge(ctx_in, 16)
                for g in range(4):
                    squares(g, lambda b: y[:, b, g * N:g * N + N])
            if k == 1:
                root("ctx")
                prep("ctx", comb, a_hi, adac[:, 6, :], scale_rows("ctx", y, y, lambda g: rstd[:, 0:1]))

        def exps2(m):
            n, b, c = 32 + m, m // 8, m % 8
            act.wait_ge(nm_ready, n + 1)
            act.wait_ge(pt_turned, n - 3)
            act.activation(sm2[:, m % 4, :], G[:, m % 4, :], ACT.Exp, scale=SCALE, bias=nm[:, b, c:c + 1],
                           accum_out=rs[:, b, c:c + 1]).then_inc(p_ready, 1)
            if c == 7:
                act.wait_ge(es_in, 4 + b + 1)
                act.activation(es[:, b, :], es[:, b, :], ACT.Exp).then_inc(es_ready, 1)

        exps2(0)
        exps2(1)
        for m in range(2 * HEADS):
            if m + 2 < 2 * HEADS:
                exps2(m + 2)
            act.wait_ge(pt_turned, 32 + m + 1)
            act.wait_ge(pt_used, 32 + m - 3)
            act.activation(pt2[:, m % 4, :], T[:, m % 2, :], ACT.Copy).then_inc(pt_ready, 1)
        for g in range(4):
            act.wait_ge(pooled_mm, g + 1)
            act.activation(pooled[:, 2 * g:2 * g + 2, :], G[:, g, :].rearrange("p (a n) -> p a n", a=2),
                           ACT.Copy).then_inc(pooled_ev, 1)
        prep("out2", None, h_hi)

        s0 = 2 * FIRST_LOAD["out2"]
        for c in range(4):
            body(s0 + 8 * c)
            if c:
                new_squares("out2")(c - 1)
        new_squares("out2")(3)
        root("up2")
        prep("up2", comb, h_hi, adac[:, 3, :], scale_rows("up2", x, y))

        s0, u0 = 2 * FIRST_LOAD["mlp2"], UP0["mlp2"]

        def post2(u, du):
            def square():
                act.wait_ge(turned, u + 1 + du)
                act.wait_ge(a_ready, u + du)
                act.activation(conv[:], tt(0), ACT.Square).then_inc(up_read, 1)

            return square, lambda: None

        def group2(s, u, d, du, last=False):
            for c in range(4):
                body(s + 8 * c, d, post2(u + c - 1, du) if c else None)
                up_evac(c, s + 8 * c + 8, d, ACT.Relu)
            for c in range(4):
                body(s + 32 + 8 * c, d, None if c else post2(u + 3, du))
                if last and c:
                    new_squares("final")(c - 1)
            if last:
                new_squares("final")(3)
                root("final")

        with act.Fori(0, GROUPS2 - 1) as g:
            group2(s0, u0, g * 64, g * 4)
        group2(s0 + 64 * (GROUPS2 - 1), u0 + 4 * (GROUPS2 - 1), 0, 0, True)

    @block.vector
    def _(dve):
        chain = [0]

        def link(ins):
            chain[0] += 1
            ins.then_inc(vchain, 1)
            dve.wait_ge(vchain, chain[0])

        def lo(s, d=0):
            if s >= STEPS:
                return
            dve.wait_ge(hi_ready, s + 1 + d)
            dve.tensor_tensor(w_lo[:, s % 4], raw[:, s // 2 % 4, STEPK * (s % 2):STEPK * (s % 2) + STEPK, :],
                              w_hi[:, s % 4].bitcast(F32), ALU.subtract).then_inc(lo_ready, 1)

        def los(s, n, d=0):
            for k in range(n):
                lo(s + k, d)

        def ada_op(run, k, d=0, dt=0):
            q, first, _ = ADA_RUNS[run]
            half, n = k % 2, ADA_BASE[run] + k
            dve.wait_ge(ada_full[half], 16 * (n // 2 + 1) + dt * 16)
            if n:
                dve.wait_ge(ada_used, n + d)
            for c, acc in enumerate(accs(q)):
                ins = dve.scalar_tensor_tensor(out=acc[:, half, :], in0=ada_w[:, half, :],
                                               scalar=silu[:, c, bass.ds(dt + (first + k) // 2, 1)],
                                               in1=acc[:, half, :], op0=ALU.mult, op1=ALU.add)
            ins.then_inc(ada_used, 1)

        def ada_zeros():
            dve.memset(ada_acc[:], 0.0).then_inc(ada_zero, 1)

        def ada_finish(q):
            dve.wait_ge(ada_summed, q + 1)
            part, bufs = ADA_ORDER[q]
            dve.tensor_tensor(adac[:, part, :], T[:, 3, 0:KT], bada[:, KT * part:KT * part + KT], ALU.add)
            if len(bufs) == 2:
                dve.tensor_tensor(adac[:, 6 + part, :], T[:, 3, KT:2 * KT], bada[:, KT * part:KT * part + KT], ALU.add)
            dve.memset(ones_again[:], 1.0).then_inc(ada_col, 1)
            if q in (1, 2, 3):
                ada_clear(q)
            dve.wait_ge(ada_col, q + 1)

        def ada_clear(q):
            dve.memset(ada_acc[:, 0:min(len(ADA_ORDER[q][1]), 2)], 0.0).then_inc(ada_zero, 1)
            dve.wait_ge(ada_zero, q + 2)

        def root(name, dst, width=D, w=NB):
            k = STAT[name]
            dve.wait_ge(squared, SQUARED[name])
            link(dve.tensor_reduce(ssq[:, 0:w], sq[:].rearrange("p b (h c) -> p (b h) c", c=NB * 4 // w), AX_X, ALU.add))
            dve.tensor_scalar(ssq[:, 0:w], ssq[:, 0:w], 1.0 / width, EPS, ALU.mult, ALU.add).then_inc(mean_ready, 1)
            dve.wait_ge(root_ready, k + 1)
            dve.reciprocal(dst[:, 0:w], ssq[:, 4:4 + w]).then_inc(rstd_ready, 1)
            dve.wait_ge(rstd_ready, k + 1)

        def scale_rows(src, dst, r=lambda g: rstdx[:, 1:2]):
            def scale(g):
                dve.tensor_scalar(dst[:, 1, g * N:(g + 1) * N], src[:, 1, g * N:(g + 1) * N], r(g), None,
                                  ALU.mult).then_inc(xn_dve, 1)
            return scale

        def prep(name, gain, hi, lo_out, shift=None, pre=None):
            n0, n = PREP[name]

            def scale(g):
                dve.wait_ge(prep_turned, n0 + g + 1)
                if g >= 2:
                    dve.wait_ge(h_ready, n0 + g - 1)
                for j in range(2, 4):
                    k = 4 * g + j
                    out = (u_buf, conv)[g % 2][:].rearrange("p a b -> p (a b)")[:, TOK * j:TOK * j + TOK]
                    if gain is None:
                        ins = dve.tensor_copy(out, tt(g % 2)[:, j, :])
                    elif shift is None:
                        ins = dve.tensor_scalar(out, tt(g % 2)[:, j, :], gain[:, k:k + 1], None, ALU.mult)
                    else:
                        ins = dve.tensor_scalar(out, tt(g % 2)[:, j, :], gain[:, k:k + 1], shift[:, k:k + 1],
                                                ALU.mult, ALU.add)
                ins.then_inc(tmp_dve, 1)

            def rest(g):
                dve.wait_ge(prep_hi, n0 + g + 1)
                tmp = (u_buf, conv)[g % 2][:].rearrange("p a b -> p (a b)")
                dve.tensor_tensor(lo_out[:, 4 * g:4 * g + 4, :].rearrange("p a b -> p (a b)"), tmp,
                                  hi[:, 4 * g:4 * g + 4, :].rearrange("p a b -> p (a b)").bitcast(F32),
                                  ALU.subtract).then_inc(h_ready, 1)

            pipeline(n, pre, scale, rest)

        dve.memset(ones_col[:], 1.0)
        ada_zeros()
        dve.wait_ge(vec_turned, 1)
        dve.tensor_copy(gains[:], T[:, 3, 0:120]).then_inc(cols_ready, 1)
        dve.wait_ge(cols_ready, 1)
        prep("in1", gains[:, PRE_MIX:], h_hi, h_lo, pre=lambda g: lo(0) if g == 3 else None)
        los(1, 2)
        root("in1", rstdx)
        dve.wait_ge(silu_e, 1)
        flat = silu[:].rearrange("p a b -> p (a b)")
        link(dve.tensor_scalar(flat, flat, 1.0, None, ALU.add))
        link(dve.reciprocal(flat, flat))
        link(dve.tensor_tensor(flat, flat, gains[:, 0:32], ALU.mult))
        dve.wait_ge(ada_zero, 1)

        s0 = 2 * FIRST_LOAD["in1"]
        with dve.Fori(0, 8) as i:
            for k in range(8):
                lo(s0 + 3 + k, i * 8)
                if k % 2 == 1:
                    half = (k // 2) % 2
                    dve.wait_ge(ada_full[half], 16 + i * 32 + 16 * (k // 4))
                    for c in range(2):
                        ins = dve.scalar_tensor_tensor(out=ada_acc[:, c, half, :], in0=ada_w[:, half, :],
                                                       scalar=silu[:, c, bass.ds(i * 2 + k // 4, 1)],
                                                       in1=ada_acc[:, c, half, :], op0=ALU.mult, op1=ALU.add)
                    ins.then_inc(ada_used, 1)
                    dve.wait_ge(ada_used, i * 4 + k // 2 + 1)
        los(s0 + 67, 8)
        dve.wait_ge(vec2_turned, 1)
        dve.tensor_copy(convw[:].rearrange("p a b -> p (a b)"), T[:, 1, 0:4 * CTS])
        dve.tensor_copy(bada[:], T[:, 2, 0:96]).then_inc(cols2_ready, 1)
        dve.wait_ge(cols2_ready, 1)
        ada_finish(0)

        dve.wait_ge(bank_evac, FIRST_EVAC["out1"])
        dve.wait_ge(misc_in, 48)
        for n, sink in enumerate((sink1, sink2)):
            dve.tensor_scalar(nsink[:, n, :], sink[:], -1.0, None, ALU.mult)
        for b in range(NB):
            ins = dve.tensor_tensor(ct8[:, b, :], p1[:, b, FB:FB + HEADS], bforget[:], ALU.add)
        link(ins)
        link(dve.tensor_scalar(z[:], ct8[:], -1.0, None, ALU.mult))
        dve.tensor_tensor(z[:], z[:], ct8[:], ALU.max).then_inc(z_ready, 1)
        link(dve.tensor_scalar(ct8[:], ct8[:], 0.0, None, ALU.min))
        dve.wait_ge(e_ready, 1)
        dve.tensor_scalar(lf[:], lf[:], 1.0, None, ALU.add).then_inc(e1_ready, 1)
        dve.wait_ge(l_ready, 1)
        dve.tensor_tensor(lf[:], ct8[:], lf[:], ALU.subtract).then_inc(lf_ready, 1)
        def turned1(g):
            dve.wait_ge(qk_turned, g + 1)
            dve.tensor_copy(qk1[:, 4 * g + 2:4 * g + 4, :], tt(g % 2)[:, 2:4, :]).then_inc(qk_dve, 1)

        turned1(0)
        turned1(1)
        dve.wait_ge(c_done, 1)
        link(dve.memset(cT[:], 0.0))
        dve.tensor_scalar(cT[0:HEADS, 0:P], G[0:HEADS, 1, 0:P], -1 / SCALE, None, ALU.mult)
        dve.tensor_scalar(cT[0:HEADS, P:3 * P], G[0:HEADS, 1, 0:TOK], -1 / SCALE, None, ALU.mult).then_inc(c_ready, 1)
        for g in range(2, 6):
            turned1(g)
        ada_clear(0)

        def shift(n, slot, cols, nsinks):
            dve.wait_ge(s_max, n + 1)
            dst, src = nm[:, slot, cols], mx[:, slot, cols]
            if nsinks is None:
                dve.tensor_scalar(dst, src, -SCALE, None, ALU.mult).then_inc(nm_ready, 1)
            else:
                dve.tensor_scalar(dst, src, -SCALE, nsinks, ALU.mult, ALU.min).then_inc(nm_ready, 1)

        def sinks(n, slot, sink):
            dve.wait_ge(nm_ready, n + 1)
            dve.tensor_tensor(es[:, slot, :].rearrange("p (h b) -> p h b", b=NB), nm[:, slot, :].rearrange("p (h b) -> p h b", b=NB),
                              sink.unsqueeze(2).broadcast_to([P, 4, NB]), ALU.add).then_inc(es_in, 1)

        def outputs(b, used, exped, dst):
            dve.wait_ge(pt_used, used)
            r = rs[:, b % 4, :]
            if exped is not None:
                dve.wait_ge(es_ready, exped)
                link(dve.tensor_tensor(r, r, es[:, b % 4, :], ALU.add))
            link(dve.reciprocal(r, r))
            dve.tensor_tensor(dst.rearrange("p k (h d) -> p k h d", d=DH),
                              T[:, 2 + b % 2, :].rearrange("p (k h d) -> p k h d", k=NB, d=DH),
                              r.rearrange("p (h k) -> p k h", k=NB).unsqueeze(3).broadcast_to([P, NB, 4, DH]),
                              ALU.mult).then_inc(o_evac, 1)

        def outputs1(b):
            outputs(b, 4 * b + 4, b + 1 if b < 4 else None, o1[:, :, TOK * b:TOK * b + TOK])

        for n in range(2 * HEADS):
            b, i = n // 4, n % 4
            dve.wait_ge(s_ready, n + 1)
            dve.reduce_max(mx[:, b % 4, 2 * i:2 * i + 1], G[:, n % 4, 0:P], AX_X)
            dve.reduce_max(mx[:, b % 4, 2 * i + 1:2 * i + 2], G[:, n % 4, P:3 * P], AX_X).then_inc(s_max, 1)
            shift(n, b % 4, slice(2 * i, 2 * i + 2), nsink[:, 0, n:n + 1] if n < HEADS else None)
            if i == 3 and n < HEADS:
                sinks(n, b, sink1[:, n - 3:n + 1])
            if n % 2:
                ada_op(1, n // 2)
            if n >= 8 and i == 0:
                outputs1(b - 2)
        outputs1(6)
        outputs1(7)
        dve.wait_ge(o_evac, 8)
        root("out1", rstd, 1024, 2 * NB)
        prep("out1", gains[:, GRP:], h_hi, h_lo,
             pre=scale_rows(o1, o1, lambda g: rstd[:, 2 + g // 2:3 + g // 2]))

        s0 = 2 * FIRST_LOAD["out1"]
        dve.wait_ge(row_full, 16)
        for c in range(4):
            for k in range(8):
                lo(s0 + 8 * c + 3 + k)
                if k % 2:
                    ada_op(2, 4 * c + k // 2)
            dve.wait_ge(squared, SQUARED["out1"] + 2 * c + 2)
            for b in range(NB):
                dve.tensor_tensor(y[:, b, c * N:c * N + N], G[:, 2 * (c % 2) + b, :], row[:, c * N:c * N + N],
                                  ALU.mult).then_inc(bank_evac, 1)

        root("y1", rstd)
        dve.wait_ge(x_again, 16)

        def residual(name):
            def add(g):
                for b in range(NB):
                    ins = dve.scalar_tensor_tensor(out=x[:, b, g * N:g * N + N], in0=y[:, b, g * N:g * N + N],
                                                   scalar=rstd[:, b:b + 1], in1=x[:, b, g * N:g * N + N],
                                                   op0=ALU.mult, op1=ALU.add)
                ins.then_inc(x_new, 1)
            return add

        prep("up1", gains[:, PRE_FFN:], h_hi, h_lo, pre=residual("up1"))
        root("up1", rstdx)

        def body(s, d=0, post=None, n=8, adas=()):
            adas = list(adas)
            for k in range(n):
                lo(s + 3 + k, d)
                if post and k == 2:
                    post[0]()
                elif post and k == 3:
                    post[1]()
                elif not post or k >= 4:
                    left = n - k if not post else n - max(k, 4)
                    for _ in range(-(-len(adas) // left)):
                        ada_op(*adas.pop(0))

        def post1(u, tile, a_tile, du=0, dt=0):
            def taps():
                dve.wait_ge(base_ready, u + 1 + du)
                for tap in (1, 0):
                    k = 2 - tap
                    for j in range(CK):
                        t = (tile + j) if j < 2 else (CT1 + tile + j - 2)
                        ins = dve.scalar_tensor_tensor(out=conv[:, j, k:TOK], in0=tt(0)[:, j, 0:TOK - k],
                                                       scalar=convw[:, tap, bass.ds(t + dt, 1)], in1=conv[:, j, k:TOK],
                                                       op0=ALU.mult, op1=ALU.add)
                    if tap:
                        ins.then_inc(tap1, 1)
                        dve.wait_ge(tap1, u + 1 + du)
                ins.then_inc(up_read, 1)

            def product():
                hi, lo_ = (t[:, bass.ds(a_tile + dt, 2), :] for t in (a_hi, a_lo))
                dve.wait_ge(gelu_done, u + 1 + du)
                dve.tensor_tensor(prod[:], conv[:, 0:2, :], conv[:, 2:4, :], ALU.mult).then_inc(conv_used, 1)
                dve.wait_ge(conv_used, u + 1 + du)
                dve.tensor_copy(hi, prod[:]).then_inc(a_first, 1)
                dve.wait_ge(a_first, u + 1 + du)
                dve.tensor_tensor(lo_, prod[:], hi.bitcast(F32), ALU.subtract).then_inc(a_ready, 1)

            return taps, product

        def down_evac(c, e, d=0):
            dve.wait_ge(step_done, e + d)
            for b in range(NB):
                dve.tensor_tensor(y[:, b, c * N:c * N + N], y[:, b, c * N:c * N + N], G[:, 2 * (c % 2) + b, :],
                                  ALU.add).then_inc(bank_evac, 1)

        def times_row(c):
            dve.wait_ge(squared, SQUARED["up1"] + 2 * c + 2)
            cols = slice(c * N, c * N + N)
            link(dve.tensor_tensor(y[:, :, cols], y[:, :, cols], row[:, cols].unsqueeze(1).broadcast_to([P, NB, N]),
                                   ALU.mult))

        tile = 0
        for g, n, run_up, run_down, fin_up, fin_down in (("a", 8, 3, 4, None, 2), ("b", 8, 5, 6, None, 3),
                                                         ("c", 6, 7, None, 4, 5)):
            s0, u0 = 2 * FIRST_LOAD["up1" + g], UP0["up1" + g]
            first, each = (4, 4) if n == 8 else (7, 5)
            if g == "a":
                los(s0 + 3, 2)
                ada_finish(1)
                body(s0 + 2, n=6, adas=[(run_up, k) for k in range(first)])
            else:
                body(s0, adas=[(run_up, k) for k in range(first)])
            if fin_up is not None:
                ada_finish(fin_up)
            if g == "a":
                dve.wait_ge(y_zero, 2)
            if n == 8:
                with dve.Fori(0, n - 1) as i:
                    body(s0 + 8, i * 8, post1(u0, tile, 0, i, i * 2),
                         adas=[(run_up, first + k, i * each, i * (each // 2)) for k in range(each)])
            else:
                for c in range(1, n):
                    body(s0 + 8 * c, 0, post1(u0 + c - 1, tile + 2 * c - 2, 2 * c - 2),
                         adas=[(run_up, first + each * (c - 1) + k) for k in range(each)])
            tile += 2 * n
            s0, per = 2 * FIRST_LOAD["down1" + g], 8 if n == 8 else 6
            for c in range(4):
                body(s0 + per * c, 0, post1(u0 + n - 1, tile - 2, 2 * n - 2) if c == 0 else None, per,
                     adas=[(run_down, 4 * c + k) for k in range(4)] if run_down is not None else ())
                down_evac(c, s0 + per * c + per)
                if c == 0:
                    ada_finish(fin_down)
                if n == 6 and c:
                    if c == 1:
                        dve.wait_ge(row_full, 32)
                    times_row(c - 1)
        times_row(3)
        root("y2", rstd)
        for g in range(4):
            residual("in2")(g)
        root("in2", rstdx)

        def combine(norm, part):
            link(dve.tensor_scalar(comb[:], adac[:, part, :], 1.0, None, ALU.add))
            link(dve.tensor_tensor(comb[:], comb[:], gains[:, norm:norm + KT], ALU.mult))

        dve.wait_ge(g_turned, 1)
        dve.tensor_copy(grow[:].rearrange("t r p -> t (r p)"), T[0:16, 3, 0:2 * P]).then_inc(g_copied, 1)
        combine(NORM_A, 1)
        prep("in2", comb, h_hi, h_lo, adac[:, 0, :], scale_rows(x, y))

        cos = tab2[:, COS2:COS2 + 2 * DH].rearrange("p (b d) -> p b d", b=NB)
        sin = tab2[:, SIN2:SIN2 + 2 * DH].rearrange("p (b r s d) -> p b r s d", b=NB, r=2, s=2)

        def rotate(b, first, heads, done):
            cols = slice(DH * first, DH * (first + heads))
            qk = p2[:, b, cols].rearrange("p (h d) -> p h d", d=DH)
            qk5 = p2[:, b, cols].rearrange("p (h r s d) -> p h r s d", r=2, s=2, d=16)
            rot5 = rot[:, 0:heads, :].rearrange("p h (r s d) -> p h r s d", r=2, s=2)
            for s in range(2):
                ins = dve.tensor_tensor(rot5[:, :, :, s, :], qk5[:, :, :, 1 - s, :],
                                        sin[:, b, :, s, :].unsqueeze(1).broadcast_to([P, heads, 2, 16]), ALU.mult)
            link(ins)
            link(dve.tensor_tensor(qk, qk, cos[:, b, :].unsqueeze(1).broadcast_to([P, heads, DH]), ALU.mult))
            dve.tensor_tensor(qk, qk, rot[:, 0:heads, :], ALU.add).then_inc(rope_done, 1)
            dve.wait_ge(rope_done, done)

        def turned_qk(g):
            dve.wait_ge(qk_turned, 7 + g + 1)
            dst = q2t[:, 4 * g + 2:4 * g + 4, :] if g < 2 else k2t[:, 2 * (g - 2) + 1, :].rearrange("p (a n) -> p a n", a=2)
            dve.tensor_copy(dst, tt((7 + g) % 2)[:, 2:4, :]).then_inc(qk_dve, 1)

        s0 = 2 * FIRST_LOAD["in2"]
        los(s0 + 3, 16)
        root("ctx", rstd)
        combine(NORM_A, 7)
        prep("ctx", comb, a_hi, a_lo, adac[:, 6, :], scale_rows(y, y, lambda g: rstd[:, 1:2]))
        los(s0 + 19, 9)
        dve.wait_ge(bank_evac, FIRST_EVAC["in2"] + 8)
        dve.wait_ge(tab2_in, 16)
        rotate(0, 0, HEADS + KV2, 1)
        los(s0 + 28, 3)
        rotate(1, 0, HEADS + KV2, 2)
        los(s0 + 31, 4)
        for b in range(NB):
            ins = dve.tensor_copy(dup2[:, b], twice(p2[:, b, K2:K2 + KV2 * DH], KV2))
        ins.then_inc(dup_ready, 1)
        turned_qk(0)
        turned_qk(1)
        los(s0 + 35, 3)
        turned_qk(2)
        turned_qk(3)
        los(s0 + 38, 5)


        def outputs2(b):
            outputs(b, 32 + 8 * b + 8, 4 + b + 1, o2[:, :, TOK * b:TOK * b + TOK])

        for m in range(2 * HEADS):
            n, b, c = 32 + m, m // 8, m % 8
            dve.wait_ge(s_ready, n + 1)
            dve.reduce_max(mx[:, b, c:c + 1], G[:, m % 4, :], AX_X).then_inc(s_max, 1)
            shift(n, b, slice(c, c + 1), nsink[:, 1, m // 2:m // 2 + 1])
            if c == 7:
                sinks(n, b, sink2[:, 4 * b:4 * b + 4])
            if m >= 12 and c == 4:
                outputs2(b - 1)
        outputs2(3)
        for j in range(8):
            dve.wait_ge(mixed_mm, j + 1)
            tmp = rot[:].rearrange("p h d -> p (h d)")[:, TOK * (j % 2):TOK * (j % 2) + TOK]
            link(dve.tensor_scalar(tmp, G[:, j % 4, 0:TOK], gains[:, POOL_S + j:POOL_S + j + 1], None, ALU.mult))
            dve.tensor_copy(h_hi[:, 8 + j, :], tmp).then_inc(mixed_hi, 1)
            dve.wait_ge(mixed_hi, j + 1)
            dve.tensor_tensor(h_lo[:, 8 + j, :], tmp, h_hi[:, 8 + j, :].bitcast(F32), ALU.subtract).then_inc(mixed_lo, 1)
        prep("out2", None, h_hi, h_lo)

        s0 = 2 * FIRST_LOAD["out2"]
        dve.wait_ge(row_full, 48)
        for c in range(4):
            los(s0 + 8 * c + 3, 8)
            cols = slice(c * N, c * N + N)
            dve.wait_ge(step_done, s0 + 8 * c + 8)
            for b in range(NB):
                dve.tensor_tensor(y[:, b, cols], G[:, 2 * (c % 2) + b, :], row[:, cols], ALU.mult).then_inc(bank_evac, 1)
            dve.wait_ge(bank_evac, FIRST_EVAC["out2"] + 2 * c + 2)
            dve.tensor_tensor(x[:, :, cols], x[:, :, cols], y[:, :, cols], ALU.add).then_inc(x_new, 1)
        dve.wait_ge(x_new, X_NEW["final"])
        root("up2", rstdx)
        combine(NORM_M, 4)
        prep("up2", comb, h_hi, h_lo, adac[:, 3, :], scale_rows(x, y))

        def post2(u, c, du):
            def split():
                dve.wait_ge(up_read, u + 1 + du)
                dve.tensor_copy(a_hi[:, 4 * c:4 * c + 4, :], conv[:]).then_inc(a_first, 1)
                dve.wait_ge(a_first, u + 1 + du)
                dve.tensor_tensor(a_lo[:, 4 * c:4 * c + 4, :], conv[:], a_hi[:, 4 * c:4 * c + 4, :].bitcast(F32),
                                  ALU.subtract).then_inc(a_ready, 1)

            return lambda: None, split

        def group2(s, u, d, du, last=False):
            for c in range(4):
                body(s + 8 * c, d, post2(u + c - 1, c - 1, du) if c else None)
            for c in range(4):
                body(s + 32 + 8 * c, d, None if c else post2(u + 3, 3, du))
                down_evac(c, s + 32 + 8 * c + 8, d)
                if last:
                    cols = slice(c * N, c * N + N)
                    dve.wait_ge(bank_evac, FIRST_EVAC["mlp2"] + 16 * GROUPS2 - 8 + 2 * c + 2)
                    link(dve.tensor_tensor(y[:, :, cols], y[:, :, cols],
                                           row[:, cols].unsqueeze(1).broadcast_to([P, NB, N]), ALU.mult))
                    dve.tensor_tensor(x[:, :, cols], x[:, :, cols], y[:, :, cols], ALU.add).then_inc(x_new, 1)

        s0, u0 = 2 * FIRST_LOAD["mlp2"], UP0["mlp2"]
        dve.wait_ge(y_zero, 3)
        with dve.Fori(0, GROUPS2 - 1) as g:
            group2(s0, u0, g * 64, g * 4)
        dve.wait_ge(row_full, 64)
        group2(s0 + 64 * (GROUPS2 - 1), u0 + 4 * (GROUPS2 - 1), 0, 0, True)

        root("final", rstdx)
        dve.wait_ge(final_in, 16)
        for g in range(4):
            cols = slice(g * N, g * N + N)
            for b in range(NB):
                ins = dve.scalar_tensor_tensor(out=y[:, b, cols], in0=x[:, b, cols], scalar=rstdx[:, b:b + 1],
                                               in1=final_row[:, cols], op0=ALU.mult, op1=ALU.mult)
            ins.then_inc(out_ready, 1)

    @block.tensor
    def _(pe):
        def step(s, parity, acts, kt, first, last, ready=None, d=0, width=N):
            pe.wait_ge(hi_ready, s + 1 + d)
            pe.wait_ge(lo_ready, s + 1 + d)
            if ready is not None:
                pe.wait_ge(*ready)
            for j in range(STEPK):
                wh, wl = w_hi[:, s % 4, j, 0:width], w_lo[:, s % 4, j, 0:width]
                for n, (hi, lo) in enumerate(acts):
                    for b in range(NB):
                        out = G[:, 2 * (parity if n == 0 else 1) + b, 0:width]
                        ah, al = hi[:, kt + j, b * P:b * P + P], lo[:, kt + j, b * P:b * P + P]
                        f, l = first and j == 0, last and j == STEPK - 1
                        pe.matmul(out, ah, wh, start=f, stop=False)
                        pe.matmul(out, ah, wl, start=False, stop=False)
                        mm = pe.matmul(out, al, wh, start=False, stop=l)
            mm.then_inc(step_done, 1)

        def steps(s, k0, k1, parity, acts, ready, e=None, d=0, de=0, per=8, width=N):
            if k0 == 0 and e is not None and not (isinstance(e, int) and e <= 0):
                pe.wait_ge(bank_evac, e + de)
            for k in range(k0, k1):
                step(s + k, parity, acts, STEPK * k, k == 0, k == per - 1, ready(k), d, width)

        def prepped(name):
            n0 = PREP[name][0]
            return lambda k: (h_ready, n0 + k // 2 + 1)

        H, A = [(h_hi, h_lo)], [(a_hi, a_lo)]

        def turn_prep(name, src, waits=()):
            n0, n = PREP[name]
            for g in range(n):
                if name in NORMED:
                    pe.wait_ge(xn_act, NORMED[name] + g + 1)
                    pe.wait_ge(xn_dve, NORMED[name] + g + 1)
                if name == "up1":
                    pe.wait_ge(x_new, X_NEW[name] + g + 1)
                if name == "in1":
                    pe.wait_ge(x_in[g], 16)
                if n0 + g >= 2:
                    pe.wait_ge(tmp_act, n0 + g - 1)
                    pe.wait_ge(tmp_dve, n0 + g - 1)
                for j in range(4):
                    for b in range(NB):
                        mm = pe.transpose(tt(g % 2)[:, j, b * P:b * P + P], src[:, b, (4 * g + j) * P:(4 * g + j + 1) * P],
                                          ident[:])
                mm.then_inc(prep_turned, 1)

        def ada_sum(q):
            pe.wait_ge(ada_used, ADA_END[q])
            if q >= 1:
                pe.wait_ge(ada_col, q)
            for c, acc in enumerate(accs(q)):
                for t in range(KT):
                    mm = pe.matmul(T[:, 3, KT * c + t:KT * c + t + 1], acc[:, t // 8, (t % 8) * P:(t % 8 + 1) * P], ones_col[:],
                                   start=True, stop=True)
            mm.then_inc(ada_summed, 1)

        pe.wait_ge(table_in, 16)
        pe.wait_ge(vec_in, 16 * 9)
        pe.transpose(T[:, 3, 0:120], stage[0:120, 0, :], ident[0:120, 0:120]).then_inc(vec_turned, 1)
        pe.wait_ge(cols_ready, 1)
        turn_prep("in1", x)

        s0, r = 2 * FIRST_LOAD["in1"], prepped("in1")
        steps(s0, 0, 8, 0, H, r)
        steps(s0 + 8, 0, 8, 1, H, r)
        with pe.Fori(0, 3) as i:
            for c in range(2):
                steps(s0 + 16 + 8 * c, 0, 8, c, H, r, 2 * (c + 1), i * 16, i * 4)
        steps(s0 + 64, 0, 8, 0, H, r, 14, width=W_IN1 - 8 * N)
        pe.wait_ge(vec2_in, 16 * 5)
        for k in range(4):
            pe.transpose(T[:, 1, k * CTS:(k + 1) * CTS], stage[0:CTS, 1 + k, :], ident[0:CTS, 0:CTS])
        pe.transpose(T[:, 2, 0:96], stage[0:96, 5, :], ident[0:96, 0:96]).then_inc(vec2_turned, 1)
        ada_sum(0)

        pe.wait_ge(ada_col, 1)
        QK = ([QA + P * t for t in range(8)] + [-1, -2] + [QB + P * t for t in range(8)]
              + [KB + P * t for t in range(8)])

        for g in range(7):
            if g == 2:
                pe.wait_ge(tab1_in, 16)
                pe.wait_ge(lf_ready, 1)
                pe.matmul(G[0:HEADS, 1, 0:TOK], lf[:, 0, :], tab1[:, TRI:TRI + TOK], start=True, stop=False)
                pe.matmul(G[0:HEADS, 1, P:TOK], lf[:, 1, :], tab1[:, TRI:TRI + P], start=False, stop=True).then_inc(c_done, 1)
                pe.wait_ge(dup_ready, 1)
            if g >= 2:
                pe.wait_ge(qk_act, g - 1)
                pe.wait_ge(qk_dve, g - 1)
            for j, col in enumerate(QK[4 * g:4 * g + 4]):
                for b in range(NB):
                    src = p1[:, b, col:col + P] if col >= 0 else dup1[:, b, -1 - col].rearrange("p a d -> p (a d)")
                    mm = pe.transpose(tt(g % 2)[:, j, b * P:b * P + P], src, ident[:])
            mm.then_inc(qk_turned, 1)
        pe.wait_ge(qk_act, 7)
        pe.wait_ge(qk_dve, 6)
        pe.wait_ge(c_ready, 1)

        pe.wait_ge(slope_ready, HEADS)

        def scores1(n):
            h, bank = n % HEADS, G[:, n % 4, :]
            q, k = (h // 2, 8 + h // 8) if n < HEADS else (10 + h // 2, 18 + h // 2)
            rows = slice(DH * (h % 2), DH * (h % 2) + DH)
            if n >= 4:
                pe.wait_ge(p_ready, n - 3)
            if n < HEADS:
                pe.matmul(bank[:, 0:3 * P], slope_id[:, h, :], tab1[:, ALI:ALI + 3 * P], start=True, stop=False)
            else:
                pe.matmul(bank[:, 0:3 * P], ident[:, h:h + 1].broadcast_to([P, P]), cT[:], start=True, stop=False)
                for c0 in (0, 2 * P):
                    pe.matmul(bank[:, c0:c0 + P], ident[:], tab1[:, CAU:CAU + P], start=False, stop=False)
            for blk, (c0, w) in enumerate(((0, P), (P, 2 * P))):
                mm = pe.matmul(bank[:, c0:c0 + w], qk1[rows, q, P * blk:P * blk + P], qk1[rows, k, 0:w],
                               start=False, stop=blk == NB - 1)
            mm.then_inc(s_ready, 1)

        def turn_p(n, src, width):
            pe.wait_ge(p_ready, n + 1)
            if n >= 2:
                pe.wait_ge(pt_ready, n - 1)
            for j in range(width // P):
                mm = pe.transpose(T[:, n % 2, P * j:P * j + P], src[:, P * j:P * j + P], ident[:])
            mm.then_inc(pt_turned, 1)

        def pv1(n):
            pe.wait_ge(pt_ready, n + 1)
            b, i, h = n // 4, n % 4, n % HEADS
            if i == 0 and b >= 2:
                pe.wait_ge(o_evac, b - 1)
            v = VA + DH * (h // 8) if n < HEADS else VB + DH * h
            out = T[:, 2 + b % 2, :]
            pe.matmul(out[:, DH * i:DH * i + DH], pt1[:, n % 4, 0:P], p1[:, 0, v:v + DH], start=True, stop=True)
            pe.matmul(out[:, TOK + DH * i:TOK + DH * i + DH], pt1[:, n % 4, P:2 * P], p1[:, 0, v:v + DH],
                      start=True, stop=False)
            pe.matmul(out[:, TOK + DH * i:TOK + DH * i + DH], pt1[:, n % 4, 2 * P:3 * P], p1[:, 1, v:v + DH],
                      start=False, stop=True).then_inc(pt_used, 1)

        def attend(count, scores, turn, pv):
            for n in range(3):
                scores(n)
            for n in range(count + 2):
                if n + 3 < count:
                    scores(n + 3)
                if n < count:
                    turn(n)
                if n >= 2:
                    pv(n - 2)

        attend(2 * HEADS, scores1, lambda n: turn_p(n, sm1[:, n % 4, :], 3 * P), pv1)
        pe.wait_ge(o_evac, 8)
        turn_prep("out1", o1)

        s0, e0, r = 2 * FIRST_LOAD["out1"], FIRST_EVAC["out1"], prepped("out1")
        with pe.Fori(0, 2) as i:
            for c in range(2):
                steps(s0 + 8 * c, 0, 8, c, H, r, e0 + 2 * (c - 1), i * 16, i * 4)
        turn_prep("up1", x)

        def turn_up(u, e, d=0, du=0, de=0):
            pe.wait_ge(bank_evac, e + de)
            if u >= 1:
                pe.wait_ge(up_read, u + du)
            for j in range(CK):
                for b in range(NB):
                    mm = pe.transpose(tt(0)[:, j, b * P:b * P + P], u_buf[:, b, P * j:P * j + P], ident[:])
            mm.then_inc(turned, 1)

        for g, n, fin_up, fin_down in (("a", 8, None, 2), ("b", 8, None, 3), ("c", 6, 4, 5)):
            s0, e0, u0, r = 2 * FIRST_LOAD["up1" + g], FIRST_EVAC["up1" + g], UP0["up1" + g], prepped("up1")
            sd, ed = 2 * FIRST_LOAD["down1" + g], FIRST_EVAC["down1" + g]
            per = 8 if n == 8 else 6

            def ready(k, u0=u0):
                return a_ready, u0 + k + 1

            def up_pair(s, e, u, d, de, du, tail=False, finish=None):
                for c in range(2):
                    steps(s + 8 * c, 2, 8, c, H, r, d=d)
                    if tail and c == 1:
                        steps(sd, 0, 2, 0, A, ready, ed - 2, per=per)
                    else:
                        steps(s + 8 * c + 8, 0, 2, 1 - c, H, r, e + 2 * c, d, de)
                    turn_up(u + c, e + 2 * c + 2, d, du, de)
                    if c == 0 and finish is not None:
                        ada_sum(finish)

            steps(s0, 0, 2, 0, H, r, e0 - 2 if g != "a" else e0)
            if g == "a":
                pe.wait_ge(tmp_act, PREP["up1"][0] + 4)
                pe.wait_ge(tmp_dve, PREP["up1"][0] + 4)
                ada_sum(1)
            up_pair(s0, e0, u0, 0, 0, 0, finish=fin_up)
            with pe.Fori(0, n // 2 - 2) as i:
                up_pair(s0 + 16, e0 + 4, u0 + 2, i * 16, i * 4, i * 2)
            up_pair(s0 + 8 * n - 16, e0 + 2 * n - 4, u0 + n - 2, 0, 0, 0, tail=True)
            for c in range(4):
                steps(sd + per * c, 2 if c == 0 else 0, per, c % 2, A, ready, ed + 2 * (c - 1), per=per)
                if c == 0 and fin_down is not None:
                    ada_sum(fin_down)
        pe.wait_ge(ada_col, 6)
        for n, part in enumerate((2, 5)):
            mm = pe.transpose(T[0:KT, 3, P * n:P * n + P], adac[:, part, :], ident[:])
        mm.then_inc(g_turned, 1)
        pe.wait_ge(g_copied, 1)
        turn_prep("in2", y)

        s0, e0, r = 2 * FIRST_LOAD["in2"], FIRST_EVAC["in2"], prepped("in2")
        for k in range(2):
            steps(s0 + 8 * k, 0, 8, k, H, r, e0 + 2 * (k - 1))
        turn_prep("ctx", y)
        pe.wait_ge(bank_evac, e0 + 4)
        for k in range(8):
            step(s0 + 16 + k, 0, H + A, STEPK * k, k == 0, k == 7, (h_ready, PREP["ctx"][0] + k // 2 + 1))

        def turn_qk(g):
            pe.wait_ge(qk_act, 7 + g - 1)
            pe.wait_ge(qk_dve, 6 + g - 1)
            for j in range(4):
                for b in range(NB):
                    out = tt((7 + g) % 2)[:, j, b * P:b * P + P]
                    if g < 2:
                        src = p2[:, b, Q2 + P * (4 * g + j):Q2 + P * (4 * g + j + 1)]
                    else:
                        kv = 2 * (g - 2) + j // 2
                        src = dup2[:, NB * (j % 2) + b, kv].rearrange("p a d -> p (a d)")
                    mm = pe.transpose(out, src, ident[:])
            mm.then_inc(qk_turned, 1)

        steps(s0 + 24, 0, 8, 0, H, r, e0 + 6)
        pe.wait_ge(rope_done, 2)
        turn_qk(0)
        turn_qk(1)
        steps(s0 + 32, 0, 4, 1, H, r, e0 + 8)
        pe.wait_ge(dup_ready, 3)
        turn_qk(2)
        turn_qk(3)
        steps(s0 + 32, 4, 8, 1, H, r)

        pe.wait_ge(bank_evac, e0 + 10)
        pe.wait_ge(qk_act, 11)
        pe.wait_ge(qk_dve, 10)

        def scores2(m):
            h, blk, bank = m // 2, m % 2, G[:, m % 4, :]
            rows = slice(DH * (h % 2), DH * (h % 2) + DH)
            pe.wait_ge(p_ready, 32 + m - 3)
            if m == 2:
                pe.wait_ge(bank_evac, FIRST_EVAC["out2"])
            pe.matmul(bank, q2t[rows, h // 2, P * blk:P * blk + P], k2t[rows, h // 4, :], start=True, stop=False)
            far = P * (1 - blk)
            pe.matmul(bank[:, far:far + P], ident[:], tab2[:, MASK2 + N * blk + far:MASK2 + N * blk + far + P],
                      start=False, stop=True).then_inc(s_ready, 1)

        def pv2(m):
            pe.wait_ge(pt_ready, 32 + m + 1)
            h, blk, b = m // 2, m % 2, m // 8
            if m % 8 == 0 and b >= 2:
                pe.wait_ge(o_evac, 8 + b - 1)
            at_ = TOK * blk + DH * (h % 4)
            kv = DH * (h // 4)
            for j in range(4):
                v = p2[:, j, V2 + kv:V2 + kv + DH] if j < 2 else c2[:, j - 2, 256 + kv:256 + kv + DH]
                mm = pe.matmul(T[:, 2 + b % 2, at_:at_ + DH], pt2[:, m % 4, P * j:P * j + P], v, start=j == 0, stop=j == 3)
            mm.then_inc(pt_used, 1)

        attend(2 * HEADS, scores2, lambda m: turn_p(32 + m, sm2[:, m % 4, :], N), pv2)

        pe.wait_ge(pool_in, 32)
        pe.wait_ge(p_ready, 64)
        for g in range(4):
            for c in range(2):
                for b in range(NB):
                    mm = pe.matmul(G[:, g, TOK * c:TOK * c + TOK], p2[:, b, U2 + PG * g + P * c:U2 + PG * g + P * c + P],
                                   pool_a[:, b, g, :], start=b == 0, stop=b == NB - 1)
            mm.then_inc(pooled_mm, 1)
        pe.wait_ge(pooled_ev, 4)
        for j in range(8):
            g, dt = j // 2, j % 2
            if j >= 4:
                pe.wait_ge(mixed_lo, j - 3)
            for c in range(2):
                mm = pe.matmul(G[:, j % 4, 0:TOK], pool_w[:, g, c, P * dt:P * dt + P], pooled[:, 2 * g + c, :],
                               start=c == 0, stop=c == 1)
            mm.then_inc(mixed_mm, 1)
        pe.wait_ge(o_evac, 12)
        pe.wait_ge(mixed_lo, 8)
        turn_prep("out2", o2)

        s0, e0, n0 = 2 * FIRST_LOAD["out2"], FIRST_EVAC["out2"], PREP["out2"][0]

        def r(k):
            return h_ready, n0 + min(k // 2, 1) + 1

        with pe.Fori(0, 2) as i:
            for c in range(2):
                steps(s0 + 8 * c, 0, 8, c, H, r, e0 + 2 * (c - 1), i * 16, i * 4)
        turn_prep("up2", y)

        s0, e0, u0, r = 2 * FIRST_LOAD["mlp2"], FIRST_EVAC["mlp2"], UP0["mlp2"], prepped("up2")
        with pe.Fori(0, GROUPS2) as g:
            d, de, du = g * 64, g * 16, g * 4

            def ready(k):
                return a_ready, u0 + k // 2 + 1 + du

            steps(s0, 0, 2, 0, H, r, e0 - 2, d, de)
            for c in range(4):
                steps(s0 + 8 * c, 2, 8, c % 2, H, r, d=d)
                if c < 3:
                    steps(s0 + 8 * c + 8, 0, 2, (c + 1) % 2, H, r, e0 + 2 * c, d, de)
                else:
                    steps(s0 + 32, 0, 2, 0, A, ready, e0 + 6, d, de)
                turn_up(u0 + c, e0 + 2 * c + 2, d, du, de)
            for c in range(4):
                steps(s0 + 32 + 8 * c, 2 if c == 0 else 0, 8, c % 2, A, ready, e0 + 8 + 2 * (c - 1), d, de)

    ctx.close()


NAMES = ["x", "pre_mix_g", "w_in", "b_forget", "sinks", "grp_swa_g", "grp_fox_g", "w_out", "post_mix_g", "pre_ffn_g",
         "w_up", "conv_w", "conv_b", "w_down", "post_ffn_g", "c_2", "ctx_2", "c_ctx_2", "norm_attn_w_2", "norm_mlp_w_2",
         "w_ada_2", "b_ada_2", "w_in_2", "attn_sink_2", "pool_w_2", "pool_scale_2", "w_out_2", "w_mlp_up_2",
         "w_mlp_down_2", "final_norm_w_2"]


def kernel(**inputs):
    import concourse.bacc as bacc
    from concourse.bass_utils import run_bass_kernel_spmd

    nc = bacc.Bacc("TRN2", target_bir_lowering=False, num_devices=1)
    table, pool_table = constants()
    arrays, aps = {}, {}
    for name, value in [(n, inputs[n]) for n in NAMES] + [("table", table), ("pool_table", pool_table)]:
        value = np.ascontiguousarray(value)
        arrays["in_" + name] = value
        aps[name] = nc.dram_tensor("in_" + name, value.shape, mybir.dt.from_np(value.dtype), kind="ExternalInput").ap()
    aps["out"] = nc.dram_tensor("out", (1, TOK, D), F32, kind="ExternalOutput").ap()
    build(nc, aps)
    result = run_bass_kernel_spmd(nc, [arrays], core_ids=[0])
    return result.results[0]["out"]
```
